# Optimizing a Trainium2 kernel written in Bass

```python
import math
import jax, jax.numpy as jnp
from jax import lax
import numpy as np

D_MODEL = 1024
BATCH = 1
SEQ = 1024
DEPTH = 2
DEC_BATCH = 8
DEC_SEQ = 1
PAST_LEN = 4096
PAGE_SIZE = 128

N_EVEN = (DEPTH + 1) // 2
N_ODD = DEPTH // 2
N_MEM = 256
NORM_EPS = 1e-6
RW_HD = 64
RW_W = D_MODEL // 2
RW_HEADS = RW_W // RW_HD
LORA_W = 64
LORA_A = 64
LORA_G = 128
RW_COLS = 3 * RW_W + LORA_W + LORA_A + LORA_G
RW_SPLITS = [RW_W, 2 * RW_W, 3 * RW_W, 3 * RW_W + LORA_W, 3 * RW_W + LORA_W + LORA_A]
RW_LN_EPS = RW_HD * 1e-5
LRU_W = D_MODEL // 2
LRU_BLOCKS = 8
LRU_BD = LRU_W // LRU_BLOCKS
CONV_W = 4
LRU_C = 8.0
AB_COLS = RW_COLS + 2 * LRU_W
MIX_W = RW_W + LRU_W
SB_HD = 64
SB_W = D_MODEL
SB_HEADS = SB_W // SB_HD
Q_BLOCK = 128
SB_BIAS_LO = -8.0
SB_BIAS_HI = -5.0
MEM_HEADS = 4
MEM_W = D_MODEL // 2
MEM_HD = MEM_W // MEM_HEADS
D_FF = -(-8 * D_MODEL // (3 * 256)) * 256

kernel_name = "rwkv7_rglru_stickbreak_hybrid_step"

def rms_norm(x, g, eps=NORM_EPS):
    xf = x.astype(jnp.float32)
    y = xf * lax.rsqrt(jnp.mean(xf * xf, axis=-1, keepdims=True) + eps)
    return (y * g.astype(jnp.float32)).astype(x.dtype)

def swiglu(h, w_gate, w_up, w_down):
    return (jax.nn.silu(h @ w_gate) * (h @ w_up)) @ w_down

def memory_kv(mem, g, wk, wv, kn):
    b, m, _ = mem.shape
    mn = rms_norm(mem, g)
    k = rms_norm((mn @ wk).reshape(b, m, MEM_HEADS, MEM_HD), kn)
    v = (mn @ wv).reshape(b, m, MEM_HEADS, MEM_HD)
    return k, v

def memory_xattn(h, k, v, wq, qn, wo):
    b, t, _ = h.shape
    q = rms_norm((h @ wq).reshape(b, t, MEM_HEADS, MEM_HD), qn)
    s = jnp.einsum('bthd,bmhd->bhtm', q, k, preferred_element_type=jnp.float32) * (MEM_HD ** -0.5)
    p = jax.nn.softmax(s, axis=-1).astype(v.dtype)
    o = jnp.einsum('bhtm,bmhd->bthd', p, v).reshape(b, t, MEM_W)
    return o @ wo

def rwkv_lru_mixer(h, wkv0, shift0, h0, conv0, w_in, mu, w0, w2, a0, a2, g2, k_k, k_a, r_k,
                   lnx_w, lnx_b, conv_w, conv_b, wa, ba, wx, bx, lam, w_out):
    b, t, _ = h.shape
    f32 = jnp.float32
    p = (h @ w_in).astype(f32)
    p_rw, p_x, p_gate = jnp.split(p, [RW_COLS, RW_COLS + LRU_W], axis=-1)

    prev = jnp.concatenate([shift0.astype(f32)[:, None], p_rw[:, :-1]], axis=1)
    xs = p_rw + mu * (prev - p_rw)
    r, k, v, dw, da, dg = jnp.split(xs, RW_SPLITS, axis=-1)
    log_w = -jnp.exp(-jax.nn.softplus(-(w0 + jnp.tanh(dw) @ w2)) - 0.5)
    a = jax.nn.sigmoid(a0 + da @ a2)
    g = jax.nn.sigmoid(dg) @ g2
    heads = lambda z: z.reshape(b, t, RW_HEADS, RW_HD)
    kk = heads(k * k_k)
    kk = kk / jnp.maximum(jnp.linalg.norm(kk, axis=-1, keepdims=True), 1e-12)
    k = k * (1.0 + (a - 1.0) * k_a)
    r, k, v, a, w = heads(r), heads(k), heads(v), heads(a), heads(jnp.exp(log_w))

    def step(S, inp):
        r_t, w_t, k_t, v_t, kk_t, a_t = inp
        sa = jnp.einsum('bhvk,bhk->bhv', S, -kk_t)
        S = (S * w_t[:, :, None, :] + sa[..., None] * (kk_t * a_t)[:, :, None, :]
             + v_t[..., None] * k_t[:, :, None, :])
        return S, jnp.einsum('bhvk,bhk->bhv', S, r_t)

    tm = lambda z: jnp.moveaxis(z, 1, 0)
    wkv, y = lax.scan(step, wkv0.astype(f32), (tm(r), tm(w), tm(k), tm(v), tm(kk), tm(a)))
    y = jnp.moveaxis(y, 0, 1)
    mean = jnp.mean(y, axis=-1, keepdims=True)
    var = jnp.mean(jnp.square(y - mean), axis=-1, keepdims=True)
    y = ((y - mean) * lax.rsqrt(var + RW_LN_EPS)).reshape(b, t, RW_W) * lnx_w + lnx_b
    bonus = jnp.sum(r * k * r_k.reshape(RW_HEADS, RW_HD), axis=-1, keepdims=True) * v
    out_rw = (y + bonus.reshape(b, t, RW_W)) * g

    xin = jnp.concatenate([conv0.astype(f32), p_x], axis=1)
    xc = conv_b + sum(conv_w[j] * xin[:, j:j + t] for j in range(CONV_W))
    new_conv = xin[:, -(CONV_W - 1):]
    xb = xc.reshape(b, t, LRU_BLOCKS, LRU_BD)
    gate_r = jax.nn.sigmoid(jnp.einsum('btnd,nde->btne', xb, wa).reshape(b, t, LRU_W) + ba)
    gate_i = jax.nn.sigmoid(jnp.einsum('btnd,nde->btne', xb, wx).reshape(b, t, LRU_W) + bx)
    log_a = -LRU_C * gate_r * jax.nn.softplus(-lam)
    a_t = jnp.exp(log_a)
    b_t = jnp.sqrt(-jnp.expm1(2.0 * log_a)) * (gate_i * xc)
    b_t = b_t.at[:, 0].add(a_t[:, 0] * h0.astype(f32))
    _, hs = lax.associative_scan(lambda l, rr: (l[0] * rr[0], rr[0] * l[1] + rr[1]),
                                 (a_t, b_t), axis=1)
    out_lru = hs * jax.nn.gelu(p_gate)

    mix = jnp.concatenate([out_rw, out_lru], axis=-1).astype(h.dtype) @ w_out
    dt = h.dtype
    return mix, (wkv.astype(dt), p_rw[:, -1].astype(dt), hs[:, -1].astype(dt), new_conv.astype(dt))

def sb_block(q, k, v, q_pos, k_pos, bias):
    z = (jnp.einsum('bqhd,bkhd->bhqk', q, k, preferred_element_type=jnp.float32) * (SB_HD ** -0.5)
         + bias.astype(jnp.float32)[None, :, None, None])
    mask = k_pos[None, :] < q_pos[:, None]
    log_1m = jnp.where(mask, jax.nn.log_sigmoid(-z), 0.0)
    after = lax.cumsum(log_1m, axis=3, reverse=True) - log_1m
    att = jnp.where(mask, jnp.exp(jax.nn.log_sigmoid(z) + after), 0.0)
    return jnp.einsum('bhqk,bkhd->bqhd', att.astype(v.dtype), v)

def sb_sweep(q, k, v, offset, bias):
    t = q.shape[1]
    pos = jnp.arange(offset + t)
    outs = []
    for s in range(0, t, Q_BLOCK):
        e = min(s + Q_BLOCK, t)
        outs.append(sb_block(q[:, s:e], k[:, :offset + e], v[:, :offset + e],
                             pos[offset + s:offset + e], pos[:offset + e], bias))
    return jnp.concatenate(outs, axis=1)

def stick_breaking_mixer(h, w_qkv, w_out, bias, past):
    b, t, _ = h.shape
    qkv = (h @ w_qkv).reshape(b, t, 3, SB_HEADS, SB_HD)
    q, k, v = qkv[:, :, 0], qkv[:, :, 1], qkv[:, :, 2]
    if past is None:
        k_all, v_all, offset = k, v, 0
    else:
        k_pool, v_pool, layer, page_table = past
        offset = page_table.shape[1] * PAGE_SIZE
        k_past = k_pool[layer][page_table].reshape(b, offset, SB_HEADS, SB_HD)
        v_past = v_pool[layer][page_table].reshape(b, offset, SB_HEADS, SB_HD)
        k_all = jnp.concatenate([k_past, k], axis=1)
        v_all = jnp.concatenate([v_past, v], axis=1)
    o = sb_sweep(q, k_all, v_all, offset, bias)
    return o.reshape(b, t, SB_W) @ w_out, (k, v)

def setup_inputs(seed: int = 0) -> dict:
    key = jax.random.key(seed)
    keys = iter(jax.random.split(key, 80))

    def nrm(shape, scale=1.0):
        return jax.random.normal(next(keys), shape, jnp.float32) * scale

    def gain(shape):
        return 1.0 + nrm(shape, 0.05)

    n_pages = PAST_LEN // PAGE_SIZE
    used = DEC_BATCH * n_pages
    pool = used + max(1, used // 4)
    page_table = jax.random.permutation(next(keys), pool)[:used].reshape(DEC_BATCH, n_pages).astype(jnp.int32)
    u = jax.random.uniform(next(keys), (N_EVEN, LRU_W), jnp.float32, minval=0.9, maxval=0.999)
    return {
        "x_prompt": nrm((BATCH, SEQ, D_MODEL)),
        "x_sample": nrm((DEC_BATCH, DEC_SEQ, D_MODEL)),
        "state_rwkv_wkv": nrm((N_EVEN, DEC_BATCH, RW_HEADS, RW_HD, RW_HD), 0.1),
        "state_rwkv_shift": nrm((N_EVEN, DEC_BATCH, RW_COLS)),
        "state_lru_h": nrm((N_EVEN, DEC_BATCH, LRU_W), 0.5),
        "state_lru_conv": nrm((N_EVEN, DEC_BATCH, CONV_W - 1, LRU_W)),
        "cache_sb_k": nrm((N_ODD, pool, PAGE_SIZE, SB_HEADS, SB_HD)),
        "cache_sb_v": nrm((N_ODD, pool, PAGE_SIZE, SB_HEADS, SB_HD)),
        "page_table": page_table,
        "cache_mem_k": nrm((DEPTH, DEC_BATCH, N_MEM, MEM_HEADS, MEM_HD)),
        "cache_mem_v": nrm((DEPTH, DEC_BATCH, N_MEM, MEM_HEADS, MEM_HD)),
        "mem_prompt": nrm((BATCH, N_MEM, D_MODEL)),
        "g_mix": gain((DEPTH, D_MODEL)),
        "g_mem": gain((DEPTH, D_MODEL)),
        "g_memkv": gain((DEPTH, D_MODEL)),
        "g_ffn": gain((DEPTH, D_MODEL)),
        "wq_mem": nrm((DEPTH, D_MODEL, MEM_W), D_MODEL ** -0.5),
        "wk_mem": nrm((DEPTH, D_MODEL, MEM_W), D_MODEL ** -0.5),
        "wv_mem": nrm((DEPTH, D_MODEL, MEM_W), D_MODEL ** -0.5),
        "wo_mem": nrm((DEPTH, MEM_W, D_MODEL), MEM_W ** -0.5),
        "qn_mem": gain((DEPTH, MEM_HD)),
        "kn_mem": gain((DEPTH, MEM_HD)),
        "w_ffn_gate": nrm((DEPTH, D_MODEL, D_FF), D_MODEL ** -0.5),
        "w_ffn_up": nrm((DEPTH, D_MODEL, D_FF), D_MODEL ** -0.5),
        "w_ffn_down": nrm((DEPTH, D_FF, D_MODEL), D_FF ** -0.5),
        "w_in_ab": nrm((N_EVEN, D_MODEL, AB_COLS), D_MODEL ** -0.5),
        "mu_shift": jax.random.uniform(next(keys), (N_EVEN, RW_COLS), jnp.float32),
        "rw_w0": jax.random.uniform(next(keys), (N_EVEN, RW_W), jnp.float32, minval=-6.0, maxval=1.0),
        "rw_w2": nrm((N_EVEN, LORA_W, RW_W), 0.5 * LORA_W ** -0.5),
        "rw_a0": nrm((N_EVEN, RW_W), 0.5),
        "rw_a2": nrm((N_EVEN, LORA_A, RW_W), 0.5 * LORA_A ** -0.5),
        "rw_g2": nrm((N_EVEN, LORA_G, RW_W), LORA_G ** -0.5),
        "rw_kk": 0.85 + nrm((N_EVEN, RW_W), 0.05),
        "rw_ka": 1.0 + nrm((N_EVEN, RW_W), 0.05),
        "rw_rk": nrm((N_EVEN, RW_W), 0.1),
        "rw_lnx_w": gain((N_EVEN, RW_W)),
        "rw_lnx_b": nrm((N_EVEN, RW_W), 0.01),
        "lru_conv_w": nrm((N_EVEN, CONV_W, LRU_W), CONV_W ** -0.5),
        "lru_conv_b": nrm((N_EVEN, LRU_W), 0.01),
        "lru_wa": nrm((N_EVEN, LRU_BLOCKS, LRU_BD, LRU_BD), LRU_BD ** -0.5),
        "lru_ba": nrm((N_EVEN, LRU_W), 0.01),
        "lru_wx": nrm((N_EVEN, LRU_BLOCKS, LRU_BD, LRU_BD), LRU_BD ** -0.5),
        "lru_bx": nrm((N_EVEN, LRU_W), 0.01),
        "lru_lambda": jnp.log(u) - jnp.log1p(-u),
        "w_out_ab": nrm((N_EVEN, MIX_W, D_MODEL), MIX_W ** -0.5),
        "w_qkv_sb": nrm((N_ODD, D_MODEL, 3 * SB_W), D_MODEL ** -0.5),
        "w_out_sb": nrm((N_ODD, SB_W, D_MODEL), SB_W ** -0.5),
        "sb_bias": jax.random.uniform(next(keys), (N_ODD, SB_HEADS), jnp.float32,
                                      minval=SB_BIAS_LO, maxval=SB_BIAS_HI),
    }

def reference(x_prompt, x_sample, state_rwkv_wkv, state_rwkv_shift, state_lru_h, state_lru_conv,
              cache_sb_k, cache_sb_v, page_table, cache_mem_k, cache_mem_v, mem_prompt,
              g_mix, g_mem, g_memkv, g_ffn, wq_mem, wk_mem, wv_mem, wo_mem, qn_mem, kn_mem,
              w_ffn_gate, w_ffn_up, w_ffn_down, w_in_ab, mu_shift, rw_w0, rw_w2, rw_a0, rw_a2,
              rw_g2, rw_kk, rw_ka, rw_rk, rw_lnx_w, rw_lnx_b, lru_conv_w, lru_conv_b, lru_wa,
              lru_ba, lru_wx, lru_bx, lru_lambda, w_out_ab, w_qkv_sb, w_out_sb, sb_bias):

    def trunk(x, sample):
        bsz = x.shape[0]
        st = {n: [] for n in ("wkv", "shift", "lru_h", "lru_conv", "sb_k", "sb_v", "mem_k", "mem_v")}
        for i in range(DEPTH):
            h = rms_norm(x, g_mix[i])
            if i % 2 == 0:
                e = i // 2
                if sample:
                    init = (state_rwkv_wkv[e], state_rwkv_shift[e], state_lru_h[e], state_lru_conv[e])
                else:
                    init = (jnp.zeros((bsz, RW_HEADS, RW_HD, RW_HD), x.dtype),
                            jnp.zeros((bsz, RW_COLS), x.dtype),
                            jnp.zeros((bsz, LRU_W), x.dtype),
                            jnp.zeros((bsz, CONV_W - 1, LRU_W), x.dtype))
                mix, (s_wkv, s_shift, s_h, s_conv) = rwkv_lru_mixer(
                    h, init[0], init[1], init[2], init[3], w_in_ab[e], mu_shift[e], rw_w0[e], rw_w2[e],
                    rw_a0[e], rw_a2[e], rw_g2[e], rw_kk[e], rw_ka[e], rw_rk[e], rw_lnx_w[e], rw_lnx_b[e],
                    lru_conv_w[e], lru_conv_b[e], lru_wa[e], lru_ba[e], lru_wx[e], lru_bx[e],
                    lru_lambda[e], w_out_ab[e])
                st["wkv"].append(s_wkv)
                st["shift"].append(s_shift)
                st["lru_h"].append(s_h)
                st["lru_conv"].append(s_conv)
            else:
                o = i // 2
                past = (cache_sb_k, cache_sb_v, o, page_table) if sample else None
                mix, (k_rows, v_rows) = stick_breaking_mixer(h, w_qkv_sb[o], w_out_sb[o], sb_bias[o], past)
                st["sb_k"].append(k_rows)
                st["sb_v"].append(v_rows)
            x = x + mix
            if sample:
                mk, mv = cache_mem_k[i], cache_mem_v[i]
            else:
                mk, mv = memory_kv(mem_prompt, g_memkv[i], wk_mem[i], wv_mem[i], kn_mem[i])
                st["mem_k"].append(mk)
                st["mem_v"].append(mv)
            x = x + memory_xattn(rms_norm(x, g_mem[i]), mk, mv, wq_mem[i], qn_mem[i], wo_mem[i])
            x = x + swiglu(rms_norm(x, g_ffn[i]), w_ffn_gate[i], w_ffn_up[i], w_ffn_down[i])
        return x, st

    y_prompt, sp = trunk(x_prompt, False)
    y_sample, ss = trunk(x_sample, True)
    stack = lambda arrs: jnp.stack(arrs, axis=0)
    return (y_prompt, y_sample,
            stack(sp["wkv"]), stack(ss["wkv"]),
            stack(sp["shift"]), stack(ss["shift"]),
            stack(sp["lru_h"]), stack(ss["lru_h"]),
            stack(sp["lru_conv"]), stack(ss["lru_conv"]),
            stack(sp["sb_k"]), stack(ss["sb_k"]),
            stack(sp["sb_v"]), stack(ss["sb_v"]),
            stack(sp["mem_k"]), stack(sp["mem_v"]))


_drawn_inputs = setup_inputs


def setup_inputs(seed=0):
    import zlib

    import numpy as np

    out = dict(_drawn_inputs(seed))
    spreads = {}
    factors = {'g_mem': 7.761, 'qn_mem': 8.0, 'rw_lnx_b': 8.0, 'lru_ba': 23.486, 'lru_bx': 8.0}
    for name, (base, spread) in spreads.items():
        noise = np.random.default_rng([zlib.crc32(name.encode()), seed]).standard_normal(out[name].shape)
        drawn = base * np.exp(spread * noise) if base else spread * noise
        out[name] = __import__('jax').numpy.asarray(drawn.astype(out[name].dtype))
    for name, factor in factors.items():
        out[name] = (out[name] * factor).astype(out[name].dtype)
    return out
```

```python
from contextlib import ExitStack, contextmanager
from collections import namedtuple

import numpy as np
import concourse.bass as bass
from concourse import mybir

F32 = mybir.dt.float32
I32 = mybir.dt.int32
ALU = mybir.AluOpType
ACT = mybir.ActivationFunctionType
AX = mybir.AxisListType
ds = bass.DynSlice

P = 128
D = 1024
DT = D // P
T = 1024
TT = T // P
NS = 8
NT = T + NS
N3 = NT // 3
PAD = 4
RW = 512
RWT = RW // P
RW_COLS = 1792
RWC_T = RW_COLS // P
LRU_T = 4
AB_T = 22
AB_COLS = AB_T * P
FF = 2816
FF_T = FF // P
HD = 64
C = 64
NC = T // C
MEM = 256
MH = 4
SBH = 16
PAGES = 32
EPS = 1e-6
LN_EPS = HD * 1e-5
DECAY = -float(np.exp(-0.5))

ROWS_A = [("mu_shift", 14), ("rw_w0", 4), ("rw_a0", 4), ("rw_kk", 4), ("rw_ka", 4), ("rw_rk", 4),
          ("rw_lnx_w", 4), ("rw_lnx_b", 4), ("lru_conv_w", 16), ("lru_conv_b", 4), ("lru_ba", 4),
          ("lru_bx", 4), ("lru_lambda", 4)]
ROWS_B = [("g_mix", 16), ("g_mem", 16), ("g_memkv", 16), ("g_ffn", 16), ("qn_mem", 2)]
COL = {}
for _base, _rows in ((0, ROWS_A), (P, ROWS_B)):
    for _name, _n in _rows:
        COL[_name] = _base
        _base += _n
NA = sum(n for _, n in ROWS_A)
NB = sum(n for _, n in ROWS_B)
FIRST_SEM = [0]


def record(**fields):
    return namedtuple("Record", list(fields))(**fields)


TENSORS = [0]


def tensor(nc, name, shape, dt=F32):
    TENSORS[0] += 1
    return nc.sbuf_tensor(f"{name}_{TENSORS[0]}", shape, dt)


@contextmanager
def phase(nc, *names):
    with ExitStack() as stack:
        sems = {}
        for name in names:
            if isinstance(name, tuple):
                sems[name[0]] = [stack.enter_context(nc.semaphore(f"{name[0]}{i}")) for i in range(name[1])]
            else:
                sems[name] = stack.enter_context(nc.semaphore(name))
        with nc.Block() as block:
            yield record(**sems), block
    nc.all_engine_barrier(sems_to_clear=range(FIRST_SEM[0], 256))


def linker(eng, sem):
    count = [0]

    def link(ins):
        count[0] += 1
        ins.then_inc(sem, 1)
        eng.wait_ge(sem, count[0])

    return link


def bank3(ps, first):
    return ps[:, first:first + 3, 0:N3]


def cols3(ap):
    return ap.rearrange("p (n c) -> p n c", n=3)


def constants(nc, g):
    with phase(nc, "filled", "cut", "made") as (s, block):
        @block.gpsimd
        def _(pool):
            link = linker(pool, s.made)
            link(pool.memset(g.ones[:, :], 1.0))
            link(pool.memset(g.ident[:, :], 0.0))
            link(pool.affine_select(out=g.ident[:, :], in_=g.ident[:, :], compare_op=ALU.not_equal, fill=1.0,
                                    base=0, pattern=[[-1, P]], channel_multiplier=1))
            link(pool.memset(g.blockones[:, :], 0.0))
            link(pool.memset(g.blockones[0:64, 0:64], 1.0))
            link(pool.memset(g.blockones[64:128, 64:128], 1.0))
            link(pool.tensor_tensor(g.ident2[:, :], g.ident[:, 0:64], g.ident[:, 64:128], ALU.add))
            link(pool.affine_select(out=g.tail[:, :], in_=g.ones[:, :], compare_op=ALU.is_ge, fill=0.0,
                                    base=0, pattern=[[-1, P]], channel_multiplier=1))
            link(pool.tensor_tensor(g.rest[:, :], g.ones[:, :], g.tail[:, :], ALU.subtract))
            link(pool.tensor_scalar(g.blocked[:, :], g.tail[:, :], -1e30, None, ALU.mult))
            link(pool.memset(g.epsc[:, 0:1], EPS))
            link(pool.memset(g.epsc[:, 1:2], LN_EPS))


def load_inputs(nc, g, d, ps):
    NG = 2 * (TT + 1)
    with ExitStack() as mem:
        tok = mem.enter_context(tensor(nc, "tokens", [P, TT + 1, D], F32))
        rows = mem.enter_context(tensor(nc, "param_rows", [P, 2, P], F32))
        st = mem.enter_context(tensor(nc, "state_rows", [24, 3, RW_COLS], F32))
        with phase(nc, ("tok_in", TT + 1), "rows_in", "state_in", "turned", "taken_act", "taken_dve", "copied",
                   "stored") as (s, block):
            @block.sync
            def _(sp):
                for t in range(TT):
                    sp.dma_start(tok[:, t, :], d.x_prompt[0, t * P:(t + 1) * P, :]).then_inc(s.tok_in[t], 16)
                sp.dma_start(tok[0:NS, TT, :], d.x_sample[:, 0, :]).then_inc(s.tok_in[TT], 16)
                sp.dma_start(st[0:NS, 0, :], d.state_rwkv_shift[0]).then_inc(s.state_in, 16)
                sp.dma_start(st[0:24, 1, 0:RW], d.state_lru_conv[0].rearrange("b j c -> (b j) c")).then_inc(s.state_in, 16)
                sp.dma_start(st[0:NS, 2, 0:RW], d.state_lru_h[0]).then_inc(s.state_in, 16)
                sp.dma_start(d.lru_conv_s[0, :, 0:2, :], d.state_lru_conv[0, :, 1:3, :]).then_inc(s.stored, 16)
                sp.dma_start(g.kn[:, :, :], d.kn_mem.unsqueeze(0).to_broadcast([P, 2, P])).then_inc(s.stored, 16)
                sp.dma_start(g.sbb[:, :], d.sb_bias.to_broadcast([P, SBH])).then_inc(s.stored, 16)
                sp.dma_start(g.pages[:, :], d.page_table.rearrange("b n -> (b n)").unsqueeze(0)).then_inc(s.stored, 16)
                sp.wait_ge(s.stored, 64)

            @block.scalar
            def _(act):
                at = {}
                for group, names in enumerate((ROWS_A, ROWS_B)):
                    r = 0
                    for name, n in names:
                        src = d.rows[name].flatten().rearrange("(r c) -> r c", c=P)
                        act.dma_start(rows[r:r + n, group, :], src).then_inc(s.rows_in, 16)
                        r += n
                for n in range(0, NG, 2):
                    t = n // 2
                    w = P if t < TT else NS
                    act.wait_ge(s.turned, n + 1)
                    act.activation(g.X[:, 0:4, t * P:t * P + w],
                                   ps[:, n % 8, :].rearrange("p (k c) -> p k c", k=4)[:, :, 0:w],
                                   ACT.Copy).then_inc(s.taken_act, 1)

            @block.vector
            def _(dve):
                for n in range(1, NG, 2):
                    t = n // 2
                    w = P if t < TT else NS
                    dve.wait_ge(s.turned, n + 1)
                    dve.tensor_copy(g.X[:, 4:8, t * P:t * P + w],
                                    ps[:, n % 8, :].rearrange("p (k c) -> p k c", k=4)[:, :, 0:w]).then_inc(s.taken_dve, 1)
                dve.wait_ge(s.turned, NG + 1)
                dve.tensor_copy(g.par[:, 0:NA], ps[:, NG % 8, 0:NA]).then_inc(s.copied, 1)
                dve.tensor_copy(g.par[:, P:P + NB], ps[:, NG % 8, P:P + NB]).then_inc(s.copied, 1)
                dve.wait_ge(s.turned, NG + 2)
                dve.tensor_copy(g.shift0[:, :, :], ps[:, (NG + 1) % 8, 0:RWC_T * NS]
                                .rearrange("p (k b) -> p k b", b=NS)).then_inc(s.copied, 1)
                dve.tensor_copy(g.conv0[:, :, :], ps[:, (NG + 1) % 8, 128:128 + 96]
                                .rearrange("p (k b) -> p k b", b=24)).then_inc(s.copied, 1)
                dve.tensor_copy(g.h0[:, :, :], ps[:, (NG + 1) % 8, 256:256 + 32]
                                .rearrange("p (k b) -> p k b", b=NS)).then_inc(s.copied, 1)

            @block.tensor
            def _(pe):
                for n in range(NG):
                    t, half = n // 2, n % 2
                    w = P if t < TT else NS
                    if half == 0:
                        pe.wait_ge(s.tok_in[t], 16)
                    if n >= 8:
                        pe.wait_ge(s.taken_dve if half else s.taken_act, (n - 8) // 2 + 1)
                    for k in range(4):
                        kk = 4 * half + k
                        last = pe.transpose(ps[:, n % 8, k * P:k * P + w], tok[0:w, t, kk * P:(kk + 1) * P],
                                            g.ident[0:w, 0:w])
                    last.then_inc(s.turned, 1)
                pe.wait_ge(s.rows_in, 16 * (len(ROWS_A) + len(ROWS_B)))
                pe.wait_ge(s.taken_act, (NG - 8) // 2 + 1)
                pe.transpose(ps[:, NG % 8, 0:NA], rows[0:NA, 0, :], g.ident[0:NA, 0:NA])
                pe.transpose(ps[:, NG % 8, P:P + NB], rows[0:NB, 1, :], g.ident[0:NB, 0:NB]).then_inc(s.turned, 1)
                pe.wait_ge(s.state_in, 48)
                pe.wait_ge(s.taken_dve, (NG - 8) // 2 + 1)
                b = (NG + 1) % 8
                for k in range(RWC_T):
                    pe.transpose(ps[:, b, k * NS:(k + 1) * NS], st[0:NS, 0, k * P:(k + 1) * P], g.ident[0:NS, 0:NS])
                for k in range(LRU_T):
                    pe.transpose(ps[:, b, 128 + k * 24:152 + k * 24], st[0:24, 1, k * P:(k + 1) * P], g.ident[0:24, 0:24])
                for k in range(LRU_T):
                    last = pe.transpose(ps[:, b, 256 + k * NS:264 + k * NS], st[0:NS, 2, k * P:(k + 1) * P],
                                        g.ident[0:NS, 0:NS])
                last.then_inc(s.turned, 1)


def rms_norm(nc, g, ps, H, gains):
    with ExitStack() as mem:
        sq = mem.enter_context(tensor(nc, "squares", [P, 2, NT], F32))
        rms = mem.enter_context(tensor(nc, "rms", [P, NT], F32))
        rstd = mem.enter_context(tensor(nc, "rstd", [P, NT], F32))
        with phase(nc, "squared", "summed", "rooted", "inverted", "scaled") as (s, block):
            @block.scalar
            def _(act):
                for k in range(DT):
                    if k >= 2:
                        act.wait_ge(s.summed, k - 1)
                    act.activation(sq[:, k % 2, :], g.X[:, k, :], ACT.Square).then_inc(s.squared, 1)
                act.wait_ge(s.summed, DT)
                act.activation(cols3(rms[:, :]), bank3(ps, 0), ACT.Sqrt, scale=1.0 / D,
                               bias=g.epsc[:, 0:1]).then_inc(s.rooted, 1)

            @block.tensor
            def _(pe):
                for k in range(DT):
                    pe.wait_ge(s.squared, k + 1)
                    for n in range(3):
                        last = pe.matmul(ps[:, n, 0:N3], g.ones[:, :], sq[:, k % 2, n * N3:(n + 1) * N3],
                                         start=k == 0, stop=k == DT - 1)
                    last.then_inc(s.summed, 1)

            @block.vector
            def _(dve):
                dve.wait_ge(s.rooted, 1)
                dve.reciprocal(rstd[:, :], rms[:, :]).then_inc(s.inverted, 1)
                dve.wait_ge(s.inverted, 1)
                for k in range(DT):
                    dve.scalar_tensor_tensor(H[:, k, :], g.X[:, k, :], g.par[:, gains + k:gains + k + 1], rstd[:, :],
                                             ALU.mult, ALU.mult).then_inc(s.scaled, 1)


def weight_blocks(w, kt):
    return w.rearrange("(k p) m -> p k m", p=P, k=kt)


def project(nc, ps, w, kt, mt, rhs, take, engine):
    wv = weight_blocks(w, kt)
    with ExitStack() as mem:
        W = [mem.enter_context(tensor(nc, f"w_slot{i}", [P, kt, P], F32)) for i in range(2)]
        with phase(nc, ("w_in", 2), "product", "free_banks") as (s, block):
            @block.sync
            def _(sp):
                for h in range(2):
                    sp.dma_start(W[h][:, :, :], wv[:, :, h * P:(h + 1) * P]).then_inc(s.w_in[h], 16)
                with sp.Fori(1, mt // 2) as i:
                    for h in range(2):
                        sp.wait_ge(s.product, 2 * (i - 1) + h + 1)
                        sp.dma_start(W[h][:, :, :], wv[:, :, ds((2 * i + h) * P, P)]).then_inc(s.w_in[h], 16)

            @block.tensor
            def _(pe):
                with pe.Fori(0, mt // 2) as i:
                    for h in range(2):
                        pe.wait_ge(s.w_in[h], (i + 1) * 16)
                        pe.wait_ge(s.free_banks, 2 * i + h + 1)
                        for k in range(kt):
                            for n in range(3):
                                last = pe.matmul(ps[:, 3 * h + n, 0:N3], W[h][:, k, :], rhs(k, n),
                                                 start=k == 0, stop=k == kt - 1)
                        last.then_inc(s.product, 1)

            def takes(eng):
                eng.sem_inc(s.free_banks, 2)
                with eng.Fori(0, mt // 2) as i:
                    for h in range(2):
                        eng.wait_ge(s.product, 2 * i + h + 1)
                        take(eng, 2 * i + h, bank3(ps, 3 * h)).then_inc(s.free_banks, 1)

            if engine == "scalar":
                @block.scalar
                def _(act):
                    takes(act)
            else:
                @block.vector
                def _(dve):
                    takes(dve)


def add_to_residual(g):
    def take(dve, m, banks):
        x = g.X[:, ds(m, 1), :].rearrange("p a (n c) -> p (a n) c", n=3)
        return dve.tensor_tensor(x, banks, x, ALU.add)
    return take


def ffn(nc, g, d, ps, layer):
    wg, wu, wd = (weight_blocks(w[layer], kt) for w, kt in
                  ((d.w_ffn_gate, DT), (d.w_ffn_up, DT), (d.w_ffn_down, FF_T)))
    with ExitStack() as mem:
        hid = mem.enter_context(tensor(nc, "hidden", [P, FF_T, NT], F32))
        with ExitStack() as inner:
            H = inner.enter_context(tensor(nc, "h_ffn", [P, DT, NT], F32))
            rms_norm(nc, g, ps, H, COL["g_ffn"] + layer * DT)
            W = [inner.enter_context(tensor(nc, f"ffn_slot{i}", [P, DT, P], F32)) for i in range(4)]
            act_out = inner.enter_context(tensor(nc, "silu", [P, 2, NT], F32))
            with phase(nc, ("w_in", 4), "product", "gate_free", "up_free", "gated", "gate_used") as (s, block):
                @block.sync
                def _(sp):
                    for q in range(4):
                        sp.dma_start(W[q][:, :, :], (wg, wu)[q % 2][:, :, (q // 2) * P:(q // 2 + 1) * P]).then_inc(s.w_in[q], 16)
                    with sp.Fori(1, FF_T // 2) as i:
                        for q in range(4):
                            sp.wait_ge(s.product, 4 * (i - 1) + q + 1)
                            sp.dma_start(W[q][:, :, :], (wg, wu)[q % 2][:, :, ds((2 * i + q // 2) * P, P)]).then_inc(s.w_in[q], 16)

                @block.tensor
                def _(pe):
                    with pe.Fori(0, FF_T // 2) as i:
                        for q in range(4):
                            pe.wait_ge(s.w_in[q], (i + 1) * 16)
                            pe.wait_ge((s.gate_free, s.up_free)[q % 2], 2 * i + q // 2 + 1)
                            for k in range(DT):
                                for n in range(3):
                                    last = pe.matmul(ps[:, 3 * (q % 2) + n, 0:N3], W[q][:, k, :],
                                                     H[:, k, n * N3:(n + 1) * N3], start=k == 0, stop=k == DT - 1)
                            last.then_inc(s.product, 1)

                @block.scalar
                def _(act):
                    act.sem_inc(s.gate_free, 1)
                    with act.Fori(0, FF_T // 2) as i:
                        for h in range(2):
                            act.wait_ge(s.product, 4 * i + 2 * h + 1)
                            act.wait_ge(s.gate_used, 2 * i + h + 1)
                            act.activation(cols3(act_out[:, h, :]), bank3(ps, 0), ACT.Silu).then_inc(s.gate_free, 1)

                @block.vector
                def _(dve):
                    dve.sem_inc(s.up_free, 1)
                    dve.sem_inc(s.gate_used, 2)
                    with dve.Fori(0, FF_T // 2) as i:
                        for h in range(2):
                            dve.wait_ge(s.product, 4 * i + 2 * h + 2)
                            dve.wait_ge(s.gate_free, 2 * i + h + 2)
                            dve.tensor_tensor(hid[:, ds(2 * i + h, 1), :].rearrange("p a (n c) -> p (a n) c", n=3),
                                              bank3(ps, 3), cols3(act_out[:, h, :]), ALU.mult).then_inc(s.up_free, 1)
                            dve.wait_ge(s.up_free, 2 * i + h + 2)
                            dve.sem_inc(s.gate_used, 1)
        project(nc, ps, d.w_ffn_down[layer], FF_T, DT, lambda k, n: hid[:, k, n * N3:(n + 1) * N3],
                add_to_residual(g), "vector")


def layer0_mixer(nc, g, d, ps):
    with ExitStack() as mem:
        big = mem.enter_context(tensor(nc, "mixer", [P, AB_T, PAD + NT], F32))

        with ExitStack() as inner:
            H = inner.enter_context(tensor(nc, "h_mix", [P, DT, NT], F32))
            rms_norm(nc, g, ps, H, COL["g_mix"])

            def keep(act, m, banks):
                row = big[:, ds(m, 1), PAD:PAD + NT].rearrange("p a (n c) -> p (a n) c", n=3)
                return act.activation(row, banks, ACT.Copy)

            project(nc, ps, d.w_in_ab[0], DT, AB_T, lambda k, n: H[:, k, n * N3:(n + 1) * N3], keep, "scalar")

        store_shift_rows(nc, g, d, ps, big)
        rg_lru(nc, g, d, ps, big)
        with ExitStack() as inner:
            w2a = inner.enter_context(tensor(nc, "w2_a2", [P, RW], F32))
            g2 = inner.enter_context(tensor(nc, "g2", [P, RW], F32))
            kept = inner.enter_context(tensor(nc, "chunk_starts", [P, NT], F32))
            masks = inner.enter_context(tensor(nc, "masks", [P, 10, C], F32))
            token_shift(nc, g, d, ps, big, w2a, g2, kept, masks)
            with nc.Fori(0, RWT) as pair:
                rwkv_pair(nc, g, d, ps, big, w2a, g2, kept, masks, pair)

        tiles = [0, 1, 2, 3, 18, 19, 20, 21]
        project(nc, ps, d.w_out_ab[0], DT, DT,
                lambda k, n: big[:, tiles[k], PAD + n * N3:PAD + (n + 1) * N3], add_to_residual(g), "vector")


def store_shift_rows(nc, g, d, ps, big):
    with ExitStack() as mem:
        rows = mem.enter_context(tensor(nc, "shift_rows", [16, 5, 512], F32))
        with phase(nc, "turned", "copied", "stored") as (s, block):
            @block.tensor
            def _(pe):
                last_row = PAD + T - 1
                for k in range(RWC_T):
                    last = pe.transpose(ps[0:9, k // 4, (k % 4) * P:(k % 4 + 1) * P], big[:, k, last_row:last_row + 9],
                                        g.ident[:, :])
                for k in range(LRU_T):
                    last = pe.transpose(ps[0:11, 4, k * P:(k + 1) * P], big[:, RWC_T + k, last_row - 2:last_row + 9],
                                        g.ident[:, :])
                last.then_inc(s.turned, 1)

            @block.scalar
            def _(act):
                act.wait_ge(s.turned, 1)
                act.activation(rows[0:9, 0:3, :], ps[0:9, 0:3, :], ACT.Copy).then_inc(s.copied, 1)
                act.activation(rows[0:9, 3, 0:256], ps[0:9, 3, 0:256], ACT.Copy).then_inc(s.copied, 1)
                act.activation(rows[0:11, 4, :], ps[0:11, 4, :], ACT.Copy).then_inc(s.copied, 1)

            @block.sync
            def _(sp):
                flat = rows[:, 0:4, :].rearrange("p a c -> p (a c)")
                sp.wait_ge(s.copied, 3)
                sp.dma_start(d.shift_p[0], flat[0:1, 0:RW_COLS]).then_inc(s.stored, 16)
                sp.dma_start(d.shift_s[0], flat[1:9, 0:RW_COLS]).then_inc(s.stored, 16)
                sp.dma_start(d.lru_conv_p[0, 0], rows[0:3, 4, :]).then_inc(s.stored, 16)
                sp.dma_start(d.lru_conv_s[0, :, 2, :], rows[3:11, 4, :]).then_inc(s.stored, 16)
                sp.wait_ge(s.stored, 64)


def rg_lru(nc, g, d, ps, big):
    px = big[:, 14:18, :]
    gate = big[:, 18:22, PAD:PAD + NT]
    par, q = g.par, COL
    with ExitStack() as mem:
        xc = mem.enter_context(tensor(nc, "conv_out", [P, LRU_T, NT], F32))
        gr = mem.enter_context(tensor(nc, "gate_r", [P, LRU_T, NT], F32))
        gi = mem.enter_context(tensor(nc, "gate_i", [P, LRU_T, NT], F32))
        tmp = mem.enter_context(tensor(nc, "lru_tmp", [P, NT], F32))
        wax = mem.enter_context(tensor(nc, "lru_gates", [P, 2, LRU_T, P], F32))
        lam = mem.enter_context(tensor(nc, "lambda", [P, 6, LRU_T], F32))
        h_rows = mem.enter_context(tensor(nc, "h_rows", [9, RW], F32))
        with phase(nc, "cleared", "w_in", "padded", "steps", "lam_x", "gated", "lam_exp", "lam_sum", "lam_log", "conv", "gates_a", "gates_x", "gate_sig",
                   "log_a", "decayed", "tanhs", "under_root", "rooted", "gelus", "scanned", "turned", "rows", "stored", "act_steps", "gate_free") as (s, block):
            @block.gpsimd
            def _(pool):
                pool.memset(wax[:, :, :, :], 0.0).then_inc(s.cleared, 1)
                pool.memset(big[:, 14:18, 0:PAD], 0.0).then_inc(s.padded, 1)

            @block.sync
            def _(sp):
                sp.wait_ge(s.cleared, 1)
                for n, w in enumerate((d.lru_wa, d.lru_wx)):
                    for o in range(2):
                        sp.dma_start(wax[64 * o:64 * o + 64, n, :, 64 * o:64 * o + 64],
                                     w[0].rearrange("(k o) i e -> o i k e", o=2)[o]).then_inc(s.w_in, 16)
                sp.wait_ge(s.rows, 1)
                sp.dma_start(d.lru_h_p[0], h_rows[0:1, :]).then_inc(s.stored, 16)
                sp.dma_start(d.lru_h_s[0], h_rows[1:9, :]).then_inc(s.stored, 16)
                sp.wait_ge(s.stored, 32)

            @block.vector
            def _(dve):
                link = linker(dve, s.steps)
                lq = q["lru_lambda"]
                dve.tensor_scalar(lam[:, 5, :], par[:, lq:lq + 4], -1.0, 40.0, ALU.mult, ALU.min).then_inc(s.lam_x, 1)
                dve.wait_ge(s.lam_exp, 1)
                dve.tensor_scalar(lam[:, 1, :], lam[:, 0, :], 1.0, None, ALU.add).then_inc(s.lam_sum, 1)
                dve.wait_ge(s.lam_log, 1)
                link(dve.tensor_scalar(lam[:, 3, :], lam[:, 1, :], 1.0, 1e-30, ALU.subtract, ALU.max))
                link(dve.reciprocal(lam[:, 4, :], lam[:, 3, :]))
                link(dve.tensor_tensor(lam[:, 3, :], lam[:, 0, :], lam[:, 4, :], ALU.mult))
                link(dve.tensor_tensor(lam[:, 4, :], lam[:, 2, :], lam[:, 3, :], ALU.mult))
                link(dve.scalar_tensor_tensor(lam[:, 4, :], lam[:, 0, :], 2.0 ** -24, lam[:, 4, :], ALU.min, ALU.max))
                link(dve.scalar_tensor_tensor(lam[:, 4, :], par[:, lq:lq + 4], -1.0, lam[:, 4, :], ALU.mult, ALU.max))
                link(dve.tensor_scalar(lam[:, 4, :], lam[:, 4, :], -8.0, None, ALU.mult))
                dve.wait_ge(s.padded, 1)
                cw, cb = q["lru_conv_w"], q["lru_conv_b"]
                c0 = g.conv0[:, :, :].rearrange("p k (b j) -> p k j b", j=3)
                for k in range(LRU_T):
                    w = [par[:, cw + 4 * j + k:cw + 4 * j + k + 1] for j in range(4)]
                    link(dve.tensor_scalar(xc[:, k, 0:T], px[:, k, 1:1 + T], w[0], par[:, cb + k:cb + k + 1], ALU.mult, ALU.add))
                    link(dve.tensor_scalar(xc[:, k, T:NT], c0[:, k, 0, :], w[0], par[:, cb + k:cb + k + 1], ALU.mult, ALU.add))
                    for j in range(1, 4):
                        link(dve.scalar_tensor_tensor(xc[:, k, 0:T], px[:, k, 1 + j:1 + j + T], w[j], xc[:, k, 0:T], ALU.mult, ALU.add))
                        old = c0[:, k, j, :] if j < 3 else px[:, k, PAD + T:PAD + NT]
                        link(dve.scalar_tensor_tensor(xc[:, k, T:NT], old, w[j], xc[:, k, T:NT], ALU.mult, ALU.add))
                    dve.sem_inc(s.conv, 1)
                for k in range(LRU_T):
                    dve.wait_ge(s.gate_sig, 2 * k + 2)
                    dve.tensor_scalar(gr[:, k, :], gr[:, k, :], lam[:, 4, k:k + 1], None, ALU.mult).then_inc(s.log_a, 1)
                    dve.tensor_tensor(gi[:, k, :], gi[:, k, :], xc[:, k, :], ALU.mult).then_inc(s.gated, 1)
                for k in range(LRU_T):
                    dve.wait_ge(s.tanhs, k + 1)
                    link(dve.tensor_scalar(tmp[:, :], gr[:, k, :], 1.0, None, ALU.add))
                    link(dve.reciprocal(tmp[:, :], tmp[:, :]))
                    dve.scalar_tensor_tensor(gr[:, k, :], gr[:, k, :], 2.0, tmp[:, :], ALU.mult, ALU.mult).then_inc(s.under_root, 1)
                    dve.wait_ge(s.under_root, k + 1)
                dve.wait_ge(s.gated, LRU_T)
                for k in range(LRU_T):
                    dve.wait_ge(s.rooted, k + 1)
                    link(dve.tensor_tensor(gi[:, k, :], gi[:, k, :], gr[:, k, :], ALU.mult))
                    link(dve.tensor_tensor_scan(gr[:, k, 0:T], xc[:, k, 0:T], gi[:, k, 0:T], 0.0, ALU.mult, ALU.add))
                    link(dve.tensor_tensor(gr[:, k, T:NT], xc[:, k, T:NT], g.h0[:, k, :], ALU.mult))
                    dve.tensor_tensor(gr[:, k, T:NT], gr[:, k, T:NT], gi[:, k, T:NT], ALU.add).then_inc(s.scanned, 1)
                for k in range(LRU_T):
                    dve.wait_ge(s.gelus, k + 1)
                    dve.wait_ge(s.scanned, k + 1)
                    link(dve.tensor_tensor(gate[:, k, :], gate[:, k, :], gr[:, k, :], ALU.mult))
                dve.wait_ge(s.turned, 1)
                dve.tensor_copy(h_rows[:, :], ps[0:9, 6, :]).then_inc(s.rows, 1)

            @block.tensor
            def _(pe):
                pe.wait_ge(s.w_in, 64)
                for k in range(LRU_T):
                    pe.wait_ge(s.conv, k + 1)
                    for o, done in ((0, s.gates_a), (1, s.gates_x)):
                        if k:
                            pe.wait_ge(s.gate_sig, 2 * k + o - 1)
                        for n in range(3):
                            last = pe.matmul(ps[:, 3 * o + n, 0:N3], wax[:, o, k, :], xc[:, k, n * N3:(n + 1) * N3],
                                             start=True, stop=True)
                        last.then_inc(done, 1)
                pe.wait_ge(s.scanned, LRU_T)
                for k in range(LRU_T):
                    last = pe.transpose(ps[0:9, 6, k * P:(k + 1) * P], gr[:, k, T - 1:NT], g.ident[:, :])
                last.then_inc(s.turned, 1)

            @block.scalar
            def _(act):
                act.wait_ge(s.lam_x, 1)
                act.activation(lam[:, 0, :], lam[:, 5, :], ACT.Exp).then_inc(s.lam_exp, 1)
                act.wait_ge(s.lam_sum, 1)
                act.activation(lam[:, 2, :], lam[:, 1, :], ACT.Ln).then_inc(s.lam_log, 1)
                for k in range(LRU_T):
                    act.wait_ge(s.gates_a, k + 1)
                    act.activation(cols3(gr[:, k, :]), bank3(ps, 0), ACT.Sigmoid, bias=par[:, q["lru_ba"] + k:q["lru_ba"] + k + 1]).then_inc(s.gate_sig, 1)
                    act.wait_ge(s.gates_x, k + 1)
                    act.activation(cols3(gi[:, k, :]), bank3(ps, 3), ACT.Sigmoid, bias=par[:, q["lru_bx"] + k:q["lru_bx"] + k + 1]).then_inc(s.gate_sig, 1)
                act.wait_ge(s.gated, LRU_T)
                for k in range(LRU_T):
                    act.activation(xc[:, k, :], gr[:, k, :], ACT.Exp).then_inc(s.decayed, 1)
                    act.wait_ge(s.decayed, k + 1)
                    act.activation(gr[:, k, :], gr[:, k, :], ACT.Tanh, scale=-1.0).then_inc(s.tanhs, 1)
                for k in range(LRU_T):
                    act.wait_ge(s.under_root, k + 1)
                    act.activation(gr[:, k, :], gr[:, k, :], ACT.Sqrt).then_inc(s.rooted, 1)
                for k in range(LRU_T):
                    act.activation(gate[:, k, :], gate[:, k, :], ACT.Gelu_apprx_tanh).then_inc(s.gelus, 1)


def token_shift(nc, g, d, ps, big, w2a, g2, kept, masks):
    mu = COL["mu_shift"]
    with ExitStack() as mem:
        diff = mem.enter_context(tensor(nc, "diff", [P, 2, T], F32))
        sdiff = mem.enter_context(tensor(nc, "sample_diff", [P, RWC_T, NS], F32))
        with phase(nc, "padded", "w_in", "steps", "pool_steps", "shifted", "act_steps", "mask_steps") as (s, block):
            @block.sync
            def _(sp):
                sp.dma_start(w2a[0:64, :], d.rw_w2[0]).then_inc(s.w_in, 16)
                sp.dma_start(w2a[64:128, :], d.rw_a2[0]).then_inc(s.w_in, 16)
                sp.dma_start(g2[:, :], d.rw_g2[0]).then_inc(s.w_in, 16)
                sp.wait_ge(s.w_in, 48)

            @block.vector
            def _(dve):
                link = linker(dve, s.steps)
                link(dve.memset(big[:, 0:RWC_T, 0:PAD], 0.0))
                p_s = big[:, 0:RWC_T, PAD + T:PAD + NT]
                link(dve.tensor_tensor(sdiff[:, :, :], g.shift0[:, :, :], p_s, ALU.subtract))
                link(dve.tensor_tensor(sdiff[:, :, :], sdiff[:, :, :],
                                       g.par[:, mu:mu + RWC_T].unsqueeze(2).to_broadcast([P, RWC_T, NS]), ALU.mult))
                link(dve.tensor_tensor(p_s, p_s, sdiff[:, :, :], ALU.add))
                order = [12, 13] + list(range(12))
                for n, k in enumerate(order):
                    row = big[:, k, :]
                    link(dve.tensor_tensor(diff[:, n % 2, :], row[:, PAD - 1:PAD - 1 + T], row[:, PAD:PAD + T], ALU.subtract))
                    dve.scalar_tensor_tensor(row[:, PAD:PAD + T], diff[:, n % 2, :], g.par[:, mu + k:mu + k + 1],
                                             row[:, PAD:PAD + T], ALU.mult, ALU.add).then_inc(s.shifted, 1)

            @block.scalar
            def _(act):
                act.wait_ge(s.shifted, 2)
                act.wait_ge(s.steps, 4)
                act.activation(big[:, 13, PAD:PAD + NT], big[:, 13, PAD:PAD + NT], ACT.Sigmoid).then_inc(s.act_steps, 1)
                act.activation(big[0:64, 12, PAD:PAD + NT], big[0:64, 12, PAD:PAD + NT], ACT.Tanh).then_inc(s.act_steps, 1)

            @block.gpsimd
            def _(pool):
                link = linker(pool, s.pool_steps)
                link(pool.memset(kept[:, :], 1.0))
                link(pool.memset(kept[:, 0:T:C], 0.0))
                link(pool.memset(kept[:, T:NT], 0.0))
                for m in range(10):
                    link(pool.memset(masks[:, m, :], 1.0))
                for h in range(2):
                    rows = slice(64 * h, 64 * h + 64)

                    def cut(m, pattern, base, mult, keep_where, shape=None):
                        v = masks[rows, m, :]
                        if shape:
                            v = v.rearrange("p (a b) -> p a b", b=shape)
                        link(pool.affine_select(out=v, in_=v, compare_op=keep_where, fill=0.0, base=base,
                                                pattern=pattern, channel_multiplier=mult))
                    cut(0, [[1, C]], 0, -1, ALU.is_gt)
                    cut(1, [[1, C]], 0, -1, ALU.is_ge)
                    cut(2, [[-1, C]], 0, 1, ALU.is_gt)
                    for lvl in range(6):
                        b = 1 << lvl
                        n = C // (2 * b)
                        v = masks[rows, 3 + lvl, :].rearrange("p (a b) -> p a b", b=2 * b)
                        link(pool.affine_select(out=v, in_=v, compare_op=ALU.is_ge, fill=0.0, base=0,
                                                pattern=[[-2 * b, n], [0, 2 * b]], channel_multiplier=1))
                        link(pool.affine_select(out=v, in_=v, compare_op=ALU.is_gt, fill=0.0, base=b,
                                                pattern=[[2 * b, n], [0, 2 * b]], channel_multiplier=-1))
                        link(pool.affine_select(out=v, in_=v, compare_op=ALU.is_ge, fill=0.0, base=-b,
                                                pattern=[[0, n], [1, 2 * b]], channel_multiplier=0))
                    v = masks[rows, 9, :].rearrange("p (a b) -> p a b", b=2)
                    link(pool.affine_select(out=v, in_=v, compare_op=ALU.is_equal, fill=0.0, base=-1,
                                            pattern=[[-2, C // 2], [0, 2]], channel_multiplier=1))
                    link(pool.affine_select(out=v, in_=v, compare_op=ALU.is_equal, fill=0.0, base=0,
                                            pattern=[[0, C // 2], [1, 2]], channel_multiplier=0))


def rwkv_pair(nc, g, d, ps, big, w2a, g2, kept, masks, i):
    par = g.par
    with ExitStack() as mem:
        def sb(name, shape):
            return mem.enter_context(tensor(nc, name, shape, F32))

        names = ["r", "k", "v", "lw", "cum", "a", "kk", "bonus", "e_cum", "e_neg", "e_prev", "tmp"]
        buf = {n: sb(f"pair_{n}", [P, NT]) for n in names}
        rs, ks, vs, lw, cum, a, kk, bonus, e_cum, e_neg, e_prev, tmp = (buf[n] for n in names)
        col = sb("pair_par", [P, 8])
        w2s, g2s = sb("w2_slice", [P, P]), sb("g2_slice", [P, P])
        vec = sb("sample_vec", [P, 5, NS])
        vs8 = sb("sample_v", [P, NS])
        dend = sb("chunk_decay", [P, NC])
        S = sb("state", [P, 3, HD])
        u = sb("u", [P, 2, 2, HD])
        s8 = sb("sample_state", [P, NS, HD])
        t8 = sb("sample_tmp", [P, 2, NS, HD])
        p8 = sb("sample_prod", [P, NS, HD])
        sa = sb("sample_sa", [P, NS])
        s_rows = sb("state_rows_out", [HD, P])
        inv, prod = sb("inverse", [P, T]), sb("level_product", [P, T])
        spare = [big[:, 14 + n, 0:T] for n in range(4)]
        a_tok, b_tok, k_tok, v_tok = spare
        inv_t, lt, mak, mrb, mrk = (x[:, 0:T] for x in (lw, cum, e_cum, e_neg, e_prev))
        gt, hh = kk[:, 0:T], ks[:, 0:T]

        def tokm(x):
            return x.rearrange("p (t h c) -> p t h c", t=TT, h=2)

        def halves(x, b):
            return x[:, b * 512:(b + 1) * 512].rearrange("p (n c) -> p n c", c=64)

        def bank(b):
            return ps[:, b, :].rearrange("p (n c) -> p n c", c=64)

        def mask(m):
            return masks[:, m, :].unsqueeze(1).to_broadcast([P, 8, C])

        two = (0, 1)

        def blocks(half):
            for t in range(4):
                for cp in two:
                    for hp in two:
                        c = 2 * (4 * half + t) + cp
                        yield (slice(t * P + hp * 64, t * P + hp * 64 + 64), slice(64 * cp, 64 * cp + 64),
                               slice(64 * hp, 64 * hp + 64), slice(c * C, (c + 1) * C), 4 * half + t, hp)

        with phase(nc, "copied", "z_made", "a_made", "sig", "lw_done", "dve", "cummed", "exps", "sq", "ssum", "root",
                   "bon", "bsum", "ready", "turned", "tok_copied", "gram", "gram_taken", "level_t", "p_made",
                   "p_taken", "x_made", "x_taken", "xt_made", "xt_taken", "g_made", "g_taken", "u_made", "u_taken",
                   "s_made", "s_taken", "y_made", "y_taken", "vec_taken", "spread", "spread_made", "spread_used",
                   "s8_in", "s8_done", "stored", "mean", "cent", "csq", "var", "vroot", "gsum", "rows_t", "rows_c",
                   "decayed", "y8", "act_steps") as (s, block):

            @block.sync
            def _(sp):
                states = d.state_rwkv_wkv[0].rearrange("b h v k -> b (h v) k")
                sp.dma_start(s8[:, :, :], states[:, ds(i * P, P), :].rearrange("b p k -> p b k")).then_inc(s.s8_in, 16)
                sp.wait_ge(s.s8_done, 1)
                out_s = d.wkv_s[0].rearrange("b h v k -> b (h v) k")
                sp.dma_start(out_s[:, ds(i * P, P), :].rearrange("b p k -> p b k"), s8[:, :, :]).then_inc(s.stored, 16)
                sp.wait_ge(s.rows_c, 1)
                sp.dma_start(d.wkv_p[0, 0, ds(2 * i, 2), :, :].rearrange("h v k -> v h k"),
                             s_rows[:, :].rearrange("v (h k) -> v h k", h=2)).then_inc(s.stored, 16)
                sp.wait_ge(s.stored, 32)

            @block.gpsimd
            def _(pool):
                pool.tensor_copy(w2s[:, :], w2a[:, ds(i * P, P)]).then_inc(s.copied, 1)
                pool.tensor_copy(col[:, 0:7], par[:, ds(COL["rw_w0"] + i, 7, 4)]).then_inc(s.copied, 1)
                for x, t in ((ks, 4), (rs, 0), (vs, 8)):
                    pool.tensor_copy(x[:, :], big[:, ds(t + i, 1), PAD:PAD + NT].rearrange("p a c -> p (a c)")).then_inc(s.copied, 1)
                pool.tensor_copy(g2s[:, :], g2[:, ds(i * P, P)]).then_inc(s.copied, 1)
                pool.memset(S[:, 0, :], 0.0).then_inc(s.copied, 1)
                pool.wait_ge(s.gram_taken, 10)
                for lvl in range(1, 6):
                    if lvl > 1:
                        pool.wait_ge(s.p_taken, 2 * (lvl - 1))
                    for b in two:
                        pool.tensor_tensor(halves(tmp, b), halves(lt, b), mask(3 + lvl), ALU.mult).then_inc(s.level_t, 1)

            @block.vector
            def _(dve):
                link = linker(dve, s.dve)
                w0, a0, c_kk, c_ka, c_rk, lnw, lnb = (col[:, n:n + 1] for n in range(7))
                dve.wait_ge(s.copied, 5)
                link(dve.tensor_scalar(col[:, 7:8], c_ka, -1.0, 1.0, ALU.mult, ALU.add))
                link(dve.tensor_scalar(kk[:, :], ks[:, :], c_kk, None, ALU.mult))
                dve.sem_inc(s.sq, 1)
                dve.wait_ge(s.sig, 2)
                link(dve.tensor_scalar(lw[:, :], lw[:, :], DECAY, None, ALU.mult))
                link(dve.tensor_copy(vec[:, 0, :], lw[:, T:NT]))
                link(dve.memset(lw[:, T:NT], 0.0))
                link(dve.tensor_tensor_scan(cum[:, :], kept[:, :], lw[:, :], 0.0, ALU.mult, ALU.add))
                link(dve.tensor_tensor(e_prev[:, :], cum[:, :], lw[:, :], ALU.subtract))
                dve.sem_inc(s.cummed, 1)
                link(dve.tensor_scalar(bonus[:, :], a[:, :], c_ka, col[:, 7:8], ALU.mult, ALU.add))
                link(dve.tensor_tensor(ks[:, :], ks[:, :], bonus[:, :], ALU.mult))
                link(dve.scalar_tensor_tensor(bonus[:, :], rs[:, :], c_rk, ks[:, :], ALU.mult, ALU.mult))
                dve.sem_inc(s.bon, 1)
                dve.wait_ge(s.root, 1)
                link(dve.tensor_scalar(tmp[:, :], tmp[:, :], 1e-12, None, ALU.max))
                link(dve.reciprocal(tmp[:, :], tmp[:, :]))
                link(dve.tensor_tensor(kk[:, :], kk[:, :], tmp[:, :], ALU.mult))
                dve.wait_ge(s.bsum, 1)
                link(dve.tensor_tensor(cols3(bonus[:, :]), bank3(ps, 3), cols3(vs[:, :]), ALU.mult))
                dve.wait_ge(s.exps, 4)
                link(dve.tensor_tensor(a[:, :], kk[:, :], a[:, :], ALU.mult))
                link(dve.tensor_tensor(a[:, :], a[:, :], e_neg[:, :], ALU.mult))
                dve.sem_inc(s.ready, 1)
                link(dve.scalar_tensor_tensor(kk[:, :], kk[:, :], -1.0, e_prev[:, :], ALU.mult, ALU.mult))
                dve.sem_inc(s.ready, 1)
                link(dve.tensor_tensor(ks[:, :], ks[:, :], e_neg[:, :], ALU.mult))
                dve.sem_inc(s.ready, 1)
                link(dve.tensor_tensor(rs[:, :], rs[:, :], e_cum[:, :], ALU.mult))
                dve.sem_inc(s.ready, 1)
                for n, x in ((1, kk), (2, a), (3, ks), (4, rs)):
                    link(dve.tensor_copy(vec[:, n, :], x[:, T:NT]))
                link(dve.tensor_copy(vs8[:, :], vs[:, T:NT]))
                link(dve.tensor_copy(dend[:, :], e_cum[:, C - 1:T:C]))
                dve.sem_inc(s.vec_taken, 1)
                for n in range(1, 8, 2):
                    dve.wait_ge(s.turned, n + 1)
                    dst = (b_tok, a_tok, k_tok, v_tok)[n // 2]
                    dve.tensor_copy(dst[:, 512:1024], ps[:, n, :]).then_inc(s.tok_copied, 1)
                for n, (dst, m) in enumerate(((lt, 0), (inv, 9), (mak, 0), (mrb, 1), (mrk, 1))):
                    for h in two:
                        dve.wait_ge(s.gram, 2 * n + h + 1)
                        dve.tensor_tensor(tokm(dst)[:, :, h, :], bank((2 * n + h) % 6), mask(m), ALU.mult).then_inc(s.gram_taken, 1)
                dve.wait_ge(s.gram_taken, 10)
                idb = g.ident2[:, :].unsqueeze(1).to_broadcast([P, 8, C])
                for b in two:
                    link(dve.tensor_tensor(halves(inv_t, b), halves(lt, b), mask(3), ALU.mult))
                    link(dve.tensor_tensor(halves(inv_t, b), halves(inv_t, b), idb, ALU.add))
                    link(dve.tensor_tensor(halves(inv, b), halves(inv, b), idb, ALU.add))
                    dve.sem_inc(s.x_taken, 1)
                    dve.sem_inc(s.xt_taken, 1)
                for lvl in range(1, 6):
                    for b in two:
                        dve.wait_ge(s.xt_made, 2 * (lvl - 1) + b + 1)
                        if lvl < 5:
                            dve.wait_ge(s.x_made, 2 * (lvl - 1) + b + 1)
                            dve.tensor_tensor(halves(inv, b), bank(2 + b), halves(inv, b), ALU.add).then_inc(s.x_taken, 1)
                        dve.tensor_tensor(halves(inv_t, b), bank(4 + b), halves(inv_t, b), ALU.add).then_inc(s.xt_taken, 1)
                dve.wait_ge(s.s8_in, 16)
                sample_step(dve, link, s, g, ps, s8, t8, p8, sa, vec, vs8, tmp)
                dve.wait_ge(s.g_taken, 6)
                for c in range(NC):
                    dve.wait_ge(s.u_made, c + 1)
                    rows = slice(64 * (c % 2), 64 * (c % 2) + 64)
                    if c >= 2:
                        dve.wait_ge(s.y_made, c - 1)
                    dve.tensor_tensor(u[rows, (c // 2) % 2, :, :], ps[rows, 4:6, 0:HD],
                                      tokm(hh)[rows, c // 2, :, :], ALU.add).then_inc(s.u_taken, 1)
                    dve.wait_ge(s.s_made, c + 1)
                    dve.wait_ge(s.decayed, c + 1)
                    dve.scalar_tensor_tensor(S[:, (c + 1) % 2, :], ps[:, 6 + c % 2, 0:HD], dend[:, c:c + 1], S[:, 2, :],
                                             ALU.mult, ALU.add).then_inc(s.s_taken, 1)
                dve.wait_ge(s.y_taken, 1)
                for cp in two:
                    y = tokm(tmp[:, 0:T])[:, :, cp, :]
                    link(dve.tensor_tensor(y, y, bank(2 + cp), ALU.add))
                dve.sem_inc(s.y8, 1)
                dve.wait_ge(s.mean, 1)
                link(dve.scalar_tensor_tensor(cols3(e_cum[:, :]), bank3(ps, 2), -1.0 / HD, cols3(tmp[:, :]), ALU.mult, ALU.add))
                dve.sem_inc(s.cent, 1)
                dve.wait_ge(s.vroot, 1)
                link(dve.reciprocal(e_prev[:, :], e_prev[:, :]))
                link(dve.tensor_tensor(e_cum[:, :], e_cum[:, :], e_prev[:, :], ALU.mult))
                link(dve.tensor_scalar(e_cum[:, :], e_cum[:, :], lnw, lnb, ALU.mult, ALU.add))
                link(dve.tensor_tensor(e_cum[:, :], e_cum[:, :], bonus[:, :], ALU.add))
                dve.wait_ge(s.gsum, 1)
                row = big[:, ds(i, 1), PAD:PAD + NT].rearrange("p a (n c) -> p (a n) c", n=3)
                link(dve.tensor_tensor(row, bank3(ps, 2), cols3(e_cum[:, :]), ALU.mult))

            @block.scalar
            def _(act):
                w0, a0 = col[:, 0:1], col[:, 1:2]
                act.wait_ge(s.copied, 2)
                act.wait_ge(s.z_made, 1)
                act.activation(cols3(lw[:, :]), bank3(ps, 0), ACT.Sigmoid, bias=w0).then_inc(s.sig, 1)
                act.wait_ge(s.a_made, 1)
                act.activation(cols3(a[:, :]), bank3(ps, 3), ACT.Sigmoid, bias=a0).then_inc(s.sig, 1)
                act.wait_ge(s.sq, 1)
                act.activation(tmp[:, :], kk[:, :], ACT.Square).then_inc(s.act_steps, 1)
                act.wait_ge(s.cummed, 1)
                act.activation(e_neg[:, :], cum[:, :], ACT.Exp, scale=-1.0).then_inc(s.exps, 1)
                act.activation(e_prev[:, :], e_prev[:, :], ACT.Exp).then_inc(s.exps, 1)
                act.activation(e_cum[:, :], cum[:, :], ACT.Exp).then_inc(s.exps, 1)
                act.activation(vec[:, 0, :], vec[:, 0, :], ACT.Exp).then_inc(s.exps, 1)
                act.wait_ge(s.ssum, 1)
                act.activation(cols3(tmp[:, :]), bank3(ps, 0), ACT.Sqrt).then_inc(s.root, 1)
                for n in range(0, 8, 2):
                    act.wait_ge(s.turned, n + 1)
                    dst = (b_tok, a_tok, k_tok, v_tok)[n // 2]
                    act.activation(dst[:, 0:512], ps[:, n, :], ACT.Copy).then_inc(s.act_steps, 1)
                for lvl in range(1, 6):
                    for b in two:
                        act.wait_ge(s.p_made, 2 * (lvl - 1) + b + 1)
                        if lvl > 1:
                            act.wait_ge(s.xt_made, 2 * (lvl - 1))
                        act.activation(halves(prod, b), bank(b), ACT.Copy).then_inc(s.p_taken, 1)
                for n, dst in enumerate((gt, prod, hh)):
                    for b in two:
                        act.wait_ge(s.g_made, 2 * n + b + 1)
                        to = tokm(dst)[:, :, b, :] if n == 0 else halves(dst, b)
                        act.activation(to, bank(2 * n + b), ACT.Copy).then_inc(s.g_taken, 1)
                for c in range(NC):
                    if c:
                        act.wait_ge(s.s_taken, c)
                    act.activation(S[:, 2, :], S[:, c % 2, :], ACT.Copy, scale=dend[:, c:c + 1]).then_inc(s.decayed, 1)
                act.wait_ge(s.y_made, NC)
                act.activation(tmp[:, 0:T].rearrange("p (b c) -> p b c", b=2), ps[:, 0:2, :], ACT.Copy).then_inc(s.y_taken, 1)
                act.wait_ge(s.rows_t, 1)
                act.activation(s_rows[:, :], ps[0:HD, 5, 0:P], ACT.Copy).then_inc(s.rows_c, 1)
                act.wait_ge(s.cent, 1)
                act.activation(e_neg[:, :], e_cum[:, :], ACT.Square).then_inc(s.csq, 1)
                act.wait_ge(s.var, 1)
                act.activation(cols3(e_prev[:, :]), bank3(ps, 5), ACT.Sqrt, scale=1.0 / HD, bias=g.epsc[:, 1:2]).then_inc(s.vroot, 1)

            @block.tensor
            def _(pe):
                def head_sums(x, first, done):
                    for n in range(3):
                        last = pe.matmul(ps[:, first + n, 0:N3], g.blockones[:, :], x[:, n * N3:(n + 1) * N3], start=True, stop=True)
                    last.then_inc(done, 1)

                def block_row(w, x, first, done):
                    for n in range(3):
                        last = pe.matmul(ps[:, first + n, 0:N3], w, x[:, PAD + n * N3:PAD + (n + 1) * N3], start=True, stop=True)
                    last.then_inc(done, 1)

                pe.wait_ge(s.copied, 1)
                block_row(w2s[0:64, :], big[0:64, 12, :], 0, s.z_made)
                block_row(w2s[64:128, :], big[64:128, 12, :], 3, s.a_made)
                pe.wait_ge(s.act_steps, 1)
                head_sums(tmp, 0, s.ssum)
                pe.wait_ge(s.sig, 2)
                pe.wait_ge(s.bon, 1)
                head_sums(bonus, 3, s.bsum)
                pe.wait_ge(s.root, 1)
                pe.wait_ge(s.ready, 4)
                for n in range(8):
                    src = (a, kk, ks, vs)[n // 2]
                    for t in range(4):
                        tt = 4 * (n % 2) + t
                        last = pe.transpose(ps[:, n, t * P:(t + 1) * P], src[:, tt * P:(tt + 1) * P], g.ident[:, :])
                    last.then_inc(s.turned, 1)
                gram = ((a, kk), (kk, a), (ks, kk), (a, rs), (ks, rs))
                for n, (l, r) in enumerate(gram):
                    for h in two:
                        g_at = 2 * n + h
                        hp = slice(64 * h, 64 * h + 64)
                        if g_at < 6:
                            if g_at % 2:
                                pe.wait_ge(s.tok_copied, g_at // 2 + 1)
                            else:
                                pe.wait_ge(s.act_steps, 2 + g_at // 2)
                        else:
                            pe.wait_ge(s.gram_taken, g_at - 5)
                        for c in range(NC):
                            cp, cols = slice(64 * (c % 2), 64 * (c % 2) + 64), slice(c * C, (c + 1) * C)
                            last = pe.matmul(ps[cp, g_at % 6, (c // 2) * 64:(c // 2 + 1) * 64], l[hp, cols], r[hp, cols],
                                             start=True, stop=True)
                        last.then_inc(s.gram, 1)
                pe.wait_ge(s.gram_taken, 10)
                for lvl in range(1, 6):
                    for b in two:
                        pe.wait_ge(s.level_t, 2 * (lvl - 1) + b + 1)
                        pe.wait_ge(s.x_taken, 2 * (lvl - 1) + b + 1)
                        for at, cp, hp, _, tt, h in blocks(b):
                            m = slice(tt * P + h * 64, tt * P + h * 64 + 64)
                            last = pe.matmul(ps[cp, b, at], tmp[cp, m], inv[cp, m], start=True, stop=True)
                        last.then_inc(s.p_made, 1)
                    for b in two:
                        pe.wait_ge(s.p_taken, 2 * (lvl - 1) + b + 1)
                        pe.wait_ge(s.xt_taken, 2 * (lvl - 1) + b + 1)
                        if lvl < 5:
                            for at, cp, hp, _, tt, h in blocks(b):
                                m = slice(tt * P + h * 64, tt * P + h * 64 + 64)
                                last = pe.matmul(ps[cp, 2 + b, at], inv_t[cp, m], prod[cp, m], start=True, stop=True)
                            last.then_inc(s.x_made, 1)
                        for at, cp, hp, _, tt, h in blocks(b):
                            m = slice(tt * P + h * 64, tt * P + h * 64 + 64)
                            last = pe.matmul(ps[cp, 4 + b, at], prod[cp, m], inv_t[cp, m], start=True, stop=True)
                        last.then_inc(s.xt_made, 1)
                pe.wait_ge(s.xt_taken, 12)
                for cp in two:
                    cpr = slice(64 * cp, 64 * cp + 64)
                    for tt in range(TT):
                        for h in two:
                            hpr = slice(64 * h, 64 * h + 64)
                            m = slice(tt * P + h * 64, tt * P + h * 64 + 64)
                            last = pe.matmul(ps[hpr, cp, tt * C:(tt + 1) * C], a_tok[cpr, m], inv_t[cpr, m],
                                             start=True, stop=True)
                    last.then_inc(s.g_made, 1)
                for n, (l, r) in enumerate(((mak, v_tok), (inv_t, prod))):
                    for b in two:
                        if n:
                            pe.wait_ge(s.g_taken, 3 + b)
                        for at, cp, hp, _, tt, h in blocks(b):
                            m = slice(tt * P + h * 64, tt * P + h * 64 + 64)
                            last = pe.matmul(ps[cp, 2 * (n + 1) + b, at], l[cp, m], r[cp, m], start=True, stop=True)
                        last.then_inc(s.g_made, 1)
                pe.wait_ge(s.act_steps, 5)
                pe.wait_ge(s.tok_copied, 4)
                for n in range(5):
                    pe.wait_ge(s.spread, n + 1)
                    if n >= 2:
                        pe.wait_ge(s.spread_used, n - 1)
                    pe.matmul(ps[:, 6 + n % 2, :], g.blockones[:, :], t8[:, n % 2, :, :].rearrange("p b k -> p (b k)"),
                              start=True, stop=True).then_inc(s.spread_made, 1)
                pe.wait_ge(s.spread_used, 5)
                pe.wait_ge(s.g_taken, 6)
                pe.wait_ge(s.copied, 7)
                for c in range(NC):
                    tt, cp = c // 2, c % 2
                    cpr = slice(64 * cp, 64 * cp + 64)
                    ub = (c // 2) % 2
                    cols = slice(c * C, (c + 1) * C)
                    if c:
                        pe.wait_ge(s.s_taken, c)
                    for h in two:
                        hpr = slice(64 * h, 64 * h + 64)
                        last = pe.matmul(ps[cpr, 4 + h, 0:HD], gt[hpr, cols], S[hpr, c % 2, :], start=True, stop=True)
                    last.then_inc(s.u_made, 1)
                    heads = [(slice(64 * h, 64 * h + 64), slice(tt * P + h * 64, tt * P + h * 64 + 64),
                              u[cpr, ub, h, :], ps[64 * h:64 * h + 64, 6 + cp, 0:HD],
                              ps[64 * h:64 * h + 64, c // 8, (c % 8) * C:(c % 8 + 1) * C],
                              ps[64 * h:64 * h + 64, 2 + cp, tt * C:(tt + 1) * C]) for h in two]
                    for hpr, m, _, new, y_s, y in heads:
                        pe.matmul(y_s, S[hpr, c % 2, :], rs[hpr, cols], start=True, stop=True)
                        pe.matmul(new, k_tok[cpr, m], v_tok[cpr, m], start=True, stop=False)
                        pe.matmul(y, v_tok[cpr, m], mrk[cpr, m], start=True, stop=False)
                    pe.wait_ge(s.u_taken, c + 1)
                    for hpr, m, uh, new, _, y in heads:
                        last = pe.matmul(new, b_tok[cpr, m], uh, start=False, stop=True)
                    last.then_inc(s.s_made, 1)
                    for hpr, m, uh, new, _, y in heads:
                        last = pe.matmul(y, uh, mrb[cpr, m], start=False, stop=True)
                    last.then_inc(s.y_made, 1)
                pe.wait_ge(s.y_taken, 1)
                pe.wait_ge(s.s_taken, NC)
                pe.transpose(ps[0:HD, 5, 0:P], S[:, NC % 2, :], g.ident[:, :]).then_inc(s.rows_t, 1)
                pe.wait_ge(s.y8, 2)
                head_sums(tmp, 2, s.mean)
                pe.wait_ge(s.csq, 1)
                pe.wait_ge(s.rows_c, 1)
                head_sums(e_neg, 5, s.var)
                pe.wait_ge(s.cent, 1)
                block_row(g2s[:, :], big[:, 13, :], 2, s.gsum)


def sample_step(dve, link, s, g, ps, s8, t8, p8, sa, vec, vs8, y):
    order = [1, 0, 2, 3, 4]

    def fill(n):
        if n >= 2:
            dve.wait_ge(s.spread_made, n - 1)
        link(dve.tensor_tensor(t8[:, n % 2, :, :], g.ident2[:, :].unsqueeze(1).to_broadcast([P, NS, HD]),
                               vec[:, order[n], :].unsqueeze(2).to_broadcast([P, NS, HD]), ALU.mult))
        dve.sem_inc(s.spread, 1)

    def spread(n):
        dve.wait_ge(s.spread_made, n + 1)
        return ps[:, 6 + n % 2, :].rearrange("p (b k) -> p b k", k=HD)

    fill(0)
    fill(1)
    for n in range(5):
        x = spread(n)
        if n == 0:
            link(dve.tensor_tensor(p8[:, :, :], s8[:, :, :], x, ALU.mult))
            link(dve.tensor_reduce(sa[:, :], p8[:, :, :], AX.X, ALU.add))
        elif n == 1:
            link(dve.tensor_tensor(s8[:, :, :], s8[:, :, :], x, ALU.mult))
        elif n < 4:
            rows = (sa, vs8)[n - 2]
            link(dve.tensor_tensor(p8[:, :, :], x, rows[:, :].unsqueeze(2).to_broadcast([P, NS, HD]), ALU.mult))
            link(dve.tensor_tensor(s8[:, :, :], s8[:, :, :], p8[:, :, :], ALU.add))
        else:
            dve.sem_inc(s.s8_done, 1)
            link(dve.tensor_tensor(p8[:, :, :], s8[:, :, :], x, ALU.mult))
            link(dve.tensor_reduce(y[:, T:NT], p8[:, :, :], AX.X, ALU.add))
            dve.sem_inc(s.y8, 1)
        dve.sem_inc(s.spread_used, 1)
        if n + 2 < 5:
            fill(n + 2)


def memory_attention(nc, g, d, ps, layer):
    with ExitStack() as mem:
        Q = mem.enter_context(tensor(nc, "mem_q", [P, MH, NT]))
        kt = mem.enter_context(tensor(nc, "mem_kt", [P, MH, MEM]))
        vtok = mem.enter_context(tensor(nc, "mem_v", [P, 2, MH * P]))
        memory_kv(nc, g, d, ps, layer, kt, vtok)
        with ExitStack() as inner:
            H = inner.enter_context(tensor(nc, "h_mem", [P, DT, NT]))
            rms_norm(nc, g, ps, H, COL["g_mem"] + layer * DT)

            def keep(act, m, banks):
                row = Q[:, ds(m, 1), :].rearrange("p a (n c) -> p (a n) c", n=3)
                return act.activation(row, banks, ACT.Copy)

            project(nc, ps, d.wq_mem[layer], DT, MH, lambda k, n: H[:, k, n * N3:(n + 1) * N3], keep, "scalar")
        norm_queries(nc, g, ps, Q, layer)
        memory_attention_samples(nc, g, d, ps, layer, Q)
        with ExitStack() as inner:
            bufs = record(
                q=inner.enter_context(tensor(nc, "head_q", [P, T])), k=inner.enter_context(tensor(nc, "head_k", [P, MEM])),
                v=inner.enter_context(tensor(nc, "head_v", [P, 2, P])), p=inner.enter_context(tensor(nc, "probs", [P, 2, MEM])),
                pt=inner.enter_context(tensor(nc, "probs_t", [P, 2, MEM])), stat=inner.enter_context(tensor(nc, "stats", [P, 2, 4])))
            with nc.Fori(0, MH) as head:
                memory_attention_head(nc, g, ps, Q, kt, vtok, bufs, head)
        project(nc, ps, d.wo_mem[layer], MH, DT, lambda k, n: Q[:, k, n * N3:(n + 1) * N3], add_to_residual(g), "vector")


def memory_kv(nc, g, d, ps, layer, kt, vtok):
    with ExitStack() as mem:
        mt = mem.enter_context(tensor(nc, "mem_tokens", [P, 2, D]))
        mg = mem.enter_context(tensor(nc, "mem_normed", [P, DT, MEM]))
        W = [mem.enter_context(tensor(nc, f"mem_w{n}", [P, DT, 512])) for n in range(2)]
        ktok = mem.enter_context(tensor(nc, "mem_k", [P, 2, 512]))
        junk = mem.enter_context(tensor(nc, "mem_squares", [P, D]))
        ss = mem.enter_context(tensor(nc, "mem_sums", [P, 12]))
        gain = COL["g_memkv"] + layer * DT
        with phase(nc, "mem_in", ("w_in", 2), "sums", "rms", "rstd", "normed", "turned", "gained", "k_made", "v_made",
                   "k_sums", "k_rms", "k_rstd", "k_normed", "v_taken", "k_turned", "kt_taken", "stored") as (s, block):
            @block.sync
            def _(sp):
                sp.dma_start(mt[:, :, :], d.mem_prompt[0].rearrange("(t p) c -> p t c", p=P)).then_inc(s.mem_in, 16)
                for n, w in enumerate((d.wk_mem, d.wv_mem)):
                    sp.dma_start(W[n][:, :, :], weight_blocks(w[layer], DT)).then_inc(s.w_in[n], 16)
                sp.wait_ge(s.k_normed, 8)
                sp.dma_start(d.mem_k_p[layer, 0].rearrange("(t p) h c -> p t (h c)", p=P), ktok[:, :, :]).then_inc(s.stored, 16)
                sp.wait_ge(s.v_taken, 1)
                sp.dma_start(d.mem_v_p[layer, 0].rearrange("(t p) h c -> p t (h c)", p=P), vtok[:, :, :]).then_inc(s.stored, 16)
                sp.wait_ge(s.stored, 32)

            @block.scalar
            def _(act):
                act.wait_ge(s.mem_in, 16)
                for t in range(2):
                    if t:
                        act.wait_ge(s.sums, 1)
                    act.activation(junk[:, :], mt[:, t, :], ACT.Square, accum_out=ss[:, t:t + 1]).then_inc(s.sums, 1)
                act.wait_ge(s.sums, 2)
                act.activation(ss[:, 2:4], ss[:, 0:2], ACT.Sqrt, scale=1.0 / D, bias=g.epsc[:, 0:1]).then_inc(s.rms, 1)
                act.wait_ge(s.k_made, 2)
                for t in range(2):
                    for h in range(MH):
                        n = 4 * t + h
                        act.wait_ge(s.sums, 2 + n)
                        act.activation(junk[:, 0:P], ps[:, 4 + t, h * P:(h + 1) * P], ACT.Square,
                                       accum_out=ss[:, 4 + n:5 + n]).then_inc(s.sums, 1)
                act.wait_ge(s.sums, 10)
                act.activation(ss[:, 4:12], ss[:, 4:12], ACT.Sqrt, scale=1.0 / P, bias=g.epsc[:, 0:1]).then_inc(s.k_rms, 1)
                act.wait_ge(s.v_made, 2)
                act.activation(vtok[:, :, :], ps[:, 6:8, :], ACT.Copy).then_inc(s.v_taken, 1)
                act.wait_ge(s.k_turned, 1)
                for t in range(2):
                    act.activation(kt[:, :, t * P:(t + 1) * P], ps[:, t, :].rearrange("p (h c) -> p h c", h=MH), ACT.Copy).then_inc(s.kt_taken, 1)

            @block.vector
            def _(dve):
                dve.wait_ge(s.rms, 1)
                dve.reciprocal(ss[:, 2:4], ss[:, 2:4]).then_inc(s.rstd, 1)
                dve.wait_ge(s.rstd, 1)
                for t in range(2):
                    dve.tensor_scalar(mt[:, t, :], mt[:, t, :], ss[:, 2 + t:3 + t], None, ALU.mult).then_inc(s.normed, 1)
                dve.wait_ge(s.turned, 4)
                for k in range(DT):
                    dve.tensor_scalar(mg[:, k, :], ps[:, k // 2, (k % 2) * MEM:(k % 2 + 1) * MEM],
                                      g.par[:, gain + k:gain + k + 1], None, ALU.mult).then_inc(s.gained, 1)
                dve.wait_ge(s.k_rms, 1)
                dve.reciprocal(ss[:, 4:12], ss[:, 4:12]).then_inc(s.k_rstd, 1)
                dve.wait_ge(s.k_rstd, 1)
                for t in range(2):
                    for h in range(MH):
                        dve.scalar_tensor_tensor(ktok[:, t, h * P:(h + 1) * P], ps[:, 4 + t, h * P:(h + 1) * P],
                                                 ss[:, 4 + 4 * t + h:5 + 4 * t + h], g.kn[:, layer, :],
                                                 ALU.mult, ALU.mult).then_inc(s.k_normed, 1)

            @block.tensor
            def _(pe):
                pe.wait_ge(s.normed, 2)
                for k in range(DT):
                    for t in range(2):
                        last = pe.transpose(ps[:, k // 2, (k % 2) * MEM + t * P:(k % 2) * MEM + (t + 1) * P],
                                            mt[:, t, k * P:(k + 1) * P], g.ident[:, :])
                    if k % 2:
                        last.then_inc(s.turned, 1)
                pe.wait_ge(s.gained, DT)
                for n, done in enumerate((s.k_made, s.v_made)):
                    pe.wait_ge(s.w_in[n], 16)
                    for t in range(2):
                        for k in range(DT):
                            last = pe.matmul(ps[:, 4 + 2 * n + t, :], mg[:, k, t * P:(t + 1) * P], W[n][:, k, :],
                                             start=k == 0, stop=k == DT - 1)
                        last.then_inc(done, 1)
                pe.wait_ge(s.k_normed, 8)
                for t in range(2):
                    for h in range(MH):
                        last = pe.transpose(ps[:, t, h * P:(h + 1) * P], ktok[:, t, h * P:(h + 1) * P], g.ident[:, :])
                last.then_inc(s.k_turned, 1)


def norm_queries(nc, g, ps, Q, layer):
    qn = COL["qn_mem"] + layer
    with ExitStack() as mem:
        sq = mem.enter_context(tensor(nc, "q_squares", [P, 2, NT]))
        rms = mem.enter_context(tensor(nc, "q_rms", [P, 2, NT]))
        with phase(nc, "squared", "summed", "rooted", "inverted", "scaled") as (s, block):
            @block.scalar
            def _(act):
                for h in range(MH + 1):
                    if h < MH:
                        if h >= 2:
                            act.wait_ge(s.summed, h - 1)
                        act.activation(sq[:, h % 2, :], Q[:, h, :], ACT.Square).then_inc(s.squared, 1)
                    if h:
                        act.wait_ge(s.summed, h)
                        if h >= 3:
                            act.wait_ge(s.scaled, h - 2)
                        act.activation(cols3(rms[:, (h - 1) % 2, :]), bank3(ps, 3 * ((h - 1) % 2)), ACT.Sqrt, scale=1.0 / P,
                                       bias=g.epsc[:, 0:1]).then_inc(s.rooted, 1)

            @block.tensor
            def _(pe):
                for h in range(MH):
                    pe.wait_ge(s.squared, h + 1)
                    if h >= 2:
                        pe.wait_ge(s.rooted, h - 1)
                    for n in range(3):
                        last = pe.matmul(ps[:, 3 * (h % 2) + n, 0:N3], g.ones[:, :], sq[:, h % 2, n * N3:(n + 1) * N3],
                                         start=True, stop=True)
                    last.then_inc(s.summed, 1)

            @block.vector
            def _(dve):
                for h in range(MH):
                    dve.wait_ge(s.rooted, h + 1)
                    dve.reciprocal(rms[:, h % 2, :], rms[:, h % 2, :]).then_inc(s.inverted, 1)
                    dve.wait_ge(s.inverted, h + 1)
                    dve.scalar_tensor_tensor(Q[:, h, :], Q[:, h, :], g.par[:, qn:qn + 1], rms[:, h % 2, :],
                                             ALU.mult, ALU.mult).then_inc(s.scaled, 1)


def memory_attention_samples(nc, g, d, ps, layer, Q):
    scale = P ** -0.5
    NQ = NS * MH
    with ExitStack() as mem:
        KA = mem.enter_context(tensor(nc, "cache_k", [P, NS, 2, 512]))
        VA = mem.enter_context(tensor(nc, "cache_v", [P, NS, 2, 512]))
        qd = mem.enter_context(tensor(nc, "q_diag", [P, 2, MH, P]))
        prod = mem.enter_context(tensor(nc, "products", [P, 2, 512]))
        Z = mem.enter_context(tensor(nc, "scores", [P, 2, NQ]))
        stat = mem.enter_context(tensor(nc, "s_stats", [NQ, 4]))
        pz = mem.enter_context(tensor(nc, "s_probs", [NQ, MEM]))
        pt = mem.enter_context(tensor(nc, "s_probs_t", [P, 2, NQ]))
        with phase(nc, ("k_in", NS), "v_in", "diag", "spread", "steps", "scored", "z_turned", "shift", "exped",
                   "normed", "p_turned", "p_taken", "valued", "stored") as (s, block):
            @block.sync
            def _(sp):
                for b in range(NS):
                    sp.dma_start(KA[:, b, :, :], d.cache_mem_k[layer, b].rearrange("(t p) h c -> p t (h c)", p=P)).then_inc(s.k_in[b], 16)
                for b in range(NS):
                    sp.dma_start(VA[:, b, :, :], d.cache_mem_v[layer, b].rearrange("(t p) h c -> p t (h c)", p=P)).then_inc(s.v_in, 16)

            @block.gpsimd
            def _(pool):
                for b in range(NS):
                    if b >= 2:
                        pool.wait_ge(s.spread, b - 1)
                    pool.tensor_tensor(qd[:, b % 2, :, :], g.ident[:, :].unsqueeze(1).to_broadcast([P, MH, P]),
                                       Q[:, :, T + b:T + b + 1].to_broadcast([P, MH, P]), ALU.mult).then_inc(s.diag, 1)

            @block.vector
            def _(dve):
                link = linker(dve, s.steps)
                for b in range(NS):
                    dve.wait_ge(s.k_in[b], 16)
                    dve.wait_ge(s.spread, b + 1)
                    for t in range(2):
                        link(dve.tensor_tensor(prod[:, t, :], KA[:, b, t, :], ps[:, b % 2, :], ALU.mult))
                        link(dve.tensor_reduce(Z[:, t, b * MH:(b + 1) * MH], prod[:, t, :].rearrange("p (h c) -> p h c", h=MH),
                                               AX.X, ALU.add))
                    dve.sem_inc(s.scored, 1)
                dve.wait_ge(s.z_turned, 1)
                link(dve.tensor_reduce(stat[:, 0:1], ps[0:NQ, 2, 0:MEM], AX.X, ALU.max))
                dve.tensor_scalar(stat[:, 1:2], stat[:, 0:1], -scale, None, ALU.mult).then_inc(s.shift, 1)
                dve.wait_ge(s.exped, 1)
                link(dve.reciprocal(stat[:, 3:4], stat[:, 2:3]))
                dve.tensor_scalar(pz[:, :], pz[:, :], stat[:, 3:4], None, ALU.mult).then_inc(s.normed, 1)
                dve.wait_ge(s.valued, 1)
                dve.tensor_copy(Q[:, :, T:NT], ps[:, 4, 0:NQ].rearrange("p (h b) -> p h b", h=MH)).then_inc(s.stored, 1)

            @block.scalar
            def _(act):
                act.wait_ge(s.shift, 1)
                act.activation(pz[:, :], ps[0:NQ, 2, 0:MEM], ACT.Exp, scale=scale, bias=stat[:, 1:2],
                               accum_out=stat[:, 2:3]).then_inc(s.exped, 1)
                act.wait_ge(s.p_turned, 1)
                act.activation(pt[:, :, :], ps[:, 3, 0:2 * NQ].rearrange("p (t n) -> p t n", t=2), ACT.Copy).then_inc(s.p_taken, 1)

            @block.tensor
            def _(pe):
                for b in range(NS):
                    pe.wait_ge(s.diag, b + 1)
                    if b >= 2:
                        pe.wait_ge(s.scored, b - 1)
                    pe.matmul(ps[:, b % 2, :], g.ones[:, :], qd[:, b % 2, :, :].rearrange("p h c -> p (h c)"),
                              start=True, stop=True).then_inc(s.spread, 1)
                pe.wait_ge(s.scored, NS)
                for t in range(2):
                    last = pe.transpose(ps[0:NQ, 2, t * P:(t + 1) * P], Z[:, t, :], g.ident[:, :])
                last.then_inc(s.z_turned, 1)
                pe.wait_ge(s.normed, 1)
                for t in range(2):
                    last = pe.transpose(ps[:, 3, t * NQ:(t + 1) * NQ], pz[:, t * P:(t + 1) * P], g.ident[0:NQ, 0:NQ])
                last.then_inc(s.p_turned, 1)
                pe.wait_ge(s.v_in, 16 * NS)
                pe.wait_ge(s.p_taken, 1)
                for b in range(NS):
                    for h in range(MH):
                        for t in range(2):
                            last = pe.matmul(ps[:, 4, h * NS + b:h * NS + b + 1], VA[:, b, t, h * P:(h + 1) * P],
                                             pt[:, t, b * MH + h:b * MH + h + 1], start=t == 0, stop=t == 1)
                last.then_inc(s.valued, 1)


def memory_attention_head(nc, g, ps, Q, kt, vtok, b, i):
    scale = P ** -0.5
    with phase(nc, "copied", "scored", "steps", "shift", "exped", "scaled", "turned", "taken", "valued", "done") as (s, block):
        @block.gpsimd
        def _(pool):
            pool.tensor_copy(b.q[:, :], Q[:, ds(i, 1), 0:T].rearrange("p a c -> p (a c)")).then_inc(s.copied, 1)
            pool.tensor_copy(b.k[:, :], kt[:, ds(i, 1), :].rearrange("p a c -> p (a c)")).then_inc(s.copied, 1)
            pool.tensor_copy(b.v[:, :, :], vtok[:, :, ds(i * P, P)]).then_inc(s.copied, 1)

        @block.tensor
        def _(pe):
            pe.wait_ge(s.copied, 3)
            for n in range(TT + 2):
                if n < TT:
                    if n >= 2:
                        pe.wait_ge(s.exped, n - 1)
                    pe.matmul(ps[:, n % 2, 0:MEM], b.q[:, n * P:(n + 1) * P], b.k[:, :], start=True, stop=True).then_inc(s.scored, 1)
                if 1 <= n <= TT:
                    m = n - 1
                    pe.wait_ge(s.scaled, m + 1)
                    if m >= 2:
                        pe.wait_ge(s.taken, m - 1)
                    for t in range(2):
                        last = pe.transpose(ps[:, 2 + m % 2, t * P:(t + 1) * P], b.p[:, m % 2, t * P:(t + 1) * P], g.ident[:, :])
                    last.then_inc(s.turned, 1)
                if n >= 2:
                    m = n - 2
                    pe.wait_ge(s.taken, m + 1)
                    for t in range(2):
                        last = pe.matmul(ps[:, 4 + m // 4, (m % 4) * P:(m % 4 + 1) * P], b.v[:, t, :], b.pt[:, m % 2, t * P:(t + 1) * P],
                                         start=t == 0, stop=t == 1)
                    last.then_inc(s.valued, 1)

        @block.vector
        def _(dve):
            link = linker(dve, s.steps)
            for n in range(TT + 1):
                if n < TT:
                    dve.wait_ge(s.scored, n + 1)
                    st = b.stat[:, n % 2, :]
                    link(dve.tensor_reduce(st[:, 0:1], ps[:, n % 2, 0:MEM], AX.X, ALU.max))
                    dve.tensor_scalar(st[:, 1:2], st[:, 0:1], -scale, None, ALU.mult).then_inc(s.shift, 1)
                if n:
                    m = n - 1
                    dve.wait_ge(s.exped, m + 1)
                    st = b.stat[:, m % 2, :]
                    link(dve.reciprocal(st[:, 3:4], st[:, 2:3]))
                    dve.tensor_scalar(b.p[:, m % 2, :], b.p[:, m % 2, :], st[:, 3:4], None, ALU.mult).then_inc(s.scaled, 1)

        @block.scalar
        def _(act):
            for n in range(TT + 1):
                if n < TT:
                    act.wait_ge(s.shift, n + 1)
                    if n >= 2:
                        act.wait_ge(s.turned, n - 1)
                    st = b.stat[:, n % 2, :]
                    act.activation(b.p[:, n % 2, :], ps[:, n % 2, 0:MEM], ACT.Exp, scale=scale, bias=st[:, 1:2],
                                   accum_out=st[:, 2:3]).then_inc(s.exped, 1)
                if n:
                    m = n - 1
                    act.wait_ge(s.turned, m + 1)
                    if m >= 2:
                        act.wait_ge(s.valued, m - 1)
                    act.activation(b.pt[:, m % 2, :], ps[:, 2 + m % 2, 0:MEM], ACT.Copy).then_inc(s.taken, 1)
            act.wait_ge(s.valued, TT)
            act.activation(Q[:, ds(i, 1), 0:T].rearrange("p a (n c) -> p (a n) c", n=2), ps[:, 4:6, :], ACT.Copy).then_inc(s.done, 1)


def stick_breaking(nc, g, d, ps):
    wqkv = d.w_qkv_sb[0]
    with ExitStack() as mem:
        QK = mem.enter_context(tensor(nc, "sb_qk", [P, 2 * DT, NT]))
        V = mem.enter_context(tensor(nc, "sb_v", [P, TT, D]))
        with ExitStack() as inner:
            H = inner.enter_context(tensor(nc, "h_sb", [P, DT, NT]))
            rms_norm(nc, g, ps, H, COL["g_mix"] + DT)
            for first, scale in ((0, HD ** -0.5), (DT, 1.0)):
                def keep(act, m, banks, first=first, scale=scale):
                    row = QK[:, ds(first + m, 1), :].rearrange("p a (n c) -> p (a n) c", n=3)
                    return act.activation(row, banks, ACT.Copy, scale=scale)

                project(nc, ps, wqkv[:, first * P:first * P + D], DT, DT, lambda k, n: H[:, k, n * N3:(n + 1) * N3], keep, "scalar")
            sb_values(nc, g, d, ps, H, V)
        sb_store_keys(nc, g, d, ps, QK)
        sb_attention(nc, g, d, ps, QK, V)
        project(nc, ps, d.w_out_sb[0], DT, DT, lambda k, n: QK[:, k, n * N3:(n + 1) * N3], add_to_residual(g), "vector")


def sb_values(nc, g, d, ps, H, V):
    with ExitStack() as mem:
        W = [mem.enter_context(tensor(nc, f"v_w{n}", [P, DT, 256])) for n in range(2)]
        v8 = mem.enter_context(tensor(nc, "sample_v_rows", [NS, D]))
        wv = weight_blocks(d.w_qkv_sb[0][:, 2 * D:3 * D], DT)
        with phase(nc, ("w_in", 2), "made", "taken_act", "taken_dve", "stored") as (s, block):
            NG = 4 * (TT + 1)
            last_tile = TT

            @block.sync
            def _(sp):
                for q in range(4):
                    if q >= 2:
                        sp.wait_ge(s.made, (q - 1) * (TT + 1))
                    sp.dma_start(W[q % 2][:, :, :], wv[:, :, q * 256:(q + 1) * 256]).then_inc(s.w_in[q % 2], 16)
                sp.wait_ge(s.taken_act, NG // 2)
                sp.wait_ge(s.taken_dve, NG // 2)
                sp.dma_start(d.sb_v_p[0, 0].rearrange("(t p) h c -> p t (h c)", p=P), V[:, :, :]).then_inc(s.stored, 16)
                sp.dma_start(d.sb_v_s[0, :, 0].rearrange("b h c -> b (h c)"), v8[:, :]).then_inc(s.stored, 16)
                sp.wait_ge(s.stored, 32)

            @block.tensor
            def _(pe):
                for n in range(NG):
                    q, t = divmod(n, TT + 1)
                    w = P if t < last_tile else NS
                    if t == 0:
                        pe.wait_ge(s.w_in[q % 2], 16 * (q // 2 + 1))
                    if n >= 8:
                        pe.wait_ge(s.taken_dve if n % 2 else s.taken_act, (n - 8) // 2 + 1)
                    for k in range(DT):
                        last = pe.matmul(ps[0:w, n % 8, 0:256], H[:, k, t * P:t * P + w], W[q % 2][:, k, :],
                                         start=k == 0, stop=k == DT - 1)
                    last.then_inc(s.made, 1)

            def place(n):
                q, t = divmod(n, TT + 1)
                cols = slice(q * 256, (q + 1) * 256)
                return (V[:, t, cols], ps[:, n % 8, 0:256]) if t < last_tile else (v8[:, cols], ps[0:NS, n % 8, 0:256])

            @block.scalar
            def _(act):
                for n in range(0, NG, 2):
                    act.wait_ge(s.made, n + 1)
                    act.activation(*place(n), ACT.Copy).then_inc(s.taken_act, 1)

            @block.vector
            def _(dve):
                for n in range(1, NG, 2):
                    dve.wait_ge(s.made, n + 1)
                    dve.tensor_copy(*place(n)).then_inc(s.taken_dve, 1)


def sb_store_keys(nc, g, d, ps, QK):
    with ExitStack() as mem:
        rows = mem.enter_context(tensor(nc, "k_rows", [P, TT + 1, D]))
        turn_rows(nc, g, ps, lambda k: QK[:, DT + k, :], rows, d.sb_k_p[0, 0].rearrange("t h c -> t (h c)"),
                  d.sb_k_s[0, :, 0].rearrange("b h c -> b (h c)"))


def sb_attention(nc, g, d, ps, QK, V):
    with ExitStack() as mem:
        def sb(name, shape):
            return mem.enter_context(tensor(nc, name, shape))

        b = record(
            q=sb("pair_q", [P, T]), k=sb("pair_k", [P, T]), v=sb("pair_v", [P, TT, P]), bias=sb("pair_bias", [P, 2]),
            A=sb("logits", [P, 2, 2, 512]), B=sb("softplus", [P, 2, 2, 512]),
            kring=sb("k_ring", [P, KR, D]), vring=sb("v_ring", [P, VR, D]), prod=sb("products", [P, D]),
            Z=sb("cache_logits", [P, 512]), L=sb("cache_softplus", [P, 512]), tot=sb("page_totals", [P, 512]),
            att=sb("cache_weights", [P, 512]), kept=sb("page_kept", [P, 512]), qcol=sb("q_column", [P, DT]))
        with phase(nc, "made") as (s, block):
            @block.gpsimd
            def _(pool):
                link = linker(pool, s.made)
                link(pool.memset(b.kept[:, :], 1.0))
                link(pool.memset(b.kept[:, 0:512:PAGES], 0.0))
        sb_turn(nc, g, d, ps, QK, V, b, 0, prompt=False, values=False, keys=True)
        with nc.Fori(0, NS - 1) as i:
            sb_turn(nc, g, d, ps, QK, V, b, i, prompt=True, values=True, keys=True)
        sb_turn(nc, g, d, ps, QK, V, b, NS - 1, prompt=True, values=True, keys=False)


KR = 3
VR = 3
SB_STEPS = [(1, st) for st in range(7, -1, -1)] + [(0, st) for st in range(3, -1, -1)]


def sb_turn(nc, g, d, ps, QK, V, b, i, prompt, values, keys):
    steps = SB_STEPS if prompt else []
    two = (0, 1)
    b_next = i if not values else i + 1

    def span(n):
        tq, st = steps[n]
        return slice(max(0, P * st - 512 * tq), 512)

    def diagonal(n):
        tq, st = steps[n]
        return P * st >= 512 * tq

    def first(n):
        return n == 0 or steps[n][0] != steps[n - 1][0]

    def last_of(n):
        return n == len(steps) - 1 or steps[n][0] != steps[n + 1][0]

    with phase(nc, "copied", "z", "z_added", "capped", "exped", "logged", "soft", "summed", "arg", "weight", "rested",
               "out_done", "out_taken", ("k_in", KR), ("v_in", VR), "k_used", "v_used", "dve", "q_diag", "spread",
               "cz", "cexp", "clog", "csoft", "ctri", "ctot", "carg", "catt", "pv_taken", "act_steps",
               "pool_steps") as (s, block):

        @block.sync
        def _(sp):
            for p in range(PAGES):
                if keys:
                    page = sp.value_load(b_pages(g, b_next, p), min_val=0, max_val=d.cache_sb_k.shape[1] - 1)
                    if p >= KR:
                        sp.wait_ge(s.k_used, p - KR + 1)
                    sp.dma_start(b.kring[:, p % KR, :], d.cache_sb_k[0, ds(page, 1), :, :, :].rearrange("a p h c -> p (a h c)")).then_inc(s.k_in[p % KR], 16)
                if values:
                    page = sp.value_load(b_pages(g, i, p), min_val=0, max_val=d.cache_sb_v.shape[1] - 1)
                    if p >= VR:
                        sp.wait_ge(s.v_used, p - VR + 1)
                    sp.dma_start(b.vring[:, p % VR, :], d.cache_sb_v[0, ds(page, 1), :, :, :].rearrange("a p h c -> p (a h c)")).then_inc(s.v_in[p % VR], 16)

        @block.gpsimd
        def _(pool):
            if keys:
                pool.tensor_copy(b.qcol[:, :], QK[:, 0:DT, ds(b_next + T, 1)].rearrange("p k a -> p (k a)")).then_inc(s.pool_steps, 1)
                pool.wait_ge(s.pool_steps, 1)
                pool.tensor_tensor(b.prod[:, :].rearrange("p (k c) -> p k c", c=P), g.ident[:, :].unsqueeze(1).to_broadcast([P, DT, P]),
                                   b.qcol[:, :].unsqueeze(2).to_broadcast([P, DT, P]), ALU.mult).then_inc(s.q_diag, 1)
            if prompt:
                pool.tensor_copy(b.q[:, :], QK[:, ds(i, 1), 0:T].rearrange("p a c -> p (a c)")).then_inc(s.copied, 1)
                pool.tensor_copy(b.k[:, :], QK[:, ds(i + DT, 1), 0:T].rearrange("p a c -> p (a c)")).then_inc(s.copied, 1)
                pool.tensor_copy(b.v[:, :, :], V[:, :, ds(i * P, P)]).then_inc(s.copied, 1)
                pool.tensor_copy(b.bias[:, :], g.sbb[:, ds(i * 2, 2)]).then_inc(s.copied, 1)
            for n in range(len(steps)):
                c = span(n)
                for h in two:
                    A, B = b.A[:, n % 2, h, :], b.B[:, n % 2, h, :]
                    pool.wait_ge(s.z_added, 2 * n + h + 1)
                    if n >= 2:
                        pool.wait_ge(s.rested, 2 * (n - 2) + h + 1)
                    pool.tensor_scalar(B[:, c], A[:, c], 40.0, None, ALU.min).then_inc(s.capped, 1)

        @block.vector
        def _(dve):
            link = linker(dve, s.dve)
            page = [0]

            def score_page():
                p = page[0]
                page[0] += 1
                dve.wait_ge(s.k_in[p % KR], 16 * (p // KR + 1))
                link(dve.tensor_tensor(b.prod[:, :].rearrange("p (a c) -> p a c", a=2), b.kring[:, p % KR, :].rearrange("p (a c) -> p a c", a=2),
                                       ps[:, 6:8, :], ALU.mult))
                dve.sem_inc(s.k_used, 1)
                link(dve.tensor_reduce(b.Z[:, PAGES - 1 - p:512:PAGES], b.prod[:, :].rearrange("p (h c) -> p h c", c=HD), AX.X, ALU.add))

            if prompt:
                dve.wait_ge(s.copied, 4)
            if keys:
                dve.wait_ge(s.spread, 1)
            for n in range(len(steps) + 1):
                if n < len(steps):
                    c = span(n)
                    for h in two:
                        dve.wait_ge(s.z, 2 * n + h + 1)
                        if n >= 2:
                            dve.wait_ge(s.out_done, 2 * (n - 2) + h + 1)
                        dve.tensor_scalar(b.A[:, n % 2, h, c], ps[:, h, c], b.bias[:, h:h + 1], None, ALU.add).then_inc(s.z_added, 1)
                if keys and n < len(steps):
                    for _ in range(2 if n % 3 else 3):
                        score_page()
                if n < len(steps):
                    for h in two:
                        A, B = b.A[:, n % 2, h, :], b.B[:, n % 2, h, :]
                        dve.wait_ge(s.logged, 2 * n + h + 1)
                        if diagonal(n):
                            dg = slice(c.start, c.start + P)
                            link(dve.tensor_tensor(B[:, c], B[:, c], A[:, c], ALU.max))
                            dve.tensor_tensor(B[:, dg], B[:, dg], g.rest[:, :], ALU.mult).then_inc(s.soft, 1)
                        else:
                            dve.tensor_tensor(B[:, c], B[:, c], A[:, c], ALU.max).then_inc(s.soft, 1)
                    for h in two:
                        A = b.A[:, n % 2, h, :]
                        dve.wait_ge(s.summed, 2 * n + h + 1)
                        if diagonal(n):
                            dg = slice(c.start, c.start + P)
                            link(dve.tensor_tensor(A[:, c], A[:, c], ps[:, 2 + h, c], ALU.subtract))
                            dve.tensor_tensor(A[:, dg], A[:, dg], g.blocked[:, :], ALU.add).then_inc(s.arg, 1)
                        else:
                            dve.tensor_tensor(A[:, c], A[:, c], ps[:, 2 + h, c], ALU.subtract).then_inc(s.arg, 1)
            while keys and page[0] < PAGES:
                score_page()
            if values:
                dve.wait_ge(s.v_used, PAGES)
                for o in two:
                    dve.tensor_copy(QK[64 * o:64 * o + 64, 0:DT, ds(i + T, 1)], ps[64 * o:64 * o + 64, 5, o:2 * DT:2].unsqueeze(2)).then_inc(s.pv_taken, 1)
            if keys:
                Zh = b.Z[:, :].rearrange("p (h n) -> p h n", n=PAGES)
                link(dve.tensor_tensor(Zh, Zh, g.sbb[:, :].unsqueeze(2).to_broadcast([P, SBH, PAGES]), ALU.add))
                dve.tensor_scalar(b.L[:, :], b.Z[:, :], 40.0, None, ALU.min).then_inc(s.cz, 1)
                dve.wait_ge(s.clog, 1)
                dve.tensor_tensor(b.L[:, :], b.L[:, :], b.Z[:, :], ALU.max).then_inc(s.csoft, 1)
                dve.wait_ge(s.ctri, 1)
                link(dve.tensor_tensor(b.Z[:, :], b.Z[:, :], ps[:, 6, :], ALU.subtract))
                dve.wait_ge(s.ctot, 1)
                link(dve.tensor_tensor(b.Z[:, :], b.Z[:, :], b.tot[:, :], ALU.add))
                link(dve.tensor_tensor_scan(b.L[:, :], b.kept[:, :], b.tot[:, :], 0.0, ALU.mult, ALU.add))
                dve.tensor_tensor(b.Z[:, :], b.Z[:, :], b.L[:, :], ALU.subtract).then_inc(s.carg, 1)

        @block.scalar
        def _(act):
            for n in range(len(steps)):
                c = span(n)
                for h in two:
                    B = b.B[:, n % 2, h, :]
                    act.wait_ge(s.capped, 2 * n + h + 1)
                    act.activation(B[:, c], B[:, c], ACT.Exp).then_inc(s.exped, 1)
                for h in two:
                    B = b.B[:, n % 2, h, :]
                    act.wait_ge(s.exped, 2 * n + h + 1)
                    act.activation(B[:, c], B[:, c], ACT.Ln, bias=g.ones[:, 0:1]).then_inc(s.logged, 1)
                for h in two:
                    A = b.A[:, n % 2, h, :]
                    act.wait_ge(s.arg, 2 * n + h + 1)
                    act.activation(A[:, c], A[:, c], ACT.Exp).then_inc(s.weight, 1)
                if last_of(n):
                    act.wait_ge(s.out_done, 2 * n + 2)
                    tq = steps[n][0]
                    act.activation(QK[:, ds(i, 1), 512 * tq:512 * tq + 512].rearrange("p a c -> p (a c)"), ps[:, 4, :], ACT.Copy).then_inc(s.out_taken, 1)
            if keys:
                act.wait_ge(s.cz, 1)
                act.activation(b.L[:, :], b.L[:, :], ACT.Exp).then_inc(s.cexp, 1)
                act.wait_ge(s.cexp, 1)
                act.activation(b.L[:, :], b.L[:, :], ACT.Ln, bias=g.ones[:, 0:1]).then_inc(s.clog, 1)
                act.wait_ge(s.ctri, 2)
                act.activation(b.tot[:, :], ps[:, 7, :], ACT.Copy).then_inc(s.ctot, 1)
                act.wait_ge(s.carg, 1)
                if values:
                    act.wait_ge(s.v_used, PAGES)
                act.activation(b.att[:, :], b.Z[:, :], ACT.Exp).then_inc(s.catt, 1)

        @block.tensor
        def _(pe):
            page = [0]

            def value_page():
                p = page[0]
                page[0] += 1
                pe.wait_ge(s.v_in[p % VR], 16 * (p // VR + 1))
                for k in range(DT):
                    at = b.att[:, :].rearrange("p (h n) -> p n h", n=PAGES)[:, PAGES - 1 - p, 2 * k:2 * k + 2]
                    last = pe.matmul(ps[:, 5, 2 * k:2 * k + 2], b.vring[:, p % VR, k * P:(k + 1) * P], at,
                                     start=p == 0 and k == 0, stop=p == PAGES - 1, skip_group_check=True)
                last.then_inc(s.v_used, 1)
                return last

            def logits(n, h):
                tq, st = steps[n]
                c = span(n)
                r = slice(64 * h, 64 * h + 64)
                if n:
                    pe.wait_ge(s.z_added, 2 * (n - 1) + h + 1)
                pe.matmul(ps[:, h, c], b.k[r, st * P:(st + 1) * P], b.q[r, 512 * tq + c.start:512 * tq + 512],
                          start=True, stop=True).then_inc(s.z, 1)

            if keys:
                pe.wait_ge(s.q_diag, 1)
                for n in two:
                    last = pe.matmul(ps[:, 6 + n, :], g.ones[:, :], b.prod[:, n * 512:(n + 1) * 512], start=True, stop=True)
                last.then_inc(s.spread, 1)
            if prompt:
                pe.wait_ge(s.copied, 3)
                for h in two:
                    logits(0, h)
            for n in range(len(steps)):
                tq, st = steps[n]
                c = span(n)
                for h in two:
                    pe.wait_ge(s.soft, 2 * n + h + 1)
                    pe.matmul(ps[:, 2 + h, c], g.tail[:, :], b.B[:, n % 2, h, c], start=first(n), stop=last_of(n),
                              skip_group_check=True).then_inc(s.summed, 1)
                if n + 1 < len(steps):
                    for h in two:
                        logits(n + 1, h)
                if values:
                    for _ in range(2 if n % 3 else 3):
                        value_page()
                for h in two:
                    pe.wait_ge(s.arg, 2 * n + h + 1)
                    pe.matmul(ps[:, 2 + h, c], g.rest[:, :], b.B[:, n % 2, h, c], start=False, stop=last_of(n),
                              skip_group_check=True).then_inc(s.rested, 1)
                if first(n) and n:
                    pe.wait_ge(s.out_taken, 1)
                for h in two:
                    pe.wait_ge(s.weight, 2 * n + h + 1)
                    pe.matmul(ps[64 * h:64 * h + 64, 4, c], b.v[:, st, 64 * h:64 * h + 64], b.A[:, n % 2, h, c],
                              start=first(n), stop=last_of(n), skip_group_check=True).then_inc(s.out_done, 1)
            if values:
                while page[0] < PAGES:
                    value_page()
            if keys:
                pe.wait_ge(s.csoft, 1)
                for n, m in enumerate((g.tail, g.ones)):
                    pe.matmul(ps[:, 6 + n, :], m[:, :], b.L[:, :], start=True, stop=True).then_inc(s.ctri, 1)


def b_pages(g, b, p):
    at = b * PAGES + p
    return g.pages[0:1, at:at + 1] if isinstance(at, int) else g.pages[0:1, ds(at, 1)]


def store_outputs(nc, g, d, ps):
    with ExitStack() as mem:
        rows = mem.enter_context(tensor(nc, "y_rows", [P, TT + 1, D]))
        turn_rows(nc, g, ps, lambda k: g.X[:, k, :], rows, d.y_prompt[0], d.y_sample[:, 0, :])


def turn_rows(nc, g, ps, tile, out, to_prompt, to_samples):
    with phase(nc, "turned", "taken_act", "taken_dve", "stored") as (s, block):
        NG = 2 * (TT + 1)

        @block.tensor
        def _(pe):
            for n in range(NG):
                t, half = n // 2, n % 2
                w = P if t < TT else NS
                if n >= 8:
                    pe.wait_ge(s.taken_dve if half else s.taken_act, (n - 8) // 2 + 1)
                for k in range(4):
                    last = pe.transpose(ps[0:w, n % 8, k * P:(k + 1) * P], tile(4 * half + k)[:, t * P:t * P + w],
                                        g.ident[:, :])
                last.then_inc(s.turned, 1)

        @block.scalar
        def _(act):
            for n in range(0, NG, 2):
                w = P if n // 2 < TT else NS
                act.wait_ge(s.turned, n + 1)
                act.activation(out[0:w, n // 2, 0:512], ps[0:w, n % 8, :], ACT.Copy).then_inc(s.taken_act, 1)

        @block.vector
        def _(dve):
            for n in range(1, NG, 2):
                w = P if n // 2 < TT else NS
                dve.wait_ge(s.turned, n + 1)
                dve.tensor_copy(out[0:w, n // 2, 512:1024], ps[0:w, n % 8, :]).then_inc(s.taken_dve, 1)

        @block.sync
        def _(sp):
            for t in range(TT + 1):
                sp.wait_ge(s.taken_act, t + 1)
                sp.wait_ge(s.taken_dve, t + 1)
                if t < TT:
                    sp.dma_start(to_prompt[t * P:(t + 1) * P, :], out[:, t, :]).then_inc(s.stored, 16)
                else:
                    sp.dma_start(to_samples, out[0:NS, t, :]).then_inc(s.stored, 16)
            sp.wait_ge(s.stored, 16 * (TT + 1))


def program(nc, d):
    ctx = ExitStack()
    probe = ctx.enter_context(nc.semaphore("first"))
    FIRST_SEM[0] = probe.num
    with ctx:
        def sb(name, shape, dt=F32):
            return ctx.enter_context(tensor(nc, name, shape, dt))

        g = record(
            X=sb("residual", [P, DT, NT]), ones=sb("ones", [P, P]), ident=sb("ident", [P, P]),
            blockones=sb("blockones", [P, P]), ident2=sb("ident2", [P, 64]), tail=sb("tail", [P, P]),
            rest=sb("rest", [P, P]), blocked=sb("blocked", [P, P]), epsc=sb("eps", [P, 2]), par=sb("params", [P, 2 * P]),
            shift0=sb("shift0", [P, RWC_T, NS]), conv0=sb("conv0", [P, LRU_T, 24]), h0=sb("h0", [P, LRU_T, NS]),
            kn=sb("kn", [P, 2, P]), sbb=sb("sb_bias", [P, SBH]), pages=sb("pages", [1, NS * PAGES], I32))
        ps = ctx.enter_context(nc.psum_tensor("ps", [P, 8, 512], F32))
        constants(nc, g)
        load_inputs(nc, g, d, ps)
        layer0_mixer(nc, g, d, ps)
        memory_attention(nc, g, d, ps, 0)
        ffn(nc, g, d, ps, 0)
        stick_breaking(nc, g, d, ps)
        memory_attention(nc, g, d, ps, 1)
        ffn(nc, g, d, ps, 1)
        store_outputs(nc, g, d, ps)


OUTS = [("y_prompt", (1, T, D)), ("y_sample", (NS, 1, D)), ("wkv_p", (1, 1, 8, HD, HD)), ("wkv_s", (1, NS, 8, HD, HD)),
        ("shift_p", (1, 1, RW_COLS)), ("shift_s", (1, NS, RW_COLS)), ("lru_h_p", (1, 1, RW)), ("lru_h_s", (1, NS, RW)),
        ("lru_conv_p", (1, 1, 3, RW)), ("lru_conv_s", (1, NS, 3, RW)), ("sb_k_p", (1, 1, T, SBH, HD)),
        ("sb_k_s", (1, NS, 1, SBH, HD)), ("sb_v_p", (1, 1, T, SBH, HD)), ("sb_v_s", (1, NS, 1, SBH, HD)),
        ("mem_k_p", (2, 1, MEM, MH, P)), ("mem_v_p", (2, 1, MEM, MH, P))]


def kernel(**inputs):
    import numpy as _np
    import concourse.bacc as _bacc
    from concourse.bass_utils import run_bass_kernel_spmd as _run

    nc = _bacc.Bacc("TRN2", target_bir_lowering=False, num_devices=1)
    arrays, aps = {}, {}
    for name, value in inputs.items():
        a = _np.ascontiguousarray(value)
        arrays[f"in_{name}"] = a
        aps[name] = nc.dram_tensor(f"in_{name}", a.shape, mybir.dt.from_np(a.dtype), kind="ExternalInput").ap()
    for name, shape in OUTS:
        aps[name] = nc.dram_tensor(f"out_{name}", shape, F32, kind="ExternalOutput").ap()
    program(nc, record(rows=aps, **aps))
    r = _run(nc, [arrays], core_ids=[0])
    return tuple(r.results[0][f"out_{name}"] for name, _ in OUTS)
```

```python
from contextlib import ExitStack, contextmanager
from collections import namedtuple

import numpy as np
import concourse.bass as bass
from concourse import mybir

F32 = mybir.dt.float32
F32R = mybir.dt.float32r
I32 = mybir.dt.int32
ALU = mybir.AluOpType
ACT = mybir.ActivationFunctionType
AX = mybir.AxisListType
ds = bass.DynSlice

P = 128
D = 1024
DT = D // P
T = 1024
TT = T // P
NS = 8
NT = T + NS
N3 = NT // 3
PAD = 4
RW = 512
RWT = RW // P
RW_COLS = 1792
RWC_T = RW_COLS // P
LRU_T = 4
AB_T = 22
AB_COLS = AB_T * P
FF = 2816
FF_T = FF // P
FF_PARTS = [(0, 8), (8, 8), (16, 6)]
HD = 64
C = 64
NC = T // C
MEM = 256
MH = 4
SBH = 16
PAGES = 32
EPS = 1e-6
LN_EPS = HD * 1e-5
DECAY = -float(np.exp(-0.5))

ROWS_A = [("mu_shift", 14), ("rw_w0", 4), ("rw_a0", 4), ("rw_kk", 4), ("rw_ka", 4), ("rw_rk", 4),
          ("rw_lnx_w", 4), ("rw_lnx_b", 4), ("lru_conv_w", 16), ("lru_conv_b", 4), ("lru_ba", 4),
          ("lru_bx", 4), ("lru_lambda", 4)]
ROWS_B = [("g_mix", 16), ("g_mem", 16), ("g_memkv", 16), ("g_ffn", 16), ("qn_mem", 2)]
COL = {}
for _base, _rows in ((0, ROWS_A), (P, ROWS_B)):
    for _name, _n in _rows:
        COL[_name] = _base
        _base += _n
NA = sum(n for _, n in ROWS_A)
NB = sum(n for _, n in ROWS_B)
FIRST_SEM = [0]


def record(**fields):
    return namedtuple("Record", list(fields))(**fields)


TENSORS = [0]


def tensor(nc, name, shape, dt=F32):
    TENSORS[0] += 1
    return nc.sbuf_tensor(f"{name}_{TENSORS[0]}", shape, dt)


@contextmanager
def phase(nc, *names):
    with ExitStack() as stack:
        sems = {}
        for name in names:
            if isinstance(name, tuple):
                sems[name[0]] = [stack.enter_context(nc.semaphore(f"{name[0]}{i}")) for i in range(name[1])]
            else:
                sems[name] = stack.enter_context(nc.semaphore(name))
        with nc.Block() as block:
            yield record(**sems), block
    nc.all_engine_barrier(sems_to_clear=range(FIRST_SEM[0], 256))


def linker(eng, sem):
    count = [0]

    def link(ins):
        count[0] += 1
        ins.then_inc(sem, 1)
        eng.wait_ge(sem, count[0])

    return link


def bank3(ps, first):
    return ps[:, first:first + 3, 0:N3]


def cols3(ap):
    return ap.rearrange("p (n c) -> p n c", n=3)


def constants(nc, g):
    with phase(nc, "filled", "cut", "made") as (s, block):
        @block.gpsimd
        def _(pool):
            link = linker(pool, s.made)
            link(pool.memset(g.ones[:, :], 1.0))
            link(pool.memset(g.ident[:, :], 0.0))
            link(pool.affine_select(out=g.ident[:, :], in_=g.ident[:, :], compare_op=ALU.not_equal, fill=1.0,
                                    base=0, pattern=[[-1, P]], channel_multiplier=1))
            link(pool.memset(g.blockones[:, :], 0.0))
            link(pool.memset(g.blockones[0:64, 0:64], 1.0))
            link(pool.memset(g.blockones[64:128, 64:128], 1.0))
            link(pool.tensor_tensor(g.ident2[:, :], g.ident[:, 0:64], g.ident[:, 64:128], ALU.add))
            link(pool.affine_select(out=g.tail[:, :], in_=g.ones[:, :], compare_op=ALU.is_ge, fill=0.0,
                                    base=0, pattern=[[-1, P]], channel_multiplier=1))
            link(pool.tensor_tensor(g.rest[:, :], g.ones[:, :], g.tail[:, :], ALU.subtract))
            link(pool.tensor_scalar(g.blocked[:, :], g.tail[:, :], -1e30, None, ALU.mult))
            link(pool.memset(g.epsc[:, 0:1], EPS))
            link(pool.memset(g.epsc[:, 1:2], LN_EPS))


def load_inputs(nc, g, d, ps):
    NG = 2 * (TT + 1)
    with ExitStack() as mem:
        tok = mem.enter_context(tensor(nc, "tokens", [P, TT + 1, D], F32))
        rows = mem.enter_context(tensor(nc, "param_rows", [P, 2, P], F32))
        st = mem.enter_context(tensor(nc, "state_rows", [24, 3, RW_COLS], F32))
        with phase(nc, ("tok_in", TT + 1), "rows_in", "state_in", "turned", "taken_act", "taken_dve", "copied",
                   "stored") as (s, block):
            @block.sync
            def _(sp):
                for t in range(TT):
                    sp.dma_start(tok[:, t, :], d.x_prompt[0, t * P:(t + 1) * P, :]).then_inc(s.tok_in[t], 16)
                sp.dma_start(tok[0:NS, TT, :], d.x_sample[:, 0, :]).then_inc(s.tok_in[TT], 16)
                sp.dma_start(st[0:NS, 0, :], d.state_rwkv_shift[0]).then_inc(s.state_in, 16)
                sp.dma_start(st[0:24, 1, 0:RW], d.state_lru_conv[0].rearrange("b j c -> (b j) c")).then_inc(s.state_in, 16)
                sp.dma_start(st[0:NS, 2, 0:RW], d.state_lru_h[0]).then_inc(s.state_in, 16)
                sp.dma_start(d.lru_conv_s[0, :, 0:2, :], d.state_lru_conv[0, :, 1:3, :]).then_inc(s.stored, 16)
                sp.dma_start(g.kn[:, :, :], d.kn_mem.unsqueeze(0).to_broadcast([P, 2, P])).then_inc(s.stored, 16)
                sp.dma_start(g.sbb[:, :], d.sb_bias.to_broadcast([P, SBH])).then_inc(s.stored, 16)
                sp.dma_start(g.pages[:, :], d.page_table.rearrange("b n -> (b n)").unsqueeze(0)).then_inc(s.stored, 16)
                sp.wait_ge(s.stored, 64)

            @block.scalar
            def _(act):
                at = {}
                for group, names in enumerate((ROWS_A, ROWS_B)):
                    r = 0
                    for name, n in names:
                        src = d.rows[name].flatten().rearrange("(r c) -> r c", c=P)
                        act.dma_start(rows[r:r + n, group, :], src).then_inc(s.rows_in, 16)
                        r += n
                for n in range(0, NG, 2):
                    t = n // 2
                    w = P if t < TT else NS
                    act.wait_ge(s.turned, n + 1)
                    act.activation(g.X[:, 0:4, t * P:t * P + w],
                                   ps[:, n % 8, :].rearrange("p (k c) -> p k c", k=4)[:, :, 0:w],
                                   ACT.Copy).then_inc(s.taken_act, 1)

            @block.vector
            def _(dve):
                for n in range(1, NG, 2):
                    t = n // 2
                    w = P if t < TT else NS
                    dve.wait_ge(s.turned, n + 1)
                    dve.tensor_copy(g.X[:, 4:8, t * P:t * P + w],
                                    ps[:, n % 8, :].rearrange("p (k c) -> p k c", k=4)[:, :, 0:w]).then_inc(s.taken_dve, 1)
                dve.wait_ge(s.turned, NG + 1)
                dve.tensor_copy(g.par[:, 0:NA], ps[:, NG % 8, 0:NA]).then_inc(s.copied, 1)
                dve.tensor_copy(g.par[:, P:P + NB], ps[:, NG % 8, P:P + NB]).then_inc(s.copied, 1)
                dve.wait_ge(s.turned, NG + 2)
                dve.tensor_copy(g.shift0[:, :, :], ps[:, (NG + 1) % 8, 0:RWC_T * NS]
                                .rearrange("p (k b) -> p k b", b=NS)).then_inc(s.copied, 1)
                dve.tensor_copy(g.conv0[:, :, :], ps[:, (NG + 1) % 8, 128:128 + 96]
                                .rearrange("p (k b) -> p k b", b=24)).then_inc(s.copied, 1)
                dve.tensor_copy(g.h0[:, :, :], ps[:, (NG + 1) % 8, 256:256 + 32]
                                .rearrange("p (k b) -> p k b", b=NS)).then_inc(s.copied, 1)

            @block.tensor
            def _(pe):
                for n in range(NG):
                    t, half = n // 2, n % 2
                    w = P if t < TT else NS
                    if half == 0:
                        pe.wait_ge(s.tok_in[t], 16)
                    if n >= 8:
                        pe.wait_ge(s.taken_dve if half else s.taken_act, (n - 8) // 2 + 1)
                    for k in range(4):
                        kk = 4 * half + k
                        last = pe.transpose(ps[:, n % 8, k * P:k * P + w], tok[0:w, t, kk * P:(kk + 1) * P],
                                            g.ident[0:w, 0:w])
                    last.then_inc(s.turned, 1)
                pe.wait_ge(s.rows_in, 16 * (len(ROWS_A) + len(ROWS_B)))
                pe.wait_ge(s.taken_act, (NG - 8) // 2 + 1)
                pe.transpose(ps[:, NG % 8, 0:NA], rows[0:NA, 0, :], g.ident[0:NA, 0:NA])
                pe.transpose(ps[:, NG % 8, P:P + NB], rows[0:NB, 1, :], g.ident[0:NB, 0:NB]).then_inc(s.turned, 1)
                pe.wait_ge(s.state_in, 48)
                pe.wait_ge(s.taken_dve, (NG - 8) // 2 + 1)
                b = (NG + 1) % 8
                for k in range(RWC_T):
                    pe.transpose(ps[:, b, k * NS:(k + 1) * NS], st[0:NS, 0, k * P:(k + 1) * P], g.ident[0:NS, 0:NS])
                for k in range(LRU_T):
                    pe.transpose(ps[:, b, 128 + k * 24:152 + k * 24], st[0:24, 1, k * P:(k + 1) * P], g.ident[0:24, 0:24])
                for k in range(LRU_T):
                    last = pe.transpose(ps[:, b, 256 + k * NS:264 + k * NS], st[0:NS, 2, k * P:(k + 1) * P],
                                        g.ident[0:NS, 0:NS])
                last.then_inc(s.turned, 1)


def rms_norm(nc, g, ps, H, gains, spill=None):
    with ExitStack() as mem:
        sq = mem.enter_context(tensor(nc, "squares", [P, 2, NT]))
        rms = mem.enter_context(tensor(nc, "rms", [P, NT]))
        whole = [mem.enter_context(tensor(nc, f"normed{n}", [P, NT])) for n in range(2)]
        with phase(nc, "squared", "summed", "rooted", "inverted", "scaled", "high", "low", "stored") as (s, block):
            @block.scalar
            def _(act):
                for k in range(DT):
                    if k >= 2:
                        act.wait_ge(s.summed, k - 1)
                    act.activation(sq[:, k % 2, :], g.X[:, k, :], ACT.Square).then_inc(s.squared, 1)
                act.wait_ge(s.summed, DT)
                act.activation(cols3(rms[:, :]), bank3(ps, 0), ACT.Sqrt, scale=1.0 / D,
                               bias=g.epsc[:, 0:1]).then_inc(s.rooted, 1)
                for k in range(DT):
                    act.wait_ge(s.scaled, k + 1)
                    act.activation(H.hi[:, k, :], whole[k % 2][:, :], ACT.Copy).then_inc(s.high, 1)

            @block.tensor
            def _(pe):
                for k in range(DT):
                    pe.wait_ge(s.squared, k + 1)
                    for n in range(3):
                        last = pe.matmul(ps[:, n, 0:N3], g.ones[:, :], sq[:, k % 2, n * N3:(n + 1) * N3],
                                         start=k == 0, stop=k == DT - 1)
                    last.then_inc(s.summed, 1)

            @block.sync
            def _(sp):
                if spill is not None:
                    sp.dma_start(spill, g.X[:, :, :]).then_inc(s.stored, 16)
                    sp.wait_ge(s.stored, 16)

            @block.vector
            def _(dve):
                dve.wait_ge(s.rooted, 1)
                dve.reciprocal(rms[:, :], rms[:, :]).then_inc(s.inverted, 1)
                dve.wait_ge(s.inverted, 1)
                for k in range(DT + 1):
                    if k < DT:
                        if k >= 2:
                            dve.wait_ge(s.low, k - 1)
                        dve.scalar_tensor_tensor(whole[k % 2][:, :], g.X[:, k, :], g.par[:, gains + k:gains + k + 1], rms[:, :],
                                                 ALU.mult, ALU.mult).then_inc(s.scaled, 1)
                    if k:
                        dve.wait_ge(s.high, k)
                        dve.tensor_tensor(H.lo[:, k - 1, :], whole[(k - 1) % 2][:, :], H.hi[:, k - 1, :].bitcast(F32),
                                          ALU.subtract).then_inc(s.low, 1)


def parts(nc, stack, name, shape):
    return record(hi=stack.enter_context(tensor(nc, name + "_hi", shape, F32R)),
                  lo=stack.enter_context(tensor(nc, name + "_lo", shape, F32R)))


def weight_blocks(w, kt):
    return w.rearrange("(k p) m -> p k m", p=P, k=kt)


def project(nc, ps, source, kt, pairs, x, takes, split=None, reload=None):
    with ExitStack() as mem:
        raw = [mem.enter_context(tensor(nc, f"w_raw{h}", [P, kt, P])) for h in range(2)]
        W = [parts(nc, mem, f"w{h}", [P, kt, P]) for h in range(2)]
        with phase(nc, ("w_in", 2), "w_high", "w_low", "product", ("free_banks", 2), "x_high", "x_low", "x_back",
                   "hid_raw", "hid_high", "hid_low", "side_used") as (s, block):
            @block.sync
            def _(sp):
                for h in range(2):
                    sp.dma_start(raw[h][:, :, :], source(0, h)).then_inc(s.w_in[h], 16)
                if reload is not None:
                    sp.dma_start(takes.residual, reload).then_inc(s.x_back, 16)
                with sp.Fori(1, pairs) as i:
                    for h in range(2):
                        sp.wait_ge(s.w_low, 2 * (i - 1) + h + 1)
                        sp.dma_start(raw[h][:, :, :], source(i, h)).then_inc(s.w_in[h], 16)

            @block.tensor
            def _(pe):
                with pe.Fori(0, pairs) as i:
                    for h in range(2):
                        pe.wait_ge(s.w_low, 2 * i + h + 1)
                        pe.wait_ge(s.free_banks[h], i + 1)
                        for k in range(kt):
                            if split and h == 0:
                                pe.wait_ge(s.x_low, k + 1)
                            for m, (wp, xp) in enumerate(((W[h].hi, x.hi), (W[h].hi, x.lo), (W[h].lo, x.hi))):
                                for n in range(3):
                                    last = pe.matmul(ps[:, 3 * h + n, 0:N3], wp[:, k, :], xp[:, k, n * N3:(n + 1) * N3],
                                                     start=k == 0 and m == 0, stop=k == kt - 1 and m == 2)
                        last.then_inc(s.product, 1)

            @block.scalar
            def _(act):
                def high(i, h):
                    act.wait_ge(s.w_in[h], 16 * (i + 1))
                    act.activation(W[h].hi[:, :, :], raw[h][:, :, :], ACT.Copy).then_inc(s.w_high, 1)

                for h in range(2):
                    high(0, h)
                for k, tile in enumerate(split or []):
                    act.activation(x.hi[:, k, :], tile, ACT.Copy).then_inc(s.x_high, 1)

                def stores(i, h):
                    act.wait_ge(s.product, 2 * i + h + 1)
                    takes.scalar(act, s, i, h, bank3(ps, 3 * h))

                with act.Fori(0, pairs - 1) as i:
                    for h in range(2):
                        stores(i, h)
                        high(i + 1, h)
                for h in range(2):
                    stores(pairs - 1, h)

            @block.gpsimd
            def _(pool):
                with pool.Fori(0, pairs) as i:
                    for h in range(2):
                        pool.wait_ge(s.w_high, 2 * i + h + 1)
                        pool.tensor_tensor(W[h].lo[:, :, :], raw[h][:, :, :], W[h].hi[:, :, :].bitcast(F32), ALU.subtract).then_inc(s.w_low, 1)

            @block.vector
            def _(dve):
                for h in range(2):
                    dve.sem_inc(s.free_banks[h], 1)
                for k, tile in enumerate(split or []):
                    dve.wait_ge(s.x_high, k + 1)
                    dve.tensor_tensor(x.lo[:, k, :], tile, x.hi[:, k, :].bitcast(F32), ALU.subtract).then_inc(s.x_low, 1)
                takes.vector_start(dve, s)
                if reload is not None:
                    dve.wait_ge(s.x_back, 16)
                with dve.Fori(0, pairs) as i:
                    for h in range(2):
                        takes.vector(dve, s, i, h, bank3(ps, 3 * h))


def nothing(*_):
    return None


def tiles_of(w, kt):
    wv = weight_blocks(w, kt)
    return lambda i, h: wv[:, :, (2 * i + h) * P:(2 * i + h + 1) * P] if isinstance(i, int) else wv[:, :, ds((2 * i + h) * P, P)]


def at(m):
    return slice(m, m + 1) if isinstance(m, int) else ds(m, 1)


def kept_in(dst, scale=1.0):
    def take(act, s, i, h, banks):
        act.activation(dst(at(2 * i + h)).rearrange("p a (n c) -> p (a n) c", n=3), banks, ACT.Copy, scale=scale).then_inc(s.free_banks[h], 1)
    return record(scalar=take, vector=nothing, vector_start=nothing)


def add_to_residual(g):
    def take(dve, s, i, h, banks):
        dve.wait_ge(s.product, 2 * i + h + 1)
        x = g.X[:, ds(2 * i + h, 1), :].rearrange("p a (n c) -> p (a n) c", n=3)
        dve.tensor_tensor(x, banks, x, ALU.add).then_inc(s.free_banks[h], 1)
    return record(scalar=nothing, vector=take, vector_start=nothing, residual=g.X[:, :, :])


def ffn(nc, g, d, ps, layer):
    wg, wu = (weight_blocks(w[layer], DT) for w in (d.w_ffn_gate, d.w_ffn_up))
    with ExitStack() as mem:
        H = parts(nc, mem, "h_ffn", [P, DT, NT])
        rms_norm(nc, g, ps, H, COL["g_ffn"] + layer * DT)
        for first, count in FF_PARTS:
            with ExitStack() as inner:
                hid = parts(nc, inner, "hidden", [P, count, NT])
                with ExitStack() as temps:
                    gate = temps.enter_context(tensor(nc, "silu", [P, NT]))
                    whole = temps.enter_context(tensor(nc, "hidden_whole", [P, NT]))

                    def source(i, h):
                        w = (wg, wu)[h]
                        return w[:, :, (first + i) * P:(first + i + 1) * P] if isinstance(i, int) else w[:, :, ds((first + i) * P, P)]

                    def scalar(act, s, i, h, banks):
                        if h == 0:
                            act.wait_ge(s.side_used, i + 1)
                            act.activation(cols3(gate[:, :]), banks, ACT.Silu).then_inc(s.free_banks[0], 1)
                        else:
                            act.wait_ge(s.hid_raw, i + 1)
                            act.activation(hid.hi[:, at(i), :].rearrange("p a c -> p (a c)"), whole[:, :], ACT.Copy).then_inc(s.hid_high, 1)

                    def vector(dve, s, i, h, banks):
                        if h:
                            dve.wait_ge(s.product, 2 * i + 2)
                            dve.wait_ge(s.free_banks[0], i + 2)
                            dve.wait_ge(s.hid_low, i + 1)
                            dve.tensor_tensor(cols3(whole[:, :]), banks, cols3(gate[:, :]), ALU.mult).then_inc(s.hid_raw, 1)
                            dve.wait_ge(s.hid_raw, i + 1)
                            dve.sem_inc(s.free_banks[1], 1)
                            dve.sem_inc(s.side_used, 1)
                            dve.wait_ge(s.hid_high, i + 1)
                            dve.tensor_tensor(hid.lo[:, at(i), :].rearrange("p a c -> p (a c)"), whole[:, :],
                                              hid.hi[:, at(i), :].rearrange("p a c -> p (a c)").bitcast(F32), ALU.subtract).then_inc(s.hid_low, 1)

                    def start(dve, s):
                        dve.sem_inc(s.side_used, 1)
                        dve.sem_inc(s.hid_low, 1)

                    project(nc, ps, source, DT, count, H, record(scalar=scalar, vector=vector, vector_start=start))
                project(nc, ps, tiles_of(d.w_ffn_down[layer][first * P:(first + count) * P, :], count), count, DT // 2, hid,
                        add_to_residual(g))


def layer0_mixer(nc, g, d, ps):
    with ExitStack() as mem:
        lru = mem.enter_context(tensor(nc, "lru_gate", [P, LRU_T, NT]))
        big = mem.enter_context(tensor(nc, "rwkv_rows", [P, RWC_T, PAD + NT]))
        x_flat = g.X[:, :, :].rearrange("p k c -> p (k c)")
        px = x_flat[:, 0:LRU_T * (PAD + NT)].rearrange("p (k c) -> p k c", k=LRU_T)
        with ExitStack() as inner:
            H = parts(nc, inner, "h_mix", [P, DT, NT])
            rms_norm(nc, g, ps, H, COL["g_mix"], spill=d.spill)
            w = d.w_in_ab[0]
            project(nc, ps, tiles_of(w[:, 0:RW_COLS], DT), DT, RWC_T // 2, H, kept_in(lambda m: big[:, m, PAD:PAD + NT]))
            project(nc, ps, tiles_of(w[:, RW_COLS + RW:AB_COLS], DT), DT, LRU_T // 2, H, kept_in(lambda m: lru[:, m, :]))
            project(nc, ps, tiles_of(w[:, RW_COLS:RW_COLS + RW], DT), DT, LRU_T // 2, H, kept_in(lambda m: px[:, m, PAD:PAD + NT]))
        store_shift_rows(nc, g, d, ps, big, px)
        rg_lru(nc, g, d, ps, px, lru)
        with ExitStack() as inner:
            w2a = inner.enter_context(tensor(nc, "w2_a2", [P, RW]))
            g2 = inner.enter_context(tensor(nc, "g2", [P, RW]))
            kept = inner.enter_context(tensor(nc, "chunk_starts", [P, NT]))
            masks = inner.enter_context(tensor(nc, "masks", [P, 10, C]))
            token_shift(nc, g, d, ps, big, w2a, g2, kept, masks)
            with nc.Fori(0, RWT) as pair:
                rwkv_pair(nc, g, d, ps, big, w2a, g2, kept, masks, pair)
        with ExitStack() as inner:
            mix = parts(nc, inner, "mix", [P, DT, NT])
            tiles = [big[:, k, PAD:PAD + NT] for k in range(RWT)] + [lru[:, k, :] for k in range(LRU_T)]
            project(nc, ps, tiles_of(d.w_out_ab[0], DT), DT, DT // 2, mix, add_to_residual(g), split=tiles, reload=d.spill)


def store_shift_rows(nc, g, d, ps, big, px):
    with ExitStack() as mem:
        rows = mem.enter_context(tensor(nc, "shift_rows", [16, 5, 512], F32))
        with phase(nc, "turned", "copied", "stored") as (s, block):
            @block.tensor
            def _(pe):
                last_row = PAD + T - 1
                for k in range(RWC_T):
                    last = pe.transpose(ps[0:9, k // 4, (k % 4) * P:(k % 4 + 1) * P], big[:, k, last_row:last_row + 9],
                                        g.ident[:, :])
                for k in range(LRU_T):
                    last = pe.transpose(ps[0:11, 4, k * P:(k + 1) * P], px[:, k, last_row - 2:last_row + 9],
                                        g.ident[:, :])
                last.then_inc(s.turned, 1)

            @block.scalar
            def _(act):
                act.wait_ge(s.turned, 1)
                act.activation(rows[0:9, 0:3, :], ps[0:9, 0:3, :], ACT.Copy).then_inc(s.copied, 1)
                act.activation(rows[0:9, 3, 0:256], ps[0:9, 3, 0:256], ACT.Copy).then_inc(s.copied, 1)
                act.activation(rows[0:11, 4, :], ps[0:11, 4, :], ACT.Copy).then_inc(s.copied, 1)

            @block.sync
            def _(sp):
                flat = rows[:, 0:4, :].rearrange("p a c -> p (a c)")
                sp.wait_ge(s.copied, 3)
                sp.dma_start(d.shift_p[0], flat[0:1, 0:RW_COLS]).then_inc(s.stored, 16)
                sp.dma_start(d.shift_s[0], flat[1:9, 0:RW_COLS]).then_inc(s.stored, 16)
                sp.dma_start(d.lru_conv_p[0, 0], rows[0:3, 4, :]).then_inc(s.stored, 16)
                sp.dma_start(d.lru_conv_s[0, :, 2, :], rows[3:11, 4, :]).then_inc(s.stored, 16)
                sp.wait_ge(s.stored, 64)


def rg_lru(nc, g, d, ps, px, gate):
    par, q = g.par, COL
    with ExitStack() as mem:
        xc = mem.enter_context(tensor(nc, "conv_out", [P, LRU_T, NT], F32))
        gr = mem.enter_context(tensor(nc, "gate_r", [P, LRU_T, NT], F32))
        gi = mem.enter_context(tensor(nc, "gate_i", [P, LRU_T, NT], F32))
        tmp = mem.enter_context(tensor(nc, "lru_tmp", [P, NT], F32))
        wax = mem.enter_context(tensor(nc, "lru_gates", [P, 2, LRU_T, P], F32))
        lam = mem.enter_context(tensor(nc, "lambda", [P, 6, LRU_T], F32))
        h_rows = mem.enter_context(tensor(nc, "h_rows", [9, RW], F32))
        with phase(nc, "cleared", "w_in", "padded", "steps", "lam_x", "gated", "lam_exp", "lam_sum", "lam_log", "conv", "gates_a", "gates_x", "gate_sig",
                   "log_a", "decayed", "tanhs", "under_root", "rooted", "gelus", "scanned", "turned", "rows", "stored", "act_steps", "gate_free") as (s, block):
            @block.gpsimd
            def _(pool):
                pool.memset(wax[:, :, :, :], 0.0).then_inc(s.cleared, 1)
                pool.memset(px[:, :, 0:PAD], 0.0).then_inc(s.padded, 1)

            @block.sync
            def _(sp):
                sp.wait_ge(s.cleared, 1)
                for n, w in enumerate((d.lru_wa, d.lru_wx)):
                    for o in range(2):
                        sp.dma_start(wax[64 * o:64 * o + 64, n, :, 64 * o:64 * o + 64],
                                     w[0].rearrange("(k o) i e -> o i k e", o=2)[o]).then_inc(s.w_in, 16)
                sp.wait_ge(s.rows, 1)
                sp.dma_start(d.lru_h_p[0], h_rows[0:1, :]).then_inc(s.stored, 16)
                sp.dma_start(d.lru_h_s[0], h_rows[1:9, :]).then_inc(s.stored, 16)
                sp.wait_ge(s.stored, 32)

            @block.vector
            def _(dve):
                link = linker(dve, s.steps)
                lq = q["lru_lambda"]
                dve.tensor_scalar(lam[:, 5, :], par[:, lq:lq + 4], -1.0, 40.0, ALU.mult, ALU.min).then_inc(s.lam_x, 1)
                dve.wait_ge(s.lam_exp, 1)
                dve.tensor_scalar(lam[:, 1, :], lam[:, 0, :], 1.0, None, ALU.add).then_inc(s.lam_sum, 1)
                dve.wait_ge(s.lam_log, 1)
                link(dve.tensor_scalar(lam[:, 3, :], lam[:, 1, :], 1.0, 1e-30, ALU.subtract, ALU.max))
                link(dve.reciprocal(lam[:, 4, :], lam[:, 3, :]))
                link(dve.tensor_tensor(lam[:, 3, :], lam[:, 0, :], lam[:, 4, :], ALU.mult))
                link(dve.tensor_tensor(lam[:, 4, :], lam[:, 2, :], lam[:, 3, :], ALU.mult))
                link(dve.scalar_tensor_tensor(lam[:, 4, :], lam[:, 0, :], 2.0 ** -24, lam[:, 4, :], ALU.min, ALU.max))
                link(dve.scalar_tensor_tensor(lam[:, 4, :], par[:, lq:lq + 4], -1.0, lam[:, 4, :], ALU.mult, ALU.max))
                link(dve.tensor_scalar(lam[:, 4, :], lam[:, 4, :], -8.0, None, ALU.mult))
                dve.wait_ge(s.padded, 1)
                cw, cb = q["lru_conv_w"], q["lru_conv_b"]
                c0 = g.conv0[:, :, :].rearrange("p k (b j) -> p k j b", j=3)
                for k in range(LRU_T):
                    w = [par[:, cw + 4 * j + k:cw + 4 * j + k + 1] for j in range(4)]
                    link(dve.tensor_scalar(xc[:, k, 0:T], px[:, k, 1:1 + T], w[0], par[:, cb + k:cb + k + 1], ALU.mult, ALU.add))
                    link(dve.tensor_scalar(xc[:, k, T:NT], c0[:, k, 0, :], w[0], par[:, cb + k:cb + k + 1], ALU.mult, ALU.add))
                    for j in range(1, 4):
                        link(dve.scalar_tensor_tensor(xc[:, k, 0:T], px[:, k, 1 + j:1 + j + T], w[j], xc[:, k, 0:T], ALU.mult, ALU.add))
                        old = c0[:, k, j, :] if j < 3 else px[:, k, PAD + T:PAD + NT]
                        link(dve.scalar_tensor_tensor(xc[:, k, T:NT], old, w[j], xc[:, k, T:NT], ALU.mult, ALU.add))
                    dve.sem_inc(s.conv, 1)
                for k in range(LRU_T):
                    dve.wait_ge(s.gate_sig, 2 * k + 2)
                    dve.tensor_scalar(gr[:, k, :], gr[:, k, :], lam[:, 4, k:k + 1], None, ALU.mult).then_inc(s.log_a, 1)
                    dve.tensor_tensor(gi[:, k, :], gi[:, k, :], xc[:, k, :], ALU.mult).then_inc(s.gated, 1)
                for k in range(LRU_T):
                    dve.wait_ge(s.tanhs, k + 1)
                    link(dve.tensor_scalar(tmp[:, :], gr[:, k, :], 1.0, None, ALU.add))
                    link(dve.reciprocal(tmp[:, :], tmp[:, :]))
                    dve.scalar_tensor_tensor(gr[:, k, :], gr[:, k, :], 2.0, tmp[:, :], ALU.mult, ALU.mult).then_inc(s.under_root, 1)
                    dve.wait_ge(s.under_root, k + 1)
                dve.wait_ge(s.gated, LRU_T)
                for k in range(LRU_T):
                    dve.wait_ge(s.rooted, k + 1)
                    link(dve.tensor_tensor(gi[:, k, :], gi[:, k, :], gr[:, k, :], ALU.mult))
                    link(dve.tensor_tensor_scan(gr[:, k, 0:T], xc[:, k, 0:T], gi[:, k, 0:T], 0.0, ALU.mult, ALU.add))
                    link(dve.tensor_tensor(gr[:, k, T:NT], xc[:, k, T:NT], g.h0[:, k, :], ALU.mult))
                    dve.tensor_tensor(gr[:, k, T:NT], gr[:, k, T:NT], gi[:, k, T:NT], ALU.add).then_inc(s.scanned, 1)
                for k in range(LRU_T):
                    dve.wait_ge(s.gelus, k + 1)
                    dve.wait_ge(s.scanned, k + 1)
                    link(dve.tensor_tensor(gate[:, k, :], gate[:, k, :], gr[:, k, :], ALU.mult))
                dve.wait_ge(s.turned, 1)
                dve.tensor_copy(h_rows[:, :], ps[0:9, 6, :]).then_inc(s.rows, 1)

            @block.tensor
            def _(pe):
                pe.wait_ge(s.w_in, 64)
                for k in range(LRU_T):
                    pe.wait_ge(s.conv, k + 1)
                    for o, done in ((0, s.gates_a), (1, s.gates_x)):
                        if k:
                            pe.wait_ge(s.gate_sig, 2 * k + o - 1)
                        for n in range(3):
                            last = pe.matmul(ps[:, 3 * o + n, 0:N3], wax[:, o, k, :], xc[:, k, n * N3:(n + 1) * N3],
                                             start=True, stop=True)
                        last.then_inc(done, 1)
                pe.wait_ge(s.scanned, LRU_T)
                for k in range(LRU_T):
                    last = pe.transpose(ps[0:9, 6, k * P:(k + 1) * P], gr[:, k, T - 1:NT], g.ident[:, :])
                last.then_inc(s.turned, 1)

            @block.scalar
            def _(act):
                act.wait_ge(s.lam_x, 1)
                act.activation(lam[:, 0, :], lam[:, 5, :], ACT.Exp).then_inc(s.lam_exp, 1)
                act.wait_ge(s.lam_sum, 1)
                act.activation(lam[:, 2, :], lam[:, 1, :], ACT.Ln).then_inc(s.lam_log, 1)
                for k in range(LRU_T):
                    act.wait_ge(s.gates_a, k + 1)
                    act.activation(cols3(gr[:, k, :]), bank3(ps, 0), ACT.Sigmoid, bias=par[:, q["lru_ba"] + k:q["lru_ba"] + k + 1]).then_inc(s.gate_sig, 1)
                    act.wait_ge(s.gates_x, k + 1)
                    act.activation(cols3(gi[:, k, :]), bank3(ps, 3), ACT.Sigmoid, bias=par[:, q["lru_bx"] + k:q["lru_bx"] + k + 1]).then_inc(s.gate_sig, 1)
                act.wait_ge(s.gated, LRU_T)
                for k in range(LRU_T):
                    act.activation(xc[:, k, :], gr[:, k, :], ACT.Exp).then_inc(s.decayed, 1)
                    act.wait_ge(s.decayed, k + 1)
                    act.activation(gr[:, k, :], gr[:, k, :], ACT.Tanh, scale=-1.0).then_inc(s.tanhs, 1)
                for k in range(LRU_T):
                    act.wait_ge(s.under_root, k + 1)
                    act.activation(gr[:, k, :], gr[:, k, :], ACT.Sqrt).then_inc(s.rooted, 1)
                for k in range(LRU_T):
                    act.activation(gate[:, k, :], gate[:, k, :], ACT.Gelu_apprx_tanh).then_inc(s.gelus, 1)


def token_shift(nc, g, d, ps, big, w2a, g2, kept, masks):
    mu = COL["mu_shift"]
    with ExitStack() as mem:
        diff = mem.enter_context(tensor(nc, "diff", [P, 2, T], F32))
        sdiff = mem.enter_context(tensor(nc, "sample_diff", [P, RWC_T, NS], F32))
        with phase(nc, "padded", "w_in", "steps", "pool_steps", "shifted", "act_steps", "mask_steps") as (s, block):
            @block.sync
            def _(sp):
                sp.dma_start(w2a[0:64, :], d.rw_w2[0]).then_inc(s.w_in, 16)
                sp.dma_start(w2a[64:128, :], d.rw_a2[0]).then_inc(s.w_in, 16)
                sp.dma_start(g2[:, :], d.rw_g2[0]).then_inc(s.w_in, 16)
                sp.wait_ge(s.w_in, 48)

            @block.vector
            def _(dve):
                link = linker(dve, s.steps)
                link(dve.memset(big[:, 0:RWC_T, 0:PAD], 0.0))
                p_s = big[:, 0:RWC_T, PAD + T:PAD + NT]
                link(dve.tensor_tensor(sdiff[:, :, :], g.shift0[:, :, :], p_s, ALU.subtract))
                link(dve.tensor_tensor(sdiff[:, :, :], sdiff[:, :, :],
                                       g.par[:, mu:mu + RWC_T].unsqueeze(2).to_broadcast([P, RWC_T, NS]), ALU.mult))
                link(dve.tensor_tensor(p_s, p_s, sdiff[:, :, :], ALU.add))
                order = [12, 13] + list(range(12))
                for n, k in enumerate(order):
                    row = big[:, k, :]
                    link(dve.tensor_tensor(diff[:, n % 2, :], row[:, PAD - 1:PAD - 1 + T], row[:, PAD:PAD + T], ALU.subtract))
                    dve.scalar_tensor_tensor(row[:, PAD:PAD + T], diff[:, n % 2, :], g.par[:, mu + k:mu + k + 1],
                                             row[:, PAD:PAD + T], ALU.mult, ALU.add).then_inc(s.shifted, 1)

            @block.scalar
            def _(act):
                act.wait_ge(s.shifted, 2)
                act.wait_ge(s.steps, 4)
                act.activation(big[:, 13, PAD:PAD + NT], big[:, 13, PAD:PAD + NT], ACT.Sigmoid).then_inc(s.act_steps, 1)
                act.activation(big[0:64, 12, PAD:PAD + NT], big[0:64, 12, PAD:PAD + NT], ACT.Tanh).then_inc(s.act_steps, 1)

            @block.gpsimd
            def _(pool):
                link = linker(pool, s.pool_steps)
                link(pool.memset(kept[:, :], 1.0))
                link(pool.memset(kept[:, 0:T:C], 0.0))
                link(pool.memset(kept[:, T:NT], 0.0))
                for m in range(10):
                    link(pool.memset(masks[:, m, :], 1.0))
                for h in range(2):
                    rows = slice(64 * h, 64 * h + 64)

                    def cut(m, pattern, base, mult, keep_where, shape=None):
                        v = masks[rows, m, :]
                        if shape:
                            v = v.rearrange("p (a b) -> p a b", b=shape)
                        link(pool.affine_select(out=v, in_=v, compare_op=keep_where, fill=0.0, base=base,
                                                pattern=pattern, channel_multiplier=mult))
                    cut(0, [[1, C]], 0, -1, ALU.is_gt)
                    cut(1, [[1, C]], 0, -1, ALU.is_ge)
                    cut(2, [[-1, C]], 0, 1, ALU.is_gt)
                    for lvl in range(6):
                        b = 1 << lvl
                        n = C // (2 * b)
                        v = masks[rows, 3 + lvl, :].rearrange("p (a b) -> p a b", b=2 * b)
                        link(pool.affine_select(out=v, in_=v, compare_op=ALU.is_ge, fill=0.0, base=0,
                                                pattern=[[-2 * b, n], [0, 2 * b]], channel_multiplier=1))
                        link(pool.affine_select(out=v, in_=v, compare_op=ALU.is_gt, fill=0.0, base=b,
                                                pattern=[[2 * b, n], [0, 2 * b]], channel_multiplier=-1))
                        link(pool.affine_select(out=v, in_=v, compare_op=ALU.is_ge, fill=0.0, base=-b,
                                                pattern=[[0, n], [1, 2 * b]], channel_multiplier=0))
                    v = masks[rows, 9, :].rearrange("p (a b) -> p a b", b=2)
                    link(pool.affine_select(out=v, in_=v, compare_op=ALU.is_equal, fill=0.0, base=-1,
                                            pattern=[[-2, C // 2], [0, 2]], channel_multiplier=1))
                    link(pool.affine_select(out=v, in_=v, compare_op=ALU.is_equal, fill=0.0, base=0,
                                            pattern=[[0, C // 2], [1, 2]], channel_multiplier=0))


def rwkv_pair(nc, g, d, ps, big, w2a, g2, kept, masks, i):
    par = g.par
    with ExitStack() as mem:
        def sb(name, shape):
            return mem.enter_context(tensor(nc, name, shape, F32))

        names = ["r", "k", "v", "lw", "cum", "a", "kk", "bonus", "e_cum", "e_neg", "e_prev", "tmp"]
        buf = {n: sb(f"pair_{n}", [P, NT]) for n in names}
        rs, ks, vs, lw, cum, a, kk, bonus, e_cum, e_neg, e_prev, tmp = (buf[n] for n in names)
        col = sb("pair_par", [P, 8])
        w2s, g2s = sb("w2_slice", [P, P]), sb("g2_slice", [P, P])
        vec = sb("sample_vec", [P, 5, NS])
        vs8 = sb("sample_v", [P, NS])
        dend = sb("chunk_decay", [P, NC])
        S = sb("state", [P, 3, HD])
        u = sb("u", [P, 2, 2, HD])
        s8 = sb("sample_state", [P, NS, HD])
        t8 = sb("sample_tmp", [P, 2, NS, HD])
        p8 = sb("sample_prod", [P, NS, HD])
        sa = sb("sample_sa", [P, NS])
        s_rows = sb("state_rows_out", [HD, P])
        inv, prod = sb("inverse", [P, T]), sb("level_product", [P, T])
        spare = [g.X[:, :, :].rearrange("p k c -> p (k c)")[:, n * T:(n + 1) * T] for n in range(4)]
        a_tok, b_tok, k_tok, v_tok = spare
        inv_t, lt, mak, mrb, mrk = (x[:, 0:T] for x in (lw, cum, e_cum, e_neg, e_prev))
        gt, hh = kk[:, 0:T], ks[:, 0:T]

        def tokm(x):
            return x.rearrange("p (t h c) -> p t h c", t=TT, h=2)

        def halves(x, b):
            return x[:, b * 512:(b + 1) * 512].rearrange("p (n c) -> p n c", c=64)

        def bank(b):
            return ps[:, b, :].rearrange("p (n c) -> p n c", c=64)

        def mask(m):
            return masks[:, m, :].unsqueeze(1).to_broadcast([P, 8, C])

        two = (0, 1)

        def blocks(half):
            for t in range(4):
                for cp in two:
                    for hp in two:
                        c = 2 * (4 * half + t) + cp
                        yield (slice(t * P + hp * 64, t * P + hp * 64 + 64), slice(64 * cp, 64 * cp + 64),
                               slice(64 * hp, 64 * hp + 64), slice(c * C, (c + 1) * C), 4 * half + t, hp)

        with phase(nc, "copied", "z_made", "a_made", "sig", "lw_done", "dve", "cummed", "exps", "sq", "ssum", "root",
                   "bon", "bsum", "ready", "turned", "tok_copied", "gram", "gram_taken", "level_t", "p_made",
                   "p_taken", "x_made", "x_taken", "xt_made", "xt_taken", "g_made", "g_taken", "u_made", "u_taken",
                   "s_made", "s_taken", "y_made", "y_taken", "vec_taken", "spread", "spread_made", "spread_used",
                   "s8_in", "s8_done", "stored", "mean", "cent", "csq", "var", "vroot", "gsum", "rows_t", "rows_c",
                   "decayed", "y8", "act_steps") as (s, block):

            @block.sync
            def _(sp):
                states = d.state_rwkv_wkv[0].rearrange("b h v k -> b (h v) k")
                sp.dma_start(s8[:, :, :], states[:, ds(i * P, P), :].rearrange("b p k -> p b k")).then_inc(s.s8_in, 16)
                sp.wait_ge(s.s8_done, 1)
                out_s = d.wkv_s[0].rearrange("b h v k -> b (h v) k")
                sp.dma_start(out_s[:, ds(i * P, P), :].rearrange("b p k -> p b k"), s8[:, :, :]).then_inc(s.stored, 16)
                sp.wait_ge(s.rows_c, 1)
                sp.dma_start(d.wkv_p[0, 0, ds(2 * i, 2), :, :].rearrange("h v k -> v h k"),
                             s_rows[:, :].rearrange("v (h k) -> v h k", h=2)).then_inc(s.stored, 16)
                sp.wait_ge(s.stored, 32)

            @block.gpsimd
            def _(pool):
                pool.tensor_copy(w2s[:, :], w2a[:, ds(i * P, P)]).then_inc(s.copied, 1)
                pool.tensor_copy(col[:, 0:7], par[:, ds(COL["rw_w0"] + i, 7, 4)]).then_inc(s.copied, 1)
                for x, t in ((ks, 4), (rs, 0), (vs, 8)):
                    pool.tensor_copy(x[:, :], big[:, ds(t + i, 1), PAD:PAD + NT].rearrange("p a c -> p (a c)")).then_inc(s.copied, 1)
                pool.tensor_copy(g2s[:, :], g2[:, ds(i * P, P)]).then_inc(s.copied, 1)
                pool.memset(S[:, 0, :], 0.0).then_inc(s.copied, 1)
                pool.wait_ge(s.gram_taken, 10)
                for lvl in range(1, 6):
                    if lvl > 1:
                        pool.wait_ge(s.p_taken, 2 * (lvl - 1))
                    for b in two:
                        pool.tensor_tensor(halves(tmp, b), halves(lt, b), mask(3 + lvl), ALU.mult).then_inc(s.level_t, 1)

            @block.vector
            def _(dve):
                link = linker(dve, s.dve)
                w0, a0, c_kk, c_ka, c_rk, lnw, lnb = (col[:, n:n + 1] for n in range(7))
                dve.wait_ge(s.copied, 5)
                link(dve.tensor_scalar(col[:, 7:8], c_ka, -1.0, 1.0, ALU.mult, ALU.add))
                link(dve.tensor_scalar(kk[:, :], ks[:, :], c_kk, None, ALU.mult))
                dve.sem_inc(s.sq, 1)
                dve.wait_ge(s.sig, 2)
                link(dve.tensor_scalar(lw[:, :], lw[:, :], DECAY, None, ALU.mult))
                link(dve.tensor_copy(vec[:, 0, :], lw[:, T:NT]))
                link(dve.memset(lw[:, T:NT], 0.0))
                link(dve.tensor_tensor_scan(cum[:, :], kept[:, :], lw[:, :], 0.0, ALU.mult, ALU.add))
                link(dve.tensor_tensor(e_prev[:, :], cum[:, :], lw[:, :], ALU.subtract))
                dve.sem_inc(s.cummed, 1)
                link(dve.tensor_scalar(bonus[:, :], a[:, :], c_ka, col[:, 7:8], ALU.mult, ALU.add))
                link(dve.tensor_tensor(ks[:, :], ks[:, :], bonus[:, :], ALU.mult))
                link(dve.scalar_tensor_tensor(bonus[:, :], rs[:, :], c_rk, ks[:, :], ALU.mult, ALU.mult))
                dve.sem_inc(s.bon, 1)
                dve.wait_ge(s.root, 1)
                link(dve.tensor_scalar(tmp[:, :], tmp[:, :], 1e-12, None, ALU.max))
                link(dve.reciprocal(tmp[:, :], tmp[:, :]))
                link(dve.tensor_tensor(kk[:, :], kk[:, :], tmp[:, :], ALU.mult))
                dve.wait_ge(s.bsum, 1)
                link(dve.tensor_tensor(cols3(bonus[:, :]), bank3(ps, 3), cols3(vs[:, :]), ALU.mult))
                dve.wait_ge(s.exps, 4)
                link(dve.tensor_tensor(a[:, :], kk[:, :], a[:, :], ALU.mult))
                link(dve.tensor_tensor(a[:, :], a[:, :], e_neg[:, :], ALU.mult))
                dve.sem_inc(s.ready, 1)
                link(dve.scalar_tensor_tensor(kk[:, :], kk[:, :], -1.0, e_prev[:, :], ALU.mult, ALU.mult))
                dve.sem_inc(s.ready, 1)
                link(dve.tensor_tensor(ks[:, :], ks[:, :], e_neg[:, :], ALU.mult))
                dve.sem_inc(s.ready, 1)
                link(dve.tensor_tensor(rs[:, :], rs[:, :], e_cum[:, :], ALU.mult))
                dve.sem_inc(s.ready, 1)
                for n, x in ((1, kk), (2, a), (3, ks), (4, rs)):
                    link(dve.tensor_copy(vec[:, n, :], x[:, T:NT]))
                link(dve.tensor_copy(vs8[:, :], vs[:, T:NT]))
                link(dve.tensor_copy(dend[:, :], e_cum[:, C - 1:T:C]))
                dve.sem_inc(s.vec_taken, 1)
                for n in range(1, 8, 2):
                    dve.wait_ge(s.turned, n + 1)
                    dst = (b_tok, a_tok, k_tok, v_tok)[n // 2]
                    dve.tensor_copy(dst[:, 512:1024], ps[:, n, :]).then_inc(s.tok_copied, 1)
                for n, (dst, m) in enumerate(((lt, 0), (inv, 9), (mak, 0), (mrb, 1), (mrk, 1))):
                    for h in two:
                        dve.wait_ge(s.gram, 2 * n + h + 1)
                        dve.tensor_tensor(tokm(dst)[:, :, h, :], bank((2 * n + h) % 6), mask(m), ALU.mult).then_inc(s.gram_taken, 1)
                dve.wait_ge(s.gram_taken, 10)
                idb = g.ident2[:, :].unsqueeze(1).to_broadcast([P, 8, C])
                for b in two:
                    link(dve.tensor_tensor(halves(inv_t, b), halves(lt, b), mask(3), ALU.mult))
                    link(dve.tensor_tensor(halves(inv_t, b), halves(inv_t, b), idb, ALU.add))
                    link(dve.tensor_tensor(halves(inv, b), halves(inv, b), idb, ALU.add))
                    dve.sem_inc(s.x_taken, 1)
                    dve.sem_inc(s.xt_taken, 1)
                for lvl in range(1, 6):
                    for b in two:
                        dve.wait_ge(s.xt_made, 2 * (lvl - 1) + b + 1)
                        if lvl < 5:
                            dve.wait_ge(s.x_made, 2 * (lvl - 1) + b + 1)
                            dve.tensor_tensor(halves(inv, b), bank(2 + b), halves(inv, b), ALU.add).then_inc(s.x_taken, 1)
                        dve.tensor_tensor(halves(inv_t, b), bank(4 + b), halves(inv_t, b), ALU.add).then_inc(s.xt_taken, 1)
                dve.wait_ge(s.s8_in, 16)
                sample_step(dve, link, s, g, ps, s8, t8, p8, sa, vec, vs8, tmp)
                dve.wait_ge(s.g_taken, 6)
                for c in range(NC):
                    dve.wait_ge(s.u_made, c + 1)
                    rows = slice(64 * (c % 2), 64 * (c % 2) + 64)
                    if c >= 2:
                        dve.wait_ge(s.y_made, c - 1)
                    dve.tensor_tensor(u[rows, (c // 2) % 2, :, :], ps[rows, 4:6, 0:HD],
                                      tokm(hh)[rows, c // 2, :, :], ALU.add).then_inc(s.u_taken, 1)
                    dve.wait_ge(s.s_made, c + 1)
                    dve.wait_ge(s.decayed, c + 1)
                    dve.scalar_tensor_tensor(S[:, (c + 1) % 2, :], ps[:, 6 + c % 2, 0:HD], dend[:, c:c + 1], S[:, 2, :],
                                             ALU.mult, ALU.add).then_inc(s.s_taken, 1)
                dve.wait_ge(s.y_taken, 1)
                for cp in two:
                    y = tokm(tmp[:, 0:T])[:, :, cp, :]
                    link(dve.tensor_tensor(y, y, bank(2 + cp), ALU.add))
                dve.sem_inc(s.y8, 1)
                dve.wait_ge(s.mean, 1)
                link(dve.scalar_tensor_tensor(cols3(e_cum[:, :]), bank3(ps, 2), -1.0 / HD, cols3(tmp[:, :]), ALU.mult, ALU.add))
                dve.sem_inc(s.cent, 1)
                dve.wait_ge(s.vroot, 1)
                link(dve.reciprocal(e_prev[:, :], e_prev[:, :]))
                link(dve.tensor_tensor(e_cum[:, :], e_cum[:, :], e_prev[:, :], ALU.mult))
                link(dve.tensor_scalar(e_cum[:, :], e_cum[:, :], lnw, lnb, ALU.mult, ALU.add))
                link(dve.tensor_tensor(e_cum[:, :], e_cum[:, :], bonus[:, :], ALU.add))
                dve.wait_ge(s.gsum, 1)
                row = big[:, ds(i, 1), PAD:PAD + NT].rearrange("p a (n c) -> p (a n) c", n=3)
                link(dve.tensor_tensor(row, bank3(ps, 2), cols3(e_cum[:, :]), ALU.mult))

            @block.scalar
            def _(act):
                w0, a0 = col[:, 0:1], col[:, 1:2]
                act.wait_ge(s.copied, 2)
                act.wait_ge(s.z_made, 1)
                act.activation(cols3(lw[:, :]), bank3(ps, 0), ACT.Sigmoid, bias=w0).then_inc(s.sig, 1)
                act.wait_ge(s.a_made, 1)
                act.activation(cols3(a[:, :]), bank3(ps, 3), ACT.Sigmoid, bias=a0).then_inc(s.sig, 1)
                act.wait_ge(s.sq, 1)
                act.activation(tmp[:, :], kk[:, :], ACT.Square).then_inc(s.act_steps, 1)
                act.wait_ge(s.cummed, 1)
                act.activation(e_neg[:, :], cum[:, :], ACT.Exp, scale=-1.0).then_inc(s.exps, 1)
                act.activation(e_prev[:, :], e_prev[:, :], ACT.Exp).then_inc(s.exps, 1)
                act.activation(e_cum[:, :], cum[:, :], ACT.Exp).then_inc(s.exps, 1)
                act.activation(vec[:, 0, :], vec[:, 0, :], ACT.Exp).then_inc(s.exps, 1)
                act.wait_ge(s.ssum, 1)
                act.activation(cols3(tmp[:, :]), bank3(ps, 0), ACT.Sqrt).then_inc(s.root, 1)
                for n in range(0, 8, 2):
                    act.wait_ge(s.turned, n + 1)
                    dst = (b_tok, a_tok, k_tok, v_tok)[n // 2]
                    act.activation(dst[:, 0:512], ps[:, n, :], ACT.Copy).then_inc(s.act_steps, 1)
                for lvl in range(1, 6):
                    for b in two:
                        act.wait_ge(s.p_made, 2 * (lvl - 1) + b + 1)
                        if lvl > 1:
                            act.wait_ge(s.xt_made, 2 * (lvl - 1))
                        act.activation(halves(prod, b), bank(b), ACT.Copy).then_inc(s.p_taken, 1)
                for n, dst in enumerate((gt, prod, hh)):
                    for b in two:
                        act.wait_ge(s.g_made, 2 * n + b + 1)
                        to = tokm(dst)[:, :, b, :] if n == 0 else halves(dst, b)
                        act.activation(to, bank(2 * n + b), ACT.Copy).then_inc(s.g_taken, 1)
                for c in range(NC):
                    if c:
                        act.wait_ge(s.s_taken, c)
                    act.activation(S[:, 2, :], S[:, c % 2, :], ACT.Copy, scale=dend[:, c:c + 1]).then_inc(s.decayed, 1)
                act.wait_ge(s.y_made, NC)
                act.activation(tmp[:, 0:T].rearrange("p (b c) -> p b c", b=2), ps[:, 0:2, :], ACT.Copy).then_inc(s.y_taken, 1)
                act.wait_ge(s.rows_t, 1)
                act.activation(s_rows[:, :], ps[0:HD, 5, 0:P], ACT.Copy).then_inc(s.rows_c, 1)
                act.wait_ge(s.cent, 1)
                act.activation(e_neg[:, :], e_cum[:, :], ACT.Square).then_inc(s.csq, 1)
                act.wait_ge(s.var, 1)
                act.activation(cols3(e_prev[:, :]), bank3(ps, 5), ACT.Sqrt, scale=1.0 / HD, bias=g.epsc[:, 1:2]).then_inc(s.vroot, 1)

            @block.tensor
            def _(pe):
                def head_sums(x, first, done):
                    for n in range(3):
                        last = pe.matmul(ps[:, first + n, 0:N3], g.blockones[:, :], x[:, n * N3:(n + 1) * N3], start=True, stop=True)
                    last.then_inc(done, 1)

                def block_row(w, x, first, done):
                    for n in range(3):
                        last = pe.matmul(ps[:, first + n, 0:N3], w, x[:, PAD + n * N3:PAD + (n + 1) * N3], start=True, stop=True)
                    last.then_inc(done, 1)

                pe.wait_ge(s.copied, 1)
                block_row(w2s[0:64, :], big[0:64, 12, :], 0, s.z_made)
                block_row(w2s[64:128, :], big[64:128, 12, :], 3, s.a_made)
                pe.wait_ge(s.act_steps, 1)
                head_sums(tmp, 0, s.ssum)
                pe.wait_ge(s.sig, 2)
                pe.wait_ge(s.bon, 1)
                head_sums(bonus, 3, s.bsum)
                pe.wait_ge(s.root, 1)
                pe.wait_ge(s.ready, 4)
                for n in range(8):
                    src = (a, kk, ks, vs)[n // 2]
                    for t in range(4):
                        tt = 4 * (n % 2) + t
                        last = pe.transpose(ps[:, n, t * P:(t + 1) * P], src[:, tt * P:(tt + 1) * P], g.ident[:, :])
                    last.then_inc(s.turned, 1)
                gram = ((a, kk), (kk, a), (ks, kk), (a, rs), (ks, rs))
                for n, (l, r) in enumerate(gram):
                    for h in two:
                        g_at = 2 * n + h
                        hp = slice(64 * h, 64 * h + 64)
                        if g_at < 6:
                            if g_at % 2:
                                pe.wait_ge(s.tok_copied, g_at // 2 + 1)
                            else:
                                pe.wait_ge(s.act_steps, 2 + g_at // 2)
                        else:
                            pe.wait_ge(s.gram_taken, g_at - 5)
                        for c in range(NC):
                            cp, cols = slice(64 * (c % 2), 64 * (c % 2) + 64), slice(c * C, (c + 1) * C)
                            last = pe.matmul(ps[cp, g_at % 6, (c // 2) * 64:(c // 2 + 1) * 64], l[hp, cols], r[hp, cols],
                                             start=True, stop=True)
                        last.then_inc(s.gram, 1)
                pe.wait_ge(s.gram_taken, 10)
                for lvl in range(1, 6):
                    for b in two:
                        pe.wait_ge(s.level_t, 2 * (lvl - 1) + b + 1)
                        pe.wait_ge(s.x_taken, 2 * (lvl - 1) + b + 1)
                        for at, cp, hp, _, tt, h in blocks(b):
                            m = slice(tt * P + h * 64, tt * P + h * 64 + 64)
                            last = pe.matmul(ps[cp, b, at], tmp[cp, m], inv[cp, m], start=True, stop=True)
                        last.then_inc(s.p_made, 1)
                    for b in two:
                        pe.wait_ge(s.p_taken, 2 * (lvl - 1) + b + 1)
                        pe.wait_ge(s.xt_taken, 2 * (lvl - 1) + b + 1)
                        if lvl < 5:
                            for at, cp, hp, _, tt, h in blocks(b):
                                m = slice(tt * P + h * 64, tt * P + h * 64 + 64)
                                last = pe.matmul(ps[cp, 2 + b, at], inv_t[cp, m], prod[cp, m], start=True, stop=True)
                            last.then_inc(s.x_made, 1)
                        for at, cp, hp, _, tt, h in blocks(b):
                            m = slice(tt * P + h * 64, tt * P + h * 64 + 64)
                            last = pe.matmul(ps[cp, 4 + b, at], prod[cp, m], inv_t[cp, m], start=True, stop=True)
                        last.then_inc(s.xt_made, 1)
                pe.wait_ge(s.xt_taken, 12)
                for cp in two:
                    cpr = slice(64 * cp, 64 * cp + 64)
                    for tt in range(TT):
                        for h in two:
                            hpr = slice(64 * h, 64 * h + 64)
                            m = slice(tt * P + h * 64, tt * P + h * 64 + 64)
                            last = pe.matmul(ps[hpr, cp, tt * C:(tt + 1) * C], a_tok[cpr, m], inv_t[cpr, m],
                                             start=True, stop=True)
                    last.then_inc(s.g_made, 1)
                for n, (l, r) in enumerate(((mak, v_tok), (inv_t, prod))):
                    for b in two:
                        if n:
                            pe.wait_ge(s.g_taken, 3 + b)
                        for at, cp, hp, _, tt, h in blocks(b):
                            m = slice(tt * P + h * 64, tt * P + h * 64 + 64)
                            last = pe.matmul(ps[cp, 2 * (n + 1) + b, at], l[cp, m], r[cp, m], start=True, stop=True)
                        last.then_inc(s.g_made, 1)
                pe.wait_ge(s.act_steps, 5)
                pe.wait_ge(s.tok_copied, 4)
                for n in range(5):
                    pe.wait_ge(s.spread, n + 1)
                    if n >= 2:
                        pe.wait_ge(s.spread_used, n - 1)
                    pe.matmul(ps[:, 6 + n % 2, :], g.blockones[:, :], t8[:, n % 2, :, :].rearrange("p b k -> p (b k)"),
                              start=True, stop=True).then_inc(s.spread_made, 1)
                pe.wait_ge(s.spread_used, 5)
                pe.wait_ge(s.g_taken, 6)
                pe.wait_ge(s.copied, 7)
                for c in range(NC):
                    tt, cp = c // 2, c % 2
                    cpr = slice(64 * cp, 64 * cp + 64)
                    ub = (c // 2) % 2
                    cols = slice(c * C, (c + 1) * C)
                    if c:
                        pe.wait_ge(s.s_taken, c)
                    for h in two:
                        hpr = slice(64 * h, 64 * h + 64)
                        last = pe.matmul(ps[cpr, 4 + h, 0:HD], gt[hpr, cols], S[hpr, c % 2, :], start=True, stop=True)
                    last.then_inc(s.u_made, 1)
                    heads = [(slice(64 * h, 64 * h + 64), slice(tt * P + h * 64, tt * P + h * 64 + 64),
                              u[cpr, ub, h, :], ps[64 * h:64 * h + 64, 6 + cp, 0:HD],
                              ps[64 * h:64 * h + 64, c // 8, (c % 8) * C:(c % 8 + 1) * C],
                              ps[64 * h:64 * h + 64, 2 + cp, tt * C:(tt + 1) * C]) for h in two]
                    for hpr, m, _, new, y_s, y in heads:
                        pe.matmul(y_s, S[hpr, c % 2, :], rs[hpr, cols], start=True, stop=True)
                        pe.matmul(new, k_tok[cpr, m], v_tok[cpr, m], start=True, stop=False)
                        pe.matmul(y, v_tok[cpr, m], mrk[cpr, m], start=True, stop=False)
                    pe.wait_ge(s.u_taken, c + 1)
                    for hpr, m, uh, new, _, y in heads:
                        last = pe.matmul(new, b_tok[cpr, m], uh, start=False, stop=True)
                    last.then_inc(s.s_made, 1)
                    for hpr, m, uh, new, _, y in heads:
                        last = pe.matmul(y, uh, mrb[cpr, m], start=False, stop=True)
                    last.then_inc(s.y_made, 1)
                pe.wait_ge(s.y_taken, 1)
                pe.wait_ge(s.s_taken, NC)
                pe.transpose(ps[0:HD, 5, 0:P], S[:, NC % 2, :], g.ident[:, :]).then_inc(s.rows_t, 1)
                pe.wait_ge(s.y8, 2)
                head_sums(tmp, 2, s.mean)
                pe.wait_ge(s.csq, 1)
                pe.wait_ge(s.rows_c, 1)
                head_sums(e_neg, 5, s.var)
                pe.wait_ge(s.cent, 1)
                block_row(g2s[:, :], big[:, 13, :], 2, s.gsum)


def sample_step(dve, link, s, g, ps, s8, t8, p8, sa, vec, vs8, y):
    order = [1, 0, 2, 3, 4]

    def fill(n):
        if n >= 2:
            dve.wait_ge(s.spread_made, n - 1)
        link(dve.tensor_tensor(t8[:, n % 2, :, :], g.ident2[:, :].unsqueeze(1).to_broadcast([P, NS, HD]),
                               vec[:, order[n], :].unsqueeze(2).to_broadcast([P, NS, HD]), ALU.mult))
        dve.sem_inc(s.spread, 1)

    def spread(n):
        dve.wait_ge(s.spread_made, n + 1)
        return ps[:, 6 + n % 2, :].rearrange("p (b k) -> p b k", k=HD)

    fill(0)
    fill(1)
    for n in range(5):
        x = spread(n)
        if n == 0:
            link(dve.tensor_tensor(p8[:, :, :], s8[:, :, :], x, ALU.mult))
            link(dve.tensor_reduce(sa[:, :], p8[:, :, :], AX.X, ALU.add))
        elif n == 1:
            link(dve.tensor_tensor(s8[:, :, :], s8[:, :, :], x, ALU.mult))
        elif n < 4:
            rows = (sa, vs8)[n - 2]
            link(dve.tensor_tensor(p8[:, :, :], x, rows[:, :].unsqueeze(2).to_broadcast([P, NS, HD]), ALU.mult))
            link(dve.tensor_tensor(s8[:, :, :], s8[:, :, :], p8[:, :, :], ALU.add))
        else:
            dve.sem_inc(s.s8_done, 1)
            link(dve.tensor_tensor(p8[:, :, :], s8[:, :, :], x, ALU.mult))
            link(dve.tensor_reduce(y[:, T:NT], p8[:, :, :], AX.X, ALU.add))
            dve.sem_inc(s.y8, 1)
        dve.sem_inc(s.spread_used, 1)
        if n + 2 < 5:
            fill(n + 2)


def memory_attention(nc, g, d, ps, layer):
    with ExitStack() as mem:
        Q = mem.enter_context(tensor(nc, "mem_q", [P, MH, NT]))
        kt = mem.enter_context(tensor(nc, "mem_kt", [P, MH, MEM]))
        vtok = mem.enter_context(tensor(nc, "mem_v", [P, 2, MH * P]))
        memory_kv(nc, g, d, ps, layer, kt, vtok)
        with ExitStack() as inner:
            H = parts(nc, inner, "h_mem", [P, DT, NT])
            rms_norm(nc, g, ps, H, COL["g_mem"] + layer * DT)
            project(nc, ps, tiles_of(d.wq_mem[layer], DT), DT, MH // 2, H, kept_in(lambda m: Q[:, m, :]))
        norm_queries(nc, g, ps, Q, layer)
        memory_attention_samples(nc, g, d, ps, layer, Q)
        with ExitStack() as inner:
            bufs = record(
                q=inner.enter_context(tensor(nc, "head_q", [P, T])), k=inner.enter_context(tensor(nc, "head_k", [P, MEM])),
                v=inner.enter_context(tensor(nc, "head_v", [P, 2, P])), p=inner.enter_context(tensor(nc, "probs", [P, 2, MEM])),
                pt=inner.enter_context(tensor(nc, "probs_t", [P, 2, MEM])), stat=inner.enter_context(tensor(nc, "stats", [P, 2, 4])))
            with nc.Fori(0, MH) as head:
                memory_attention_head(nc, g, ps, Q, kt, vtok, bufs, head)
        with ExitStack() as inner:
            O = parts(nc, inner, "mem_out", [P, MH, NT])
            project(nc, ps, tiles_of(d.wo_mem[layer], MH), MH, DT // 2, O, add_to_residual(g), split=[Q[:, h, :] for h in range(MH)])


def memory_kv(nc, g, d, ps, layer, kt, vtok):
    with ExitStack() as mem:
        mt = mem.enter_context(tensor(nc, "mem_tokens", [P, 2, D]))
        mg = mem.enter_context(tensor(nc, "mem_normed", [P, DT, MEM]))
        W = [mem.enter_context(tensor(nc, f"mem_w{n}", [P, DT, 512])) for n in range(2)]
        ktok = mem.enter_context(tensor(nc, "mem_k", [P, 2, 512]))
        junk = mem.enter_context(tensor(nc, "mem_squares", [P, D]))
        ss = mem.enter_context(tensor(nc, "mem_sums", [P, 12]))
        gain = COL["g_memkv"] + layer * DT
        with phase(nc, "mem_in", ("w_in", 2), "sums", "rms", "rstd", "normed", "turned", "gained", "k_made", "v_made",
                   "k_sums", "k_rms", "k_rstd", "k_normed", "v_taken", "k_turned", "kt_taken", "stored") as (s, block):
            @block.sync
            def _(sp):
                sp.dma_start(mt[:, :, :], d.mem_prompt[0].rearrange("(t p) c -> p t c", p=P)).then_inc(s.mem_in, 16)
                for n, w in enumerate((d.wk_mem, d.wv_mem)):
                    sp.dma_start(W[n][:, :, :], weight_blocks(w[layer], DT)).then_inc(s.w_in[n], 16)
                sp.wait_ge(s.k_normed, 8)
                sp.dma_start(d.mem_k_p[layer, 0].rearrange("(t p) h c -> p t (h c)", p=P), ktok[:, :, :]).then_inc(s.stored, 16)
                sp.wait_ge(s.v_taken, 1)
                sp.dma_start(d.mem_v_p[layer, 0].rearrange("(t p) h c -> p t (h c)", p=P), vtok[:, :, :]).then_inc(s.stored, 16)
                sp.wait_ge(s.stored, 32)

            @block.scalar
            def _(act):
                act.wait_ge(s.mem_in, 16)
                for t in range(2):
                    if t:
                        act.wait_ge(s.sums, 1)
                    act.activation(junk[:, :], mt[:, t, :], ACT.Square, accum_out=ss[:, t:t + 1]).then_inc(s.sums, 1)
                act.wait_ge(s.sums, 2)
                act.activation(ss[:, 2:4], ss[:, 0:2], ACT.Sqrt, scale=1.0 / D, bias=g.epsc[:, 0:1]).then_inc(s.rms, 1)
                act.wait_ge(s.k_made, 2)
                for t in range(2):
                    for h in range(MH):
                        n = 4 * t + h
                        act.wait_ge(s.sums, 2 + n)
                        act.activation(junk[:, 0:P], ps[:, 4 + t, h * P:(h + 1) * P], ACT.Square,
                                       accum_out=ss[:, 4 + n:5 + n]).then_inc(s.sums, 1)
                act.wait_ge(s.sums, 10)
                act.activation(ss[:, 4:12], ss[:, 4:12], ACT.Sqrt, scale=1.0 / P, bias=g.epsc[:, 0:1]).then_inc(s.k_rms, 1)
                act.wait_ge(s.v_made, 2)
                act.activation(vtok[:, :, :], ps[:, 6:8, :], ACT.Copy).then_inc(s.v_taken, 1)
                act.wait_ge(s.k_turned, 1)
                for t in range(2):
                    act.activation(kt[:, :, t * P:(t + 1) * P], ps[:, t, :].rearrange("p (h c) -> p h c", h=MH), ACT.Copy).then_inc(s.kt_taken, 1)

            @block.vector
            def _(dve):
                dve.wait_ge(s.rms, 1)
                dve.reciprocal(ss[:, 2:4], ss[:, 2:4]).then_inc(s.rstd, 1)
                dve.wait_ge(s.rstd, 1)
                for t in range(2):
                    dve.tensor_scalar(mt[:, t, :], mt[:, t, :], ss[:, 2 + t:3 + t], None, ALU.mult).then_inc(s.normed, 1)
                dve.wait_ge(s.turned, 4)
                for k in range(DT):
                    dve.tensor_scalar(mg[:, k, :], ps[:, k // 2, (k % 2) * MEM:(k % 2 + 1) * MEM],
                                      g.par[:, gain + k:gain + k + 1], None, ALU.mult).then_inc(s.gained, 1)
                dve.wait_ge(s.k_rms, 1)
                dve.reciprocal(ss[:, 4:12], ss[:, 4:12]).then_inc(s.k_rstd, 1)
                dve.wait_ge(s.k_rstd, 1)
                for t in range(2):
                    for h in range(MH):
                        dve.scalar_tensor_tensor(ktok[:, t, h * P:(h + 1) * P], ps[:, 4 + t, h * P:(h + 1) * P],
                                                 ss[:, 4 + 4 * t + h:5 + 4 * t + h], g.kn[:, layer, :],
                                                 ALU.mult, ALU.mult).then_inc(s.k_normed, 1)

            @block.tensor
            def _(pe):
                pe.wait_ge(s.normed, 2)
                for k in range(DT):
                    for t in range(2):
                        last = pe.transpose(ps[:, k // 2, (k % 2) * MEM + t * P:(k % 2) * MEM + (t + 1) * P],
                                            mt[:, t, k * P:(k + 1) * P], g.ident[:, :])
                    if k % 2:
                        last.then_inc(s.turned, 1)
                pe.wait_ge(s.gained, DT)
                for n, done in enumerate((s.k_made, s.v_made)):
                    pe.wait_ge(s.w_in[n], 16)
                    for t in range(2):
                        for k in range(DT):
                            last = pe.matmul(ps[:, 4 + 2 * n + t, :], mg[:, k, t * P:(t + 1) * P], W[n][:, k, :],
                                             start=k == 0, stop=k == DT - 1)
                        last.then_inc(done, 1)
                pe.wait_ge(s.k_normed, 8)
                for t in range(2):
                    for h in range(MH):
                        last = pe.transpose(ps[:, t, h * P:(h + 1) * P], ktok[:, t, h * P:(h + 1) * P], g.ident[:, :])
                last.then_inc(s.k_turned, 1)


def norm_queries(nc, g, ps, Q, layer):
    qn = COL["qn_mem"] + layer
    with ExitStack() as mem:
        sq = mem.enter_context(tensor(nc, "q_squares", [P, 2, NT]))
        rms = mem.enter_context(tensor(nc, "q_rms", [P, 2, NT]))
        with phase(nc, "squared", "summed", "rooted", "inverted", "scaled") as (s, block):
            @block.scalar
            def _(act):
                for h in range(MH + 1):
                    if h < MH:
                        if h >= 2:
                            act.wait_ge(s.summed, h - 1)
                        act.activation(sq[:, h % 2, :], Q[:, h, :], ACT.Square).then_inc(s.squared, 1)
                    if h:
                        act.wait_ge(s.summed, h)
                        if h >= 3:
                            act.wait_ge(s.scaled, h - 2)
                        act.activation(cols3(rms[:, (h - 1) % 2, :]), bank3(ps, 3 * ((h - 1) % 2)), ACT.Sqrt, scale=1.0 / P,
                                       bias=g.epsc[:, 0:1]).then_inc(s.rooted, 1)

            @block.tensor
            def _(pe):
                for h in range(MH):
                    pe.wait_ge(s.squared, h + 1)
                    if h >= 2:
                        pe.wait_ge(s.rooted, h - 1)
                    for n in range(3):
                        last = pe.matmul(ps[:, 3 * (h % 2) + n, 0:N3], g.ones[:, :], sq[:, h % 2, n * N3:(n + 1) * N3],
                                         start=True, stop=True)
                    last.then_inc(s.summed, 1)

            @block.vector
            def _(dve):
                for h in range(MH):
                    dve.wait_ge(s.rooted, h + 1)
                    dve.reciprocal(rms[:, h % 2, :], rms[:, h % 2, :]).then_inc(s.inverted, 1)
                    dve.wait_ge(s.inverted, h + 1)
                    dve.scalar_tensor_tensor(Q[:, h, :], Q[:, h, :], g.par[:, qn:qn + 1], rms[:, h % 2, :],
                                             ALU.mult, ALU.mult).then_inc(s.scaled, 1)


def memory_attention_samples(nc, g, d, ps, layer, Q):
    scale = P ** -0.5
    NQ = NS * MH
    with ExitStack() as mem:
        KA = mem.enter_context(tensor(nc, "cache_k", [P, NS, 2, 512]))
        VA = mem.enter_context(tensor(nc, "cache_v", [P, NS, 2, 512]))
        qd = mem.enter_context(tensor(nc, "q_diag", [P, 2, MH, P]))
        prod = mem.enter_context(tensor(nc, "products", [P, 2, 512]))
        Z = mem.enter_context(tensor(nc, "scores", [P, 2, NQ]))
        stat = mem.enter_context(tensor(nc, "s_stats", [NQ, 4]))
        pz = mem.enter_context(tensor(nc, "s_probs", [NQ, MEM]))
        pt = mem.enter_context(tensor(nc, "s_probs_t", [P, 2, NQ]))
        with phase(nc, ("k_in", NS), "v_in", "diag", "spread", "steps", "scored", "z_turned", "shift", "exped",
                   "normed", "p_turned", "p_taken", "valued", "stored") as (s, block):
            @block.sync
            def _(sp):
                for b in range(NS):
                    sp.dma_start(KA[:, b, :, :], d.cache_mem_k[layer, b].rearrange("(t p) h c -> p t (h c)", p=P)).then_inc(s.k_in[b], 16)
                for b in range(NS):
                    sp.dma_start(VA[:, b, :, :], d.cache_mem_v[layer, b].rearrange("(t p) h c -> p t (h c)", p=P)).then_inc(s.v_in, 16)

            @block.gpsimd
            def _(pool):
                for b in range(NS):
                    if b >= 2:
                        pool.wait_ge(s.spread, b - 1)
                    pool.tensor_tensor(qd[:, b % 2, :, :], g.ident[:, :].unsqueeze(1).to_broadcast([P, MH, P]),
                                       Q[:, :, T + b:T + b + 1].to_broadcast([P, MH, P]), ALU.mult).then_inc(s.diag, 1)

            @block.vector
            def _(dve):
                link = linker(dve, s.steps)
                for b in range(NS):
                    dve.wait_ge(s.k_in[b], 16)
                    dve.wait_ge(s.spread, b + 1)
                    for t in range(2):
                        link(dve.tensor_tensor(prod[:, t, :], KA[:, b, t, :], ps[:, b % 2, :], ALU.mult))
                        link(dve.tensor_reduce(Z[:, t, b * MH:(b + 1) * MH], prod[:, t, :].rearrange("p (h c) -> p h c", h=MH),
                                               AX.X, ALU.add))
                    dve.sem_inc(s.scored, 1)
                dve.wait_ge(s.z_turned, 1)
                link(dve.tensor_reduce(stat[:, 0:1], ps[0:NQ, 2, 0:MEM], AX.X, ALU.max))
                dve.tensor_scalar(stat[:, 1:2], stat[:, 0:1], -scale, None, ALU.mult).then_inc(s.shift, 1)
                dve.wait_ge(s.exped, 1)
                link(dve.reciprocal(stat[:, 3:4], stat[:, 2:3]))
                dve.tensor_scalar(pz[:, :], pz[:, :], stat[:, 3:4], None, ALU.mult).then_inc(s.normed, 1)
                dve.wait_ge(s.valued, 1)
                dve.tensor_copy(Q[:, :, T:NT], ps[:, 4, 0:NQ].rearrange("p (h b) -> p h b", h=MH)).then_inc(s.stored, 1)

            @block.scalar
            def _(act):
                act.wait_ge(s.shift, 1)
                act.activation(pz[:, :], ps[0:NQ, 2, 0:MEM], ACT.Exp, scale=scale, bias=stat[:, 1:2],
                               accum_out=stat[:, 2:3]).then_inc(s.exped, 1)
                act.wait_ge(s.p_turned, 1)
                act.activation(pt[:, :, :], ps[:, 3, 0:2 * NQ].rearrange("p (t n) -> p t n", t=2), ACT.Copy).then_inc(s.p_taken, 1)

            @block.tensor
            def _(pe):
                for b in range(NS):
                    pe.wait_ge(s.diag, b + 1)
                    if b >= 2:
                        pe.wait_ge(s.scored, b - 1)
                    pe.matmul(ps[:, b % 2, :], g.ones[:, :], qd[:, b % 2, :, :].rearrange("p h c -> p (h c)"),
                              start=True, stop=True).then_inc(s.spread, 1)
                pe.wait_ge(s.scored, NS)
                for t in range(2):
                    last = pe.transpose(ps[0:NQ, 2, t * P:(t + 1) * P], Z[:, t, :], g.ident[:, :])
                last.then_inc(s.z_turned, 1)
                pe.wait_ge(s.normed, 1)
                for t in range(2):
                    last = pe.transpose(ps[:, 3, t * NQ:(t + 1) * NQ], pz[:, t * P:(t + 1) * P], g.ident[0:NQ, 0:NQ])
                last.then_inc(s.p_turned, 1)
                pe.wait_ge(s.v_in, 16 * NS)
                pe.wait_ge(s.p_taken, 1)
                for b in range(NS):
                    for h in range(MH):
                        for t in range(2):
                            last = pe.matmul(ps[:, 4, h * NS + b:h * NS + b + 1], VA[:, b, t, h * P:(h + 1) * P],
                                             pt[:, t, b * MH + h:b * MH + h + 1], start=t == 0, stop=t == 1)
                last.then_inc(s.valued, 1)


def memory_attention_head(nc, g, ps, Q, kt, vtok, b, i):
    scale = P ** -0.5
    with phase(nc, "copied", "scored", "steps", "shift", "exped", "scaled", "turned", "taken", "valued", "done") as (s, block):
        @block.gpsimd
        def _(pool):
            pool.tensor_copy(b.q[:, :], Q[:, ds(i, 1), 0:T].rearrange("p a c -> p (a c)")).then_inc(s.copied, 1)
            pool.tensor_copy(b.k[:, :], kt[:, ds(i, 1), :].rearrange("p a c -> p (a c)")).then_inc(s.copied, 1)
            pool.tensor_copy(b.v[:, :, :], vtok[:, :, ds(i * P, P)]).then_inc(s.copied, 1)

        @block.tensor
        def _(pe):
            pe.wait_ge(s.copied, 3)
            for n in range(TT + 2):
                if n < TT:
                    if n >= 2:
                        pe.wait_ge(s.exped, n - 1)
                    pe.matmul(ps[:, n % 2, 0:MEM], b.q[:, n * P:(n + 1) * P], b.k[:, :], start=True, stop=True).then_inc(s.scored, 1)
                if 1 <= n <= TT:
                    m = n - 1
                    pe.wait_ge(s.scaled, m + 1)
                    if m >= 2:
                        pe.wait_ge(s.taken, m - 1)
                    for t in range(2):
                        last = pe.transpose(ps[:, 2 + m % 2, t * P:(t + 1) * P], b.p[:, m % 2, t * P:(t + 1) * P], g.ident[:, :])
                    last.then_inc(s.turned, 1)
                if n >= 2:
                    m = n - 2
                    pe.wait_ge(s.taken, m + 1)
                    for t in range(2):
                        last = pe.matmul(ps[:, 4 + m // 4, (m % 4) * P:(m % 4 + 1) * P], b.v[:, t, :], b.pt[:, m % 2, t * P:(t + 1) * P],
                                         start=t == 0, stop=t == 1)
                    last.then_inc(s.valued, 1)

        @block.vector
        def _(dve):
            link = linker(dve, s.steps)
            for n in range(TT + 1):
                if n < TT:
                    dve.wait_ge(s.scored, n + 1)
                    st = b.stat[:, n % 2, :]
                    link(dve.tensor_reduce(st[:, 0:1], ps[:, n % 2, 0:MEM], AX.X, ALU.max))
                    dve.tensor_scalar(st[:, 1:2], st[:, 0:1], -scale, None, ALU.mult).then_inc(s.shift, 1)
                if n:
                    m = n - 1
                    dve.wait_ge(s.exped, m + 1)
                    st = b.stat[:, m % 2, :]
                    link(dve.reciprocal(st[:, 3:4], st[:, 2:3]))
                    dve.tensor_scalar(b.p[:, m % 2, :], b.p[:, m % 2, :], st[:, 3:4], None, ALU.mult).then_inc(s.scaled, 1)

        @block.scalar
        def _(act):
            for n in range(TT + 1):
                if n < TT:
                    act.wait_ge(s.shift, n + 1)
                    if n >= 2:
                        act.wait_ge(s.turned, n - 1)
                    st = b.stat[:, n % 2, :]
                    act.activation(b.p[:, n % 2, :], ps[:, n % 2, 0:MEM], ACT.Exp, scale=scale, bias=st[:, 1:2],
                                   accum_out=st[:, 2:3]).then_inc(s.exped, 1)
                if n:
                    m = n - 1
                    act.wait_ge(s.turned, m + 1)
                    if m >= 2:
                        act.wait_ge(s.valued, m - 1)
                    act.activation(b.pt[:, m % 2, :], ps[:, 2 + m % 2, 0:MEM], ACT.Copy).then_inc(s.taken, 1)
            act.wait_ge(s.valued, TT)
            act.activation(Q[:, ds(i, 1), 0:T].rearrange("p a (n c) -> p (a n) c", n=2), ps[:, 4:6, :], ACT.Copy).then_inc(s.done, 1)


def stick_breaking(nc, g, d, ps):
    wqkv = d.w_qkv_sb[0]
    with ExitStack() as mem:
        QK = mem.enter_context(tensor(nc, "sb_qk", [P, 2 * DT, NT]))
        V = g.X[:, :, :].rearrange("p k c -> p (k c)")[:, 0:TT * D].rearrange("p (t c) -> p t c", t=TT)
        with ExitStack() as inner:
            H = parts(nc, inner, "h_sb", [P, DT, NT])
            rms_norm(nc, g, ps, H, COL["g_mix"] + DT, spill=d.spill)
            for first, scale in ((0, HD ** -0.5), (DT, 1.0)):
                keep = kept_in(lambda m, first=first: QK[:, first + m.start:first + m.stop, :] if isinstance(m, slice)
                               else QK[:, ds(first + m.start, 1), :], scale)
                project(nc, ps, tiles_of(wqkv[:, first * P:first * P + D], DT), DT, DT // 2, H, keep)
            sb_values(nc, g, d, ps, H, V)
        sb_store_keys(nc, g, d, ps, QK)
        sb_attention(nc, g, d, ps, QK, V)
        with ExitStack() as inner:
            O = parts(nc, inner, "sb_out", [P, DT, NT])
            project(nc, ps, tiles_of(d.w_out_sb[0], DT), DT, DT // 2, O, add_to_residual(g),
                    split=[QK[:, k, :] for k in range(DT)], reload=d.spill)


def sb_values(nc, g, d, ps, H, V):
    QC = 256
    with ExitStack() as mem:
        raw = mem.enter_context(tensor(nc, "v_raw", [P, DT, QC]))
        W = parts(nc, mem, "v_w", [P, DT, QC])
        v8 = mem.enter_context(tensor(nc, "sample_v_rows", [P, D]))
        wv = weight_blocks(d.w_qkv_sb[0][:, 2 * D:3 * D], DT)
        NQ = D // QC
        NG = NQ * (TT + 1)
        with phase(nc, "w_in", "w_high", "w_low", "made", "taken_act", "taken_dve", "stored") as (s, block):
            @block.sync
            def _(sp):
                for q in range(NQ):
                    if q:
                        sp.wait_ge(s.w_low, q)
                    sp.dma_start(raw[:, :, :], wv[:, :, q * QC:(q + 1) * QC]).then_inc(s.w_in, 16)
                sp.wait_ge(s.taken_act, NG // 2)
                sp.wait_ge(s.taken_dve, NG // 2)
                sp.dma_start(d.sb_v_p[0, 0].rearrange("(t p) h c -> p t (h c)", p=P), V).then_inc(s.stored, 16)
                sp.dma_start(d.sb_v_s[0, :, 0].rearrange("b h c -> b (h c)"), v8[P - NS:P, :]).then_inc(s.stored, 16)
                sp.wait_ge(s.stored, 32)

            @block.gpsimd
            def _(pool):
                for q in range(NQ):
                    pool.wait_ge(s.w_high, q + 1)
                    pool.tensor_tensor(W.lo[:, :, :], raw[:, :, :], W.hi[:, :, :].bitcast(F32), ALU.subtract).then_inc(s.w_low, 1)

            @block.tensor
            def _(pe):
                for n in range(NG):
                    q, t = divmod(n, TT + 1)
                    c = t * P if t < TT else NT - P
                    if t == 0:
                        pe.wait_ge(s.w_low, q + 1)
                    if n >= 8:
                        pe.wait_ge(s.taken_dve if n % 2 else s.taken_act, (n - 8) // 2 + 1)
                    for k in range(DT):
                        for m, (xp, wp) in enumerate(((H.hi, W.hi), (H.lo, W.hi), (H.hi, W.lo))):
                            last = pe.matmul(ps[:, n % 8, 0:QC], xp[:, k, c:c + P], wp[:, k, :],
                                             start=k == 0 and m == 0, stop=k == DT - 1 and m == 2)
                    last.then_inc(s.made, 1)

            def place(n):
                q, t = divmod(n, TT + 1)
                cols = slice(q * QC, (q + 1) * QC)
                return (V[:, t, cols], ps[:, n % 8, 0:QC]) if t < TT else (v8[96:P, cols], ps[96:P, n % 8, 0:QC])

            @block.scalar
            def _(act):
                for q in range(NQ):
                    act.wait_ge(s.w_in, 16 * (q + 1))
                    if q:
                        act.wait_ge(s.made, q * (TT + 1))
                    act.activation(W.hi[:, :, :], raw[:, :, :], ACT.Copy).then_inc(s.w_high, 1)
                    for n in range(q * (TT + 1), (q + 1) * (TT + 1)):
                        if n % 2 == 0:
                            act.wait_ge(s.made, n + 1)
                            act.activation(*place(n), ACT.Copy).then_inc(s.taken_act, 1)

            @block.vector
            def _(dve):
                for n in range(1, NG, 2):
                    dve.wait_ge(s.made, n + 1)
                    dve.tensor_copy(*place(n)).then_inc(s.taken_dve, 1)


def sb_store_keys(nc, g, d, ps, QK):
    with ExitStack() as mem:
        rows = mem.enter_context(tensor(nc, "k_rows", [P, TT + 1, D]))
        turn_rows(nc, g, ps, lambda k: QK[:, DT + k, :], rows, d.sb_k_p[0, 0].rearrange("t h c -> t (h c)"),
                  d.sb_k_s[0, :, 0].rearrange("b h c -> b (h c)"))


def sb_attention(nc, g, d, ps, QK, V):
    with ExitStack() as mem:
        def sb(name, shape):
            return mem.enter_context(tensor(nc, name, shape))

        b = record(
            q=sb("pair_q", [P, T]), k=sb("pair_k", [P, T]), v=sb("pair_v", [P, TT, P]), bias=sb("pair_bias", [P, 2]),
            A=sb("logits", [P, 2, 2, 512]), B=sb("softplus", [P, 2, 2, 512]),
            kring=sb("k_ring", [P, KR, D]), vring=sb("v_ring", [P, VR, D]), prod=sb("products", [P, D]),
            Z=sb("cache_logits", [P, 512]), L=sb("cache_softplus", [P, 512]), tot=sb("page_totals", [P, 512]),
            att=sb("cache_weights", [P, 512]), kept=sb("page_kept", [P, 512]), qcol=sb("q_column", [P, DT]))
        with phase(nc, "made") as (s, block):
            @block.gpsimd
            def _(pool):
                link = linker(pool, s.made)
                link(pool.memset(b.kept[:, :], 1.0))
                link(pool.memset(b.kept[:, 0:512:PAGES], 0.0))
        sb_turn(nc, g, d, ps, QK, V, b, 0, prompt=False, values=False, keys=True)
        with nc.Fori(0, NS - 1) as i:
            sb_turn(nc, g, d, ps, QK, V, b, i, prompt=True, values=True, keys=True)
        sb_turn(nc, g, d, ps, QK, V, b, NS - 1, prompt=True, values=True, keys=False)


KR = 3
VR = 3
SB_STEPS = [(1, st) for st in range(7, -1, -1)] + [(0, st) for st in range(3, -1, -1)]


def sb_turn(nc, g, d, ps, QK, V, b, i, prompt, values, keys):
    steps = SB_STEPS if prompt else []
    two = (0, 1)
    b_next = i if not values else i + 1

    def span(n):
        tq, st = steps[n]
        return slice(max(0, P * st - 512 * tq), 512)

    def diagonal(n):
        tq, st = steps[n]
        return P * st >= 512 * tq

    def first(n):
        return n == 0 or steps[n][0] != steps[n - 1][0]

    def last_of(n):
        return n == len(steps) - 1 or steps[n][0] != steps[n + 1][0]

    with phase(nc, "copied", "z", "z_added", "capped", "exped", "logged", "soft", "summed", "arg", "weight", "rested",
               "out_done", "out_taken", ("k_in", KR), ("v_in", VR), "k_used", "v_used", "dve", "q_diag", "spread",
               "cz", "cexp", "clog", "csoft", "ctri", "ctot", "carg", "catt", "pv_taken", "act_steps",
               "pool_steps") as (s, block):

        @block.sync
        def _(sp):
            for p in range(PAGES):
                if keys:
                    page = sp.value_load(b_pages(g, b_next, p), min_val=0, max_val=d.cache_sb_k.shape[1] - 1)
                    if p >= KR:
                        sp.wait_ge(s.k_used, p - KR + 1)
                    sp.dma_start(b.kring[:, p % KR, :], d.cache_sb_k[0, ds(page, 1), :, :, :].rearrange("a p h c -> p (a h c)")).then_inc(s.k_in[p % KR], 16)
                if values:
                    page = sp.value_load(b_pages(g, i, p), min_val=0, max_val=d.cache_sb_v.shape[1] - 1)
                    if p >= VR:
                        sp.wait_ge(s.v_used, p - VR + 1)
                    sp.dma_start(b.vring[:, p % VR, :], d.cache_sb_v[0, ds(page, 1), :, :, :].rearrange("a p h c -> p (a h c)")).then_inc(s.v_in[p % VR], 16)

        @block.gpsimd
        def _(pool):
            if keys:
                pool.tensor_copy(b.qcol[:, :], QK[:, 0:DT, ds(b_next + T, 1)].rearrange("p k a -> p (k a)")).then_inc(s.pool_steps, 1)
                pool.wait_ge(s.pool_steps, 1)
                pool.tensor_tensor(b.prod[:, :].rearrange("p (k c) -> p k c", c=P), g.ident[:, :].unsqueeze(1).to_broadcast([P, DT, P]),
                                   b.qcol[:, :].unsqueeze(2).to_broadcast([P, DT, P]), ALU.mult).then_inc(s.q_diag, 1)
            if prompt:
                pool.tensor_copy(b.q[:, :], QK[:, ds(i, 1), 0:T].rearrange("p a c -> p (a c)")).then_inc(s.copied, 1)
                pool.tensor_copy(b.k[:, :], QK[:, ds(i + DT, 1), 0:T].rearrange("p a c -> p (a c)")).then_inc(s.copied, 1)
                pool.tensor_copy(b.v[:, :, :], V[:, :, ds(i * P, P)]).then_inc(s.copied, 1)
                pool.tensor_copy(b.bias[:, :], g.sbb[:, ds(i * 2, 2)]).then_inc(s.copied, 1)
            for n in range(len(steps)):
                c = span(n)
                for h in two:
                    A, B = b.A[:, n % 2, h, :], b.B[:, n % 2, h, :]
                    pool.wait_ge(s.z_added, 2 * n + h + 1)
                    if n >= 2:
                        pool.wait_ge(s.rested, 2 * (n - 2) + h + 1)
                    pool.tensor_scalar(B[:, c], A[:, c], 40.0, None, ALU.min).then_inc(s.capped, 1)

        @block.vector
        def _(dve):
            link = linker(dve, s.dve)
            page = [0]

            def score_page():
                p = page[0]
                page[0] += 1
                dve.wait_ge(s.k_in[p % KR], 16 * (p // KR + 1))
                link(dve.tensor_tensor(b.prod[:, :].rearrange("p (a c) -> p a c", a=2), b.kring[:, p % KR, :].rearrange("p (a c) -> p a c", a=2),
                                       ps[:, 6:8, :], ALU.mult))
                dve.sem_inc(s.k_used, 1)
                link(dve.tensor_reduce(b.Z[:, PAGES - 1 - p:512:PAGES], b.prod[:, :].rearrange("p (h c) -> p h c", c=HD), AX.X, ALU.add))

            if prompt:
                dve.wait_ge(s.copied, 4)
            if keys:
                dve.wait_ge(s.spread, 1)
            for n in range(len(steps) + 1):
                if n < len(steps):
                    c = span(n)
                    for h in two:
                        dve.wait_ge(s.z, 2 * n + h + 1)
                        if n >= 2:
                            dve.wait_ge(s.out_done, 2 * (n - 2) + h + 1)
                        dve.tensor_scalar(b.A[:, n % 2, h, c], ps[:, h, c], b.bias[:, h:h + 1], None, ALU.add).then_inc(s.z_added, 1)
                if keys and n < len(steps):
                    for _ in range(2 if n % 3 else 3):
                        score_page()
                if n < len(steps):
                    for h in two:
                        A, B = b.A[:, n % 2, h, :], b.B[:, n % 2, h, :]
                        dve.wait_ge(s.logged, 2 * n + h + 1)
                        if diagonal(n):
                            dg = slice(c.start, c.start + P)
                            link(dve.tensor_tensor(B[:, c], B[:, c], A[:, c], ALU.max))
                            dve.tensor_tensor(B[:, dg], B[:, dg], g.rest[:, :], ALU.mult).then_inc(s.soft, 1)
                        else:
                            dve.tensor_tensor(B[:, c], B[:, c], A[:, c], ALU.max).then_inc(s.soft, 1)
                    for h in two:
                        A = b.A[:, n % 2, h, :]
                        dve.wait_ge(s.summed, 2 * n + h + 1)
                        if diagonal(n):
                            dg = slice(c.start, c.start + P)
                            link(dve.tensor_tensor(A[:, c], A[:, c], ps[:, 2 + h, c], ALU.subtract))
                            dve.tensor_tensor(A[:, dg], A[:, dg], g.blocked[:, :], ALU.add).then_inc(s.arg, 1)
                        else:
                            dve.tensor_tensor(A[:, c], A[:, c], ps[:, 2 + h, c], ALU.subtract).then_inc(s.arg, 1)
            while keys and page[0] < PAGES:
                score_page()
            if values:
                dve.wait_ge(s.v_used, PAGES)
                for o in two:
                    dve.tensor_copy(QK[64 * o:64 * o + 64, 0:DT, ds(i + T, 1)], ps[64 * o:64 * o + 64, 5, o:2 * DT:2].unsqueeze(2)).then_inc(s.pv_taken, 1)
            if keys:
                Zh = b.Z[:, :].rearrange("p (h n) -> p h n", n=PAGES)
                link(dve.tensor_tensor(Zh, Zh, g.sbb[:, :].unsqueeze(2).to_broadcast([P, SBH, PAGES]), ALU.add))
                dve.tensor_scalar(b.L[:, :], b.Z[:, :], 40.0, None, ALU.min).then_inc(s.cz, 1)
                dve.wait_ge(s.clog, 1)
                dve.tensor_tensor(b.L[:, :], b.L[:, :], b.Z[:, :], ALU.max).then_inc(s.csoft, 1)
                dve.wait_ge(s.ctri, 1)
                link(dve.tensor_tensor(b.Z[:, :], b.Z[:, :], ps[:, 6, :], ALU.subtract))
                dve.wait_ge(s.ctot, 1)
                link(dve.tensor_tensor(b.Z[:, :], b.Z[:, :], b.tot[:, :], ALU.add))
                link(dve.tensor_tensor_scan(b.L[:, :], b.kept[:, :], b.tot[:, :], 0.0, ALU.mult, ALU.add))
                dve.tensor_tensor(b.Z[:, :], b.Z[:, :], b.L[:, :], ALU.subtract).then_inc(s.carg, 1)

        @block.scalar
        def _(act):
            for n in range(len(steps)):
                c = span(n)
                for h in two:
                    B = b.B[:, n % 2, h, :]
                    act.wait_ge(s.capped, 2 * n + h + 1)
                    act.activation(B[:, c], B[:, c], ACT.Exp).then_inc(s.exped, 1)
                for h in two:
                    B = b.B[:, n % 2, h, :]
                    act.wait_ge(s.exped, 2 * n + h + 1)
                    act.activation(B[:, c], B[:, c], ACT.Ln, bias=g.ones[:, 0:1]).then_inc(s.logged, 1)
                for h in two:
                    A = b.A[:, n % 2, h, :]
                    act.wait_ge(s.arg, 2 * n + h + 1)
                    act.activation(A[:, c], A[:, c], ACT.Exp).then_inc(s.weight, 1)
                if last_of(n):
                    act.wait_ge(s.out_done, 2 * n + 2)
                    tq = steps[n][0]
                    act.activation(QK[:, ds(i, 1), 512 * tq:512 * tq + 512].rearrange("p a c -> p (a c)"), ps[:, 4, :], ACT.Copy).then_inc(s.out_taken, 1)
            if keys:
                act.wait_ge(s.cz, 1)
                act.activation(b.L[:, :], b.L[:, :], ACT.Exp).then_inc(s.cexp, 1)
                act.wait_ge(s.cexp, 1)
                act.activation(b.L[:, :], b.L[:, :], ACT.Ln, bias=g.ones[:, 0:1]).then_inc(s.clog, 1)
                act.wait_ge(s.ctri, 2)
                act.activation(b.tot[:, :], ps[:, 7, :], ACT.Copy).then_inc(s.ctot, 1)
                act.wait_ge(s.carg, 1)
                if values:
                    act.wait_ge(s.v_used, PAGES)
                act.activation(b.att[:, :], b.Z[:, :], ACT.Exp).then_inc(s.catt, 1)

        @block.tensor
        def _(pe):
            page = [0]

            def value_page():
                p = page[0]
                page[0] += 1
                pe.wait_ge(s.v_in[p % VR], 16 * (p // VR + 1))
                for k in range(DT):
                    at = b.att[:, :].rearrange("p (h n) -> p n h", n=PAGES)[:, PAGES - 1 - p, 2 * k:2 * k + 2]
                    last = pe.matmul(ps[:, 5, 2 * k:2 * k + 2], b.vring[:, p % VR, k * P:(k + 1) * P], at,
                                     start=p == 0 and k == 0, stop=p == PAGES - 1, skip_group_check=True)
                last.then_inc(s.v_used, 1)
                return last

            def logits(n, h):
                tq, st = steps[n]
                c = span(n)
                r = slice(64 * h, 64 * h + 64)
                if n:
                    pe.wait_ge(s.z_added, 2 * (n - 1) + h + 1)
                pe.matmul(ps[:, h, c], b.k[r, st * P:(st + 1) * P], b.q[r, 512 * tq + c.start:512 * tq + 512],
                          start=True, stop=True).then_inc(s.z, 1)

            if keys:
                pe.wait_ge(s.q_diag, 1)
                for n in two:
                    last = pe.matmul(ps[:, 6 + n, :], g.ones[:, :], b.prod[:, n * 512:(n + 1) * 512], start=True, stop=True)
                last.then_inc(s.spread, 1)
            if prompt:
                pe.wait_ge(s.copied, 3)
                for h in two:
                    logits(0, h)
            for n in range(len(steps)):
                tq, st = steps[n]
                c = span(n)
                for h in two:
                    pe.wait_ge(s.soft, 2 * n + h + 1)
                    pe.matmul(ps[:, 2 + h, c], g.tail[:, :], b.B[:, n % 2, h, c], start=first(n), stop=last_of(n),
                              skip_group_check=True).then_inc(s.summed, 1)
                if n + 1 < len(steps):
                    for h in two:
                        logits(n + 1, h)
                if values:
                    for _ in range(2 if n % 3 else 3):
                        value_page()
                for h in two:
                    pe.wait_ge(s.arg, 2 * n + h + 1)
                    pe.matmul(ps[:, 2 + h, c], g.rest[:, :], b.B[:, n % 2, h, c], start=False, stop=last_of(n),
                              skip_group_check=True).then_inc(s.rested, 1)
                if first(n) and n:
                    pe.wait_ge(s.out_taken, 1)
                for h in two:
                    pe.wait_ge(s.weight, 2 * n + h + 1)
                    pe.matmul(ps[64 * h:64 * h + 64, 4, c], b.v[:, st, 64 * h:64 * h + 64], b.A[:, n % 2, h, c],
                              start=first(n), stop=last_of(n), skip_group_check=True).then_inc(s.out_done, 1)
            if values:
                while page[0] < PAGES:
                    value_page()
            if keys:
                pe.wait_ge(s.csoft, 1)
                for n, m in enumerate((g.tail, g.ones)):
                    pe.matmul(ps[:, 6 + n, :], m[:, :], b.L[:, :], start=True, stop=True).then_inc(s.ctri, 1)


def b_pages(g, b, p):
    at = b * PAGES + p
    return g.pages[0:1, at:at + 1] if isinstance(at, int) else g.pages[0:1, ds(at, 1)]


def store_outputs(nc, g, d, ps):
    with ExitStack() as mem:
        rows = mem.enter_context(tensor(nc, "y_rows", [P, TT + 1, D]))
        turn_rows(nc, g, ps, lambda k: g.X[:, k, :], rows, d.y_prompt[0], d.y_sample[:, 0, :])


def turn_rows(nc, g, ps, tile, out, to_prompt, to_samples):
    with phase(nc, "turned", "taken_act", "taken_dve", "stored") as (s, block):
        NG = 2 * (TT + 1)

        @block.tensor
        def _(pe):
            for n in range(NG):
                t, half = n // 2, n % 2
                w = P if t < TT else NS
                if n >= 8:
                    pe.wait_ge(s.taken_dve if half else s.taken_act, (n - 8) // 2 + 1)
                for k in range(4):
                    last = pe.transpose(ps[0:w, n % 8, k * P:(k + 1) * P], tile(4 * half + k)[:, t * P:t * P + w],
                                        g.ident[:, :])
                last.then_inc(s.turned, 1)

        @block.scalar
        def _(act):
            for n in range(0, NG, 2):
                w = P if n // 2 < TT else NS
                act.wait_ge(s.turned, n + 1)
                act.activation(out[0:w, n // 2, 0:512], ps[0:w, n % 8, :], ACT.Copy).then_inc(s.taken_act, 1)

        @block.vector
        def _(dve):
            for n in range(1, NG, 2):
                w = P if n // 2 < TT else NS
                dve.wait_ge(s.turned, n + 1)
                dve.tensor_copy(out[0:w, n // 2, 512:1024], ps[0:w, n % 8, :]).then_inc(s.taken_dve, 1)

        @block.sync
        def _(sp):
            for t in range(TT + 1):
                sp.wait_ge(s.taken_act, t + 1)
                sp.wait_ge(s.taken_dve, t + 1)
                if t < TT:
                    sp.dma_start(to_prompt[t * P:(t + 1) * P, :], out[:, t, :]).then_inc(s.stored, 16)
                else:
                    sp.dma_start(to_samples, out[0:NS, t, :]).then_inc(s.stored, 16)
            sp.wait_ge(s.stored, 16 * (TT + 1))


def program(nc, d):
    ctx = ExitStack()
    probe = ctx.enter_context(nc.semaphore("first"))
    FIRST_SEM[0] = probe.num
    with ctx:
        def sb(name, shape, dt=F32):
            return ctx.enter_context(tensor(nc, name, shape, dt))

        g = record(
            X=sb("residual", [P, DT, NT]), ones=sb("ones", [P, P]), ident=sb("ident", [P, P]),
            blockones=sb("blockones", [P, P]), ident2=sb("ident2", [P, 64]), tail=sb("tail", [P, P]),
            rest=sb("rest", [P, P]), blocked=sb("blocked", [P, P]), epsc=sb("eps", [P, 2]), par=sb("params", [P, 2 * P]),
            shift0=sb("shift0", [P, RWC_T, NS]), conv0=sb("conv0", [P, LRU_T, 24]), h0=sb("h0", [P, LRU_T, NS]),
            kn=sb("kn", [P, 2, P]), sbb=sb("sb_bias", [P, SBH]), pages=sb("pages", [1, NS * PAGES], I32))
        ps = ctx.enter_context(nc.psum_tensor("ps", [P, 8, 512], F32))
        constants(nc, g)
        load_inputs(nc, g, d, ps)
        layer0_mixer(nc, g, d, ps)
        memory_attention(nc, g, d, ps, 0)
        ffn(nc, g, d, ps, 0)
        stick_breaking(nc, g, d, ps)
        memory_attention(nc, g, d, ps, 1)
        ffn(nc, g, d, ps, 1)
        store_outputs(nc, g, d, ps)


OUTS = [("y_prompt", (1, T, D)), ("y_sample", (NS, 1, D)), ("wkv_p", (1, 1, 8, HD, HD)), ("wkv_s", (1, NS, 8, HD, HD)),
        ("shift_p", (1, 1, RW_COLS)), ("shift_s", (1, NS, RW_COLS)), ("lru_h_p", (1, 1, RW)), ("lru_h_s", (1, NS, RW)),
        ("lru_conv_p", (1, 1, 3, RW)), ("lru_conv_s", (1, NS, 3, RW)), ("sb_k_p", (1, 1, T, SBH, HD)),
        ("sb_k_s", (1, NS, 1, SBH, HD)), ("sb_v_p", (1, 1, T, SBH, HD)), ("sb_v_s", (1, NS, 1, SBH, HD)),
        ("mem_k_p", (2, 1, MEM, MH, P)), ("mem_v_p", (2, 1, MEM, MH, P))]


def kernel(**inputs):
    import numpy as _np
    import concourse.bacc as _bacc
    from concourse.bass_utils import run_bass_kernel_spmd as _run

    nc = _bacc.Bacc("TRN2", target_bir_lowering=False, num_devices=1)
    arrays, aps = {}, {}
    for name, value in inputs.items():
        a = _np.ascontiguousarray(value)
        arrays[f"in_{name}"] = a
        aps[name] = nc.dram_tensor(f"in_{name}", a.shape, mybir.dt.from_np(a.dtype), kind="ExternalInput").ap()
    for name, shape in OUTS:
        aps[name] = nc.dram_tensor(f"out_{name}", shape, F32, kind="ExternalOutput").ap()
    aps["spill"] = nc.dram_tensor("residual_spill", (P, DT, NT), F32, kind="Internal").ap()
    program(nc, record(rows=aps, **aps))
    r = _run(nc, [arrays], core_ids=[0])
    return tuple(r.results[0][f"out_{name}"] for name, _ in OUTS)
```

```python
from contextlib import ExitStack, contextmanager
from collections import namedtuple

import numpy as np
import concourse.bass as bass
from concourse import mybir

F32 = mybir.dt.float32
F32R = mybir.dt.float32r
I32 = mybir.dt.int32
ALU = mybir.AluOpType
ACT = mybir.ActivationFunctionType
AX = mybir.AxisListType
ds = bass.DynSlice

P = 128
D = 1024
DT = D // P
T = 1024
TT = T // P
NS = 8
NT = T + NS
N4 = NT // 4
N3 = NT // 3
PAD = 4
RW = 512
RWT = RW // P
RW_COLS = 1792
RWC_T = RW_COLS // P
LRU_T = 4
AB_T = 22
AB_COLS = AB_T * P
FF = 2816
FF_T = FF // P
FF_PARTS = [(0, 8), (8, 8), (16, 6)]
HD = 64
C = 64
NC = T // C
MEM = 256
MH = 4
SBH = 16
PAGES = 32
EPS = 1e-6
LN_EPS = HD * 1e-5
DECAY = -float(np.exp(-0.5))

ROWS_A = [("mu_shift", 14), ("rw_w0", 4), ("rw_a0", 4), ("rw_kk", 4), ("rw_ka", 4), ("rw_rk", 4),
          ("rw_lnx_w", 4), ("rw_lnx_b", 4), ("lru_conv_w", 16), ("lru_conv_b", 4), ("lru_ba", 4),
          ("lru_bx", 4), ("lru_lambda", 4)]
ROWS_B = [("g_mix", 16), ("g_mem", 16), ("g_memkv", 16), ("g_ffn", 16), ("qn_mem", 2)]
COL = {}
for _base, _rows in ((0, ROWS_A), (P, ROWS_B)):
    for _name, _n in _rows:
        COL[_name] = _base
        _base += _n
NA = sum(n for _, n in ROWS_A)
NB = sum(n for _, n in ROWS_B)
FIRST_SEM = [0]


def record(**fields):
    return namedtuple("Record", list(fields))(**fields)


TENSORS = [0]


def tensor(nc, name, shape, dt=F32):
    TENSORS[0] += 1
    return nc.sbuf_tensor(f"{name}_{TENSORS[0]}", shape, dt)


@contextmanager
def phase(nc, *names):
    with ExitStack() as stack:
        sems = {}
        for name in names:
            if isinstance(name, tuple):
                sems[name[0]] = [stack.enter_context(nc.semaphore(f"{name[0]}{i}")) for i in range(name[1])]
            else:
                sems[name] = stack.enter_context(nc.semaphore(name))
        with nc.Block() as block:
            yield record(**sems), block
    nc.all_engine_barrier(sems_to_clear=range(FIRST_SEM[0], 256))


def linker(eng, sem):
    count = [0]

    def link(ins):
        count[0] += 1
        ins.then_inc(sem, 1)
        eng.wait_ge(sem, count[0])

    return link


def bank3(ps, first):
    return ps[:, first:first + 3, 0:N3]


def cols3(ap):
    return ap.rearrange("p (n c) -> p n c", n=3)


def cols4(ap):
    return ap.rearrange("p (n c) -> p n c", n=4)


def row_to_all(g, r):
    return g.ident[:, r:r + 1].to_broadcast([P, P])


def constants(nc, g):
    with phase(nc, "made") as (s, block):
        @block.gpsimd
        def _(pool):
            link = linker(pool, s.made)
            link(pool.memset(g.ones[:, :], 1.0))
            link(pool.memset(g.ident[:, :], 0.0))
            link(pool.affine_select(out=g.ident[:, :], in_=g.ident[:, :], compare_op=ALU.not_equal, fill=1.0,
                                    base=0, pattern=[[-1, P]], channel_multiplier=1))
            link(pool.memset(g.blockones[:, :], 0.0))
            link(pool.memset(g.blockones[0:64, 0:64], 1.0))
            link(pool.memset(g.blockones[64:128, 64:128], 1.0))
            link(pool.tensor_tensor(g.ident2[:, :], g.ident[:, 0:64], g.ident[:, 64:128], ALU.add))
            link(pool.affine_select(out=g.tail[:, :], in_=g.ones[:, :], compare_op=ALU.is_ge, fill=0.0,
                                    base=0, pattern=[[-1, P]], channel_multiplier=1))
            link(pool.tensor_tensor(g.rest[:, :], g.ones[:, :], g.tail[:, :], ALU.subtract))
            link(pool.tensor_scalar(g.blocked[:, :], g.tail[:, :], -1e30, None, ALU.mult))
            link(pool.memset(g.epsc[:, 0:1], EPS))
            link(pool.memset(g.epsc[:, 1:2], LN_EPS))


def load_inputs(nc, g, d, ps):
    NG = 2 * (TT + 1)
    with ExitStack() as mem:
        tok = mem.enter_context(tensor(nc, "tokens", [P, TT + 1, D], F32))
        rows = mem.enter_context(tensor(nc, "param_rows", [P, 2, P], F32))
        st = mem.enter_context(tensor(nc, "state_rows", [24, 3, RW_COLS], F32))
        with phase(nc, ("tok_in", TT + 1), "rows_in", "state_in", "turned", "taken_act", "taken_dve", "copied",
                   "stored") as (s, block):
            @block.sync
            def _(sp):
                for t in range(TT):
                    sp.dma_start(tok[:, t, :], d.x_prompt[0, t * P:(t + 1) * P, :]).then_inc(s.tok_in[t], 16)
                sp.dma_start(tok[0:NS, TT, :], d.x_sample[:, 0, :]).then_inc(s.tok_in[TT], 16)
                sp.dma_start(st[0:NS, 0, :], d.state_rwkv_shift[0]).then_inc(s.state_in, 16)
                sp.dma_start(st[0:24, 1, 0:RW], d.state_lru_conv[0].rearrange("b j c -> (b j) c")).then_inc(s.state_in, 16)
                sp.dma_start(st[0:NS, 2, 0:RW], d.state_lru_h[0]).then_inc(s.state_in, 16)
                sp.dma_start(d.lru_conv_s[0, :, 0:2, :], d.state_lru_conv[0, :, 1:3, :]).then_inc(s.stored, 16)
                sp.dma_start(g.kn[:, :, :], d.kn_mem.unsqueeze(0).to_broadcast([P, 2, P])).then_inc(s.stored, 16)
                sp.dma_start(g.sbb[:, :], d.sb_bias.to_broadcast([P, SBH])).then_inc(s.stored, 16)
                sp.dma_start(g.pages[:, :], d.page_table.rearrange("b n -> (b n)").unsqueeze(0)).then_inc(s.stored, 16)
                sp.wait_ge(s.stored, 64)

            @block.scalar
            def _(act):
                for group, names in enumerate((ROWS_A, ROWS_B)):
                    r = 0
                    for name, n in names:
                        src = d.rows[name].flatten().rearrange("(r c) -> r c", c=P)
                        act.dma_start(rows[r:r + n, group, :], src).then_inc(s.rows_in, 16)
                        r += n
                for n in range(0, NG, 2):
                    t = n // 2
                    w = P if t < TT else NS
                    act.wait_ge(s.turned, n + 1)
                    act.activation(g.X[:, 0:4, t * P:t * P + w],
                                   ps[:, n % 8, :].rearrange("p (k c) -> p k c", k=4)[:, :, 0:w],
                                   ACT.Copy).then_inc(s.taken_act, 1)

            @block.vector
            def _(dve):
                for n in range(1, NG, 2):
                    t = n // 2
                    w = P if t < TT else NS
                    dve.wait_ge(s.turned, n + 1)
                    dve.tensor_copy(g.X[:, 4:8, t * P:t * P + w],
                                    ps[:, n % 8, :].rearrange("p (k c) -> p k c", k=4)[:, :, 0:w]).then_inc(s.taken_dve, 1)
                dve.wait_ge(s.turned, NG + 1)
                dve.tensor_copy(g.par[:, 0:NA], ps[:, NG % 8, 0:NA]).then_inc(s.copied, 1)
                dve.tensor_copy(g.par[:, P:P + NB], ps[:, NG % 8, P:P + NB]).then_inc(s.copied, 1)
                dve.wait_ge(s.turned, NG + 2)
                dve.tensor_copy(g.shift0[:, :, :], ps[:, (NG + 1) % 8, 0:RWC_T * NS]
                                .rearrange("p (k b) -> p k b", b=NS)).then_inc(s.copied, 1)
                dve.tensor_copy(g.conv0[:, :, :], ps[:, (NG + 1) % 8, 128:128 + 96]
                                .rearrange("p (k b) -> p k b", b=24)).then_inc(s.copied, 1)
                dve.tensor_copy(g.h0[:, :, :], ps[:, (NG + 1) % 8, 256:256 + 32]
                                .rearrange("p (k b) -> p k b", b=NS)).then_inc(s.copied, 1)

            @block.tensor
            def _(pe):
                for n in range(NG):
                    t, half = n // 2, n % 2
                    w = P if t < TT else NS
                    if half == 0:
                        pe.wait_ge(s.tok_in[t], 16)
                    if n >= 8:
                        pe.wait_ge(s.taken_dve if half else s.taken_act, (n - 8) // 2 + 1)
                    for k in range(4):
                        kk = 4 * half + k
                        last = pe.transpose(ps[:, n % 8, k * P:k * P + w], tok[0:w, t, kk * P:(kk + 1) * P],
                                            g.ident[0:w, 0:w])
                    last.then_inc(s.turned, 1)
                pe.wait_ge(s.rows_in, 16 * (len(ROWS_A) + len(ROWS_B)))
                pe.wait_ge(s.taken_act, (NG - 8) // 2 + 1)
                pe.transpose(ps[:, NG % 8, 0:NA], rows[0:NA, 0, :], g.ident[0:NA, 0:NA])
                pe.transpose(ps[:, NG % 8, P:P + NB], rows[0:NB, 1, :], g.ident[0:NB, 0:NB]).then_inc(s.turned, 1)
                pe.wait_ge(s.state_in, 48)
                pe.wait_ge(s.taken_dve, (NG - 8) // 2 + 1)
                b = (NG + 1) % 8
                for k in range(RWC_T):
                    pe.transpose(ps[:, b, k * NS:(k + 1) * NS], st[0:NS, 0, k * P:(k + 1) * P], g.ident[0:NS, 0:NS])
                for k in range(LRU_T):
                    pe.transpose(ps[:, b, 128 + k * 24:152 + k * 24], st[0:24, 1, k * P:(k + 1) * P], g.ident[0:24, 0:24])
                for k in range(LRU_T):
                    last = pe.transpose(ps[:, b, 256 + k * NS:264 + k * NS], st[0:NS, 2, k * P:(k + 1) * P],
                                        g.ident[0:NS, 0:NS])
                last.then_inc(s.turned, 1)


def rms_norm(nc, g, ps, H, gains, spill=None):
    with ExitStack() as mem:
        sq = mem.enter_context(tensor(nc, "squares", [P, 2, NT]))
        rms = mem.enter_context(tensor(nc, "rms", [P, N4]))
        whole = [mem.enter_context(tensor(nc, f"normed{n}", [P, NT])) for n in range(2)]
        with phase(nc, "squared", "summed", "rooted", "inverted", "spread", "scaled", "high", "low", "stored") as (s, block):
            @block.scalar
            def _(act):
                for k in range(DT):
                    if k >= 2:
                        act.wait_ge(s.summed, k - 1)
                    act.activation(sq[:, k % 2, :], g.X[:, k, :], ACT.Square).then_inc(s.squared, 1)
                act.wait_ge(s.summed, DT)
                act.activation(rms[:, :], ps[:, 0, 0:N4], ACT.Sqrt, scale=1.0 / D,
                               bias=g.epsc[:, 0:1]).then_inc(s.rooted, 1)
                for k in range(DT):
                    act.wait_ge(s.scaled, k + 1)
                    act.activation(H.hi[:, k, :], whole[k % 2][:, :], ACT.Copy).then_inc(s.high, 1)

            @block.tensor
            def _(pe):
                for k in range(DT):
                    pe.wait_ge(s.squared, k + 1)
                    for n in range(4):
                        last = pe.matmul(ps[32 * n:32 * n + 32, 0, 0:N4], g.ones[:, 0:32], sq[:, k % 2, n * N4:(n + 1) * N4],
                                         start=k == 0, stop=k == DT - 1, skip_group_check=True)
                    last.then_inc(s.summed, 1)
                pe.wait_ge(s.inverted, 1)
                for n in range(4):
                    last = pe.matmul(ps[:, 1 + n, 0:N4], row_to_all(g, 32 * n), rms[:, :], start=True, stop=True)
                last.then_inc(s.spread, 1)

            @block.sync
            def _(sp):
                if spill is not None:
                    sp.dma_start(spill, g.X[:, :, :]).then_inc(s.stored, 16)
                    sp.wait_ge(s.stored, 16)

            @block.vector
            def _(dve):
                dve.wait_ge(s.rooted, 1)
                dve.reciprocal(rms[:, :], rms[:, :]).then_inc(s.inverted, 1)
                dve.wait_ge(s.spread, 1)
                for k in range(DT + 1):
                    if k < DT:
                        if k >= 2:
                            dve.wait_ge(s.low, k - 1)
                        dve.scalar_tensor_tensor(cols4(whole[k % 2][:, :]), cols4(g.X[:, k, :]), g.par[:, gains + k:gains + k + 1], ps[:, 1:5, 0:N4],
                                                 ALU.mult, ALU.mult).then_inc(s.scaled, 1)
                    if k:
                        dve.wait_ge(s.high, k)
                        dve.tensor_tensor(H.lo[:, k - 1, :], whole[(k - 1) % 2][:, :], H.hi[:, k - 1, :].bitcast(F32),
                                          ALU.subtract).then_inc(s.low, 1)


def parts(nc, stack, name, shape):
    return record(hi=stack.enter_context(tensor(nc, name + "_hi", shape, F32R)),
                  lo=stack.enter_context(tensor(nc, name + "_lo", shape, F32R)))


def weight_blocks(w, kt):
    return w.rearrange("(k p) m -> p k m", p=P, k=kt)


def project(nc, ps, source, kt, pairs, x, takes, split=None, reload=None):
    with ExitStack() as mem:
        raw = [mem.enter_context(tensor(nc, f"w_raw{h}", [P, kt, P])) for h in range(2)]
        W = [parts(nc, mem, f"w{h}", [P, kt, P]) for h in range(2)]
        with phase(nc, ("w_in", 2), "w_high", "w_low", "product", ("free_banks", 2), "x_high", "x_low", "x_back",
                   "hid_raw", "hid_high", "hid_low", "side_used") as (s, block):
            @block.sync
            def _(sp):
                for h in range(2):
                    sp.dma_start(raw[h][:, :, :], source(0, h)).then_inc(s.w_in[h], 16)
                if reload is not None:
                    sp.dma_start(takes.residual, reload).then_inc(s.x_back, 16)
                with sp.Fori(1, pairs) as i:
                    for h in range(2):
                        sp.wait_ge(s.w_low, 2 * (i - 1) + h + 1)
                        sp.dma_start(raw[h][:, :, :], source(i, h)).then_inc(s.w_in[h], 16)

            @block.tensor
            def _(pe):
                with pe.Fori(0, pairs) as i:
                    for h in range(2):
                        pe.wait_ge(s.w_low, 2 * i + h + 1)
                        pe.wait_ge(s.free_banks[h], i + 1)
                        for k in range(kt):
                            if split and h == 0:
                                pe.wait_ge(s.x_low, k + 1)
                            for m, (wp, xp) in enumerate(((W[h].hi, x.hi), (W[h].hi, x.lo), (W[h].lo, x.hi))):
                                for n in range(3):
                                    last = pe.matmul(ps[:, 3 * h + n, 0:N3], wp[:, k, :], xp[:, k, n * N3:(n + 1) * N3],
                                                     start=k == 0 and m == 0, stop=k == kt - 1 and m == 2)
                        last.then_inc(s.product, 1)

            @block.scalar
            def _(act):
                def high(i, h):
                    act.wait_ge(s.w_in[h], 16 * (i + 1))
                    act.activation(W[h].hi[:, :, :], raw[h][:, :, :], ACT.Copy).then_inc(s.w_high, 1)

                for h in range(2):
                    high(0, h)
                for k, tile in enumerate(split or []):
                    act.activation(x.hi[:, k, :], tile, ACT.Copy).then_inc(s.x_high, 1)

                def stores(i, h):
                    act.wait_ge(s.product, 2 * i + h + 1)
                    takes.scalar(act, s, i, h, bank3(ps, 3 * h))

                with act.Fori(0, pairs - 1) as i:
                    for h in range(2):
                        stores(i, h)
                        high(i + 1, h)
                for h in range(2):
                    stores(pairs - 1, h)

            @block.gpsimd
            def _(pool):
                with pool.Fori(0, pairs) as i:
                    for h in range(2):
                        pool.wait_ge(s.w_high, 2 * i + h + 1)
                        pool.tensor_tensor(W[h].lo[:, :, :], raw[h][:, :, :], W[h].hi[:, :, :].bitcast(F32), ALU.subtract).then_inc(s.w_low, 1)

            @block.vector
            def _(dve):
                for h in range(2):
                    dve.sem_inc(s.free_banks[h], 1)
                for k, tile in enumerate(split or []):
                    dve.wait_ge(s.x_high, k + 1)
                    dve.tensor_tensor(x.lo[:, k, :], tile, x.hi[:, k, :].bitcast(F32), ALU.subtract).then_inc(s.x_low, 1)
                takes.vector_start(dve, s)
                if reload is not None:
                    dve.wait_ge(s.x_back, 16)
                with dve.Fori(0, pairs) as i:
                    for h in range(2):
                        takes.vector(dve, s, i, h, bank3(ps, 3 * h))


def nothing(*_):
    return None


def tiles_of(w, kt):
    wv = weight_blocks(w, kt)
    return lambda i, h: wv[:, :, (2 * i + h) * P:(2 * i + h + 1) * P] if isinstance(i, int) else wv[:, :, ds((2 * i + h) * P, P)]


def at(m):
    return slice(m, m + 1) if isinstance(m, int) else ds(m, 1)


def kept_in(dst, scale=1.0):
    def take(act, s, i, h, banks):
        act.activation(dst(at(2 * i + h)).rearrange("p a (n c) -> p (a n) c", n=3), banks, ACT.Copy, scale=scale).then_inc(s.free_banks[h], 1)
    return record(scalar=take, vector=nothing, vector_start=nothing)


def add_to_residual(g):
    def take(dve, s, i, h, banks):
        dve.wait_ge(s.product, 2 * i + h + 1)
        x = g.X[:, ds(2 * i + h, 1), :].rearrange("p a (n c) -> p (a n) c", n=3)
        dve.tensor_tensor(x, banks, x, ALU.add).then_inc(s.free_banks[h], 1)
    return record(scalar=nothing, vector=take, vector_start=nothing, residual=g.X[:, :, :])


def ffn(nc, g, d, ps, layer):
    wg, wu = (weight_blocks(w[layer], DT) for w in (d.w_ffn_gate, d.w_ffn_up))
    with ExitStack() as mem:
        H = parts(nc, mem, "h_ffn", [P, DT, NT])
        rms_norm(nc, g, ps, H, COL["g_ffn"] + layer * DT)
        for first, count in FF_PARTS:
            with ExitStack() as inner:
                hid = parts(nc, inner, "hidden", [P, count, NT])
                with ExitStack() as temps:
                    gate = temps.enter_context(tensor(nc, "silu", [P, NT]))
                    whole = temps.enter_context(tensor(nc, "hidden_whole", [P, NT]))

                    def source(i, h):
                        w = (wg, wu)[h]
                        return w[:, :, (first + i) * P:(first + i + 1) * P] if isinstance(i, int) else w[:, :, ds((first + i) * P, P)]

                    def scalar(act, s, i, h, banks):
                        if h == 0:
                            act.wait_ge(s.side_used, i + 1)
                            act.activation(cols3(gate[:, :]), banks, ACT.Silu).then_inc(s.free_banks[0], 1)
                        else:
                            act.wait_ge(s.hid_raw, i + 1)
                            act.activation(hid.hi[:, at(i), :].rearrange("p a c -> p (a c)"), whole[:, :], ACT.Copy).then_inc(s.hid_high, 1)

                    def vector(dve, s, i, h, banks):
                        if h:
                            dve.wait_ge(s.product, 2 * i + 2)
                            dve.wait_ge(s.free_banks[0], i + 2)
                            dve.wait_ge(s.hid_low, i + 1)
                            dve.tensor_tensor(cols3(whole[:, :]), banks, cols3(gate[:, :]), ALU.mult).then_inc(s.hid_raw, 1)
                            dve.wait_ge(s.hid_raw, i + 1)
                            dve.sem_inc(s.free_banks[1], 1)
                            dve.sem_inc(s.side_used, 1)
                            dve.wait_ge(s.hid_high, i + 1)
                            dve.tensor_tensor(hid.lo[:, at(i), :].rearrange("p a c -> p (a c)"), whole[:, :],
                                              hid.hi[:, at(i), :].rearrange("p a c -> p (a c)").bitcast(F32), ALU.subtract).then_inc(s.hid_low, 1)

                    def start(dve, s):
                        dve.sem_inc(s.side_used, 1)
                        dve.sem_inc(s.hid_low, 1)

                    project(nc, ps, source, DT, count, H, record(scalar=scalar, vector=vector, vector_start=start))
                project(nc, ps, tiles_of(d.w_ffn_down[layer][first * P:(first + count) * P, :], count), count, DT // 2, hid,
                        add_to_residual(g))


def layer0_mixer(nc, g, d, ps):
    with ExitStack() as mem:
        lru = mem.enter_context(tensor(nc, "lru_gate", [P, LRU_T, NT]))
        big = mem.enter_context(tensor(nc, "rwkv_rows", [P, RWC_T, PAD + NT]))
        x_flat = g.X[:, :, :].rearrange("p k c -> p (k c)")
        px = x_flat[:, 0:LRU_T * (PAD + NT)].rearrange("p (k c) -> p k c", k=LRU_T)
        with ExitStack() as inner:
            H = parts(nc, inner, "h_mix", [P, DT, NT])
            rms_norm(nc, g, ps, H, COL["g_mix"], spill=d.spill)
            w = d.w_in_ab[0]
            project(nc, ps, tiles_of(w[:, 0:RW_COLS], DT), DT, RWC_T // 2, H, kept_in(lambda m: big[:, m, PAD:PAD + NT]))
            project(nc, ps, tiles_of(w[:, RW_COLS + RW:AB_COLS], DT), DT, LRU_T // 2, H, kept_in(lambda m: lru[:, m, :]))
            project(nc, ps, tiles_of(w[:, RW_COLS:RW_COLS + RW], DT), DT, LRU_T // 2, H, kept_in(lambda m: px[:, m, PAD:PAD + NT]))
        store_shift_rows(nc, g, d, ps, big, px)
        rg_lru(nc, g, d, ps, px, lru)
        with ExitStack() as inner:
            w2a = inner.enter_context(tensor(nc, "w2_a2", [P, RW]))
            g2 = inner.enter_context(tensor(nc, "g2", [P, RW]))
            kept = inner.enter_context(tensor(nc, "chunk_starts", [P, NT]))
            masks = inner.enter_context(tensor(nc, "masks", [P, 18, C]))
            token_shift(nc, g, d, ps, big, w2a, g2, kept, masks)
            with nc.Fori(0, RWT) as pair:
                rwkv_pair(nc, g, d, ps, big, w2a, g2, kept, masks, pair)
        with ExitStack() as inner:
            mix = parts(nc, inner, "mix", [P, DT, NT])
            tiles = [big[:, k, PAD:PAD + NT] for k in range(RWT)] + [lru[:, k, :] for k in range(LRU_T)]
            project(nc, ps, tiles_of(d.w_out_ab[0], DT), DT, DT // 2, mix, add_to_residual(g), split=tiles, reload=d.spill)


def store_shift_rows(nc, g, d, ps, big, px):
    with ExitStack() as mem:
        rows = mem.enter_context(tensor(nc, "shift_rows", [16, 5, 512], F32))
        with phase(nc, "turned", "copied", "stored") as (s, block):
            @block.tensor
            def _(pe):
                last_row = PAD + T - 1
                for k in range(RWC_T):
                    last = pe.transpose(ps[0:9, k // 4, (k % 4) * P:(k % 4 + 1) * P], big[:, k, last_row:last_row + 9],
                                        g.ident[:, :])
                for k in range(LRU_T):
                    last = pe.transpose(ps[0:11, 4, k * P:(k + 1) * P], px[:, k, last_row - 2:last_row + 9],
                                        g.ident[:, :])
                last.then_inc(s.turned, 1)

            @block.scalar
            def _(act):
                act.wait_ge(s.turned, 1)
                act.activation(rows[0:9, 0:3, :], ps[0:9, 0:3, :], ACT.Copy).then_inc(s.copied, 1)
                act.activation(rows[0:9, 3, 0:256], ps[0:9, 3, 0:256], ACT.Copy).then_inc(s.copied, 1)
                act.activation(rows[0:11, 4, :], ps[0:11, 4, :], ACT.Copy).then_inc(s.copied, 1)

            @block.sync
            def _(sp):
                flat = rows[:, 0:4, :].rearrange("p a c -> p (a c)")
                sp.wait_ge(s.copied, 3)
                sp.dma_start(d.shift_p[0], flat[0:1, 0:RW_COLS]).then_inc(s.stored, 16)
                sp.dma_start(d.shift_s[0], flat[1:9, 0:RW_COLS]).then_inc(s.stored, 16)
                sp.dma_start(d.lru_conv_p[0, 0], rows[0:3, 4, :]).then_inc(s.stored, 16)
                sp.dma_start(d.lru_conv_s[0, :, 2, :], rows[3:11, 4, :]).then_inc(s.stored, 16)
                sp.wait_ge(s.stored, 64)


def rg_lru(nc, g, d, ps, px, gate):
    par, q = g.par, COL
    with ExitStack() as mem:
        xc = mem.enter_context(tensor(nc, "conv_out", [P, LRU_T, NT], F32))
        gr = mem.enter_context(tensor(nc, "gate_r", [P, LRU_T, NT], F32))
        gi = mem.enter_context(tensor(nc, "gate_i", [P, LRU_T, NT], F32))
        tmp = mem.enter_context(tensor(nc, "lru_tmp", [P, NT], F32))
        wax = mem.enter_context(tensor(nc, "lru_gates", [P, 2, LRU_T, P], F32))
        lam = mem.enter_context(tensor(nc, "lambda", [P, 6, LRU_T], F32))
        h_rows = mem.enter_context(tensor(nc, "h_rows", [9, RW], F32))
        with phase(nc, "cleared", "w_in", "padded", "steps", "lam_x", "gated", "lam_exp", "lam_sum", "lam_log", "conv", "gates_a", "gates_x", "gate_sig",
                   "log_a", "decayed", "tanhs", "under_root", "rooted", "gelus", "scanned", "turned", "rows", "stored") as (s, block):
            @block.gpsimd
            def _(pool):
                pool.memset(wax[:, :, :, :], 0.0).then_inc(s.cleared, 1)
                pool.memset(px[:, :, 0:PAD], 0.0).then_inc(s.padded, 1)

            @block.sync
            def _(sp):
                sp.wait_ge(s.cleared, 1)
                for n, w in enumerate((d.lru_wa, d.lru_wx)):
                    for o in range(2):
                        sp.dma_start(wax[64 * o:64 * o + 64, n, :, 64 * o:64 * o + 64],
                                     w[0].rearrange("(k o) i e -> o i k e", o=2)[o]).then_inc(s.w_in, 16)
                sp.wait_ge(s.rows, 1)
                sp.dma_start(d.lru_h_p[0], h_rows[0:1, :]).then_inc(s.stored, 16)
                sp.dma_start(d.lru_h_s[0], h_rows[1:9, :]).then_inc(s.stored, 16)
                sp.wait_ge(s.stored, 32)

            @block.vector
            def _(dve):
                link = linker(dve, s.steps)
                lq = q["lru_lambda"]
                dve.tensor_scalar(lam[:, 5, :], par[:, lq:lq + 4], -1.0, 40.0, ALU.mult, ALU.min).then_inc(s.lam_x, 1)
                dve.wait_ge(s.lam_exp, 1)
                dve.tensor_scalar(lam[:, 1, :], lam[:, 0, :], 1.0, None, ALU.add).then_inc(s.lam_sum, 1)
                dve.wait_ge(s.lam_log, 1)
                link(dve.tensor_scalar(lam[:, 3, :], lam[:, 1, :], 1.0, 1e-30, ALU.subtract, ALU.max))
                link(dve.reciprocal(lam[:, 4, :], lam[:, 3, :]))
                link(dve.tensor_tensor(lam[:, 3, :], lam[:, 0, :], lam[:, 4, :], ALU.mult))
                link(dve.tensor_tensor(lam[:, 4, :], lam[:, 2, :], lam[:, 3, :], ALU.mult))
                link(dve.scalar_tensor_tensor(lam[:, 4, :], lam[:, 0, :], 2.0 ** -24, lam[:, 4, :], ALU.min, ALU.max))
                link(dve.scalar_tensor_tensor(lam[:, 4, :], par[:, lq:lq + 4], -1.0, lam[:, 4, :], ALU.mult, ALU.max))
                link(dve.tensor_scalar(lam[:, 4, :], lam[:, 4, :], -8.0, None, ALU.mult))
                dve.wait_ge(s.padded, 1)
                cw, cb = q["lru_conv_w"], q["lru_conv_b"]
                c0 = g.conv0[:, :, :].rearrange("p k (b j) -> p k j b", j=3)
                for k in range(LRU_T):
                    w = [par[:, cw + 4 * j + k:cw + 4 * j + k + 1] for j in range(4)]
                    link(dve.tensor_scalar(xc[:, k, 0:T], px[:, k, 1:1 + T], w[0], par[:, cb + k:cb + k + 1], ALU.mult, ALU.add))
                    link(dve.tensor_scalar(xc[:, k, T:NT], c0[:, k, 0, :], w[0], par[:, cb + k:cb + k + 1], ALU.mult, ALU.add))
                    for j in range(1, 4):
                        link(dve.scalar_tensor_tensor(xc[:, k, 0:T], px[:, k, 1 + j:1 + j + T], w[j], xc[:, k, 0:T], ALU.mult, ALU.add))
                        old = c0[:, k, j, :] if j < 3 else px[:, k, PAD + T:PAD + NT]
                        link(dve.scalar_tensor_tensor(xc[:, k, T:NT], old, w[j], xc[:, k, T:NT], ALU.mult, ALU.add))
                    dve.sem_inc(s.conv, 1)
                for k in range(LRU_T):
                    dve.wait_ge(s.gate_sig, 2 * k + 2)
                    dve.tensor_scalar(gr[:, k, :], gr[:, k, :], lam[:, 4, k:k + 1], None, ALU.mult).then_inc(s.log_a, 1)
                    dve.tensor_tensor(gi[:, k, :], gi[:, k, :], xc[:, k, :], ALU.mult).then_inc(s.gated, 1)
                for k in range(LRU_T):
                    dve.wait_ge(s.tanhs, k + 1)
                    link(dve.tensor_scalar(tmp[:, :], gr[:, k, :], 1.0, None, ALU.add))
                    link(dve.reciprocal(tmp[:, :], tmp[:, :]))
                    dve.scalar_tensor_tensor(gr[:, k, :], gr[:, k, :], 2.0, tmp[:, :], ALU.mult, ALU.mult).then_inc(s.under_root, 1)
                    dve.wait_ge(s.under_root, k + 1)
                dve.wait_ge(s.gated, LRU_T)
                for k in range(LRU_T):
                    dve.wait_ge(s.rooted, k + 1)
                    link(dve.tensor_tensor(gi[:, k, :], gi[:, k, :], gr[:, k, :], ALU.mult))
                    link(dve.tensor_tensor_scan(gr[:, k, 0:T], xc[:, k, 0:T], gi[:, k, 0:T], 0.0, ALU.mult, ALU.add))
                    link(dve.tensor_tensor(gr[:, k, T:NT], xc[:, k, T:NT], g.h0[:, k, :], ALU.mult))
                    dve.tensor_tensor(gr[:, k, T:NT], gr[:, k, T:NT], gi[:, k, T:NT], ALU.add).then_inc(s.scanned, 1)
                for k in range(LRU_T):
                    dve.wait_ge(s.gelus, k + 1)
                    dve.wait_ge(s.scanned, k + 1)
                    link(dve.tensor_tensor(gate[:, k, :], gate[:, k, :], gr[:, k, :], ALU.mult))
                dve.wait_ge(s.turned, 1)
                dve.tensor_copy(h_rows[:, :], ps[0:9, 6, :]).then_inc(s.rows, 1)

            @block.tensor
            def _(pe):
                pe.wait_ge(s.w_in, 64)
                for k in range(LRU_T):
                    pe.wait_ge(s.conv, k + 1)
                    for o, done in ((0, s.gates_a), (1, s.gates_x)):
                        if k:
                            pe.wait_ge(s.gate_sig, 2 * k + o - 1)
                        for n in range(3):
                            last = pe.matmul(ps[:, 3 * o + n, 0:N3], wax[:, o, k, :], xc[:, k, n * N3:(n + 1) * N3],
                                             start=True, stop=True)
                        last.then_inc(done, 1)
                pe.wait_ge(s.scanned, LRU_T)
                for k in range(LRU_T):
                    last = pe.transpose(ps[0:9, 6, k * P:(k + 1) * P], gr[:, k, T - 1:NT], g.ident[:, :])
                last.then_inc(s.turned, 1)

            @block.scalar
            def _(act):
                act.wait_ge(s.lam_x, 1)
                act.activation(lam[:, 0, :], lam[:, 5, :], ACT.Exp).then_inc(s.lam_exp, 1)
                act.wait_ge(s.lam_sum, 1)
                act.activation(lam[:, 2, :], lam[:, 1, :], ACT.Ln).then_inc(s.lam_log, 1)
                for k in range(LRU_T):
                    act.wait_ge(s.gates_a, k + 1)
                    act.activation(cols3(gr[:, k, :]), bank3(ps, 0), ACT.Sigmoid, bias=par[:, q["lru_ba"] + k:q["lru_ba"] + k + 1]).then_inc(s.gate_sig, 1)
                    act.wait_ge(s.gates_x, k + 1)
                    act.activation(cols3(gi[:, k, :]), bank3(ps, 3), ACT.Sigmoid, bias=par[:, q["lru_bx"] + k:q["lru_bx"] + k + 1]).then_inc(s.gate_sig, 1)
                act.wait_ge(s.gated, LRU_T)
                for k in range(LRU_T):
                    act.activation(xc[:, k, :], gr[:, k, :], ACT.Exp).then_inc(s.decayed, 1)
                    act.wait_ge(s.decayed, k + 1)
                    act.activation(gr[:, k, :], gr[:, k, :], ACT.Tanh, scale=-1.0).then_inc(s.tanhs, 1)
                for k in range(LRU_T):
                    act.wait_ge(s.under_root, k + 1)
                    act.activation(gr[:, k, :], gr[:, k, :], ACT.Sqrt).then_inc(s.rooted, 1)
                for k in range(LRU_T):
                    act.activation(gate[:, k, :], gate[:, k, :], ACT.Gelu_apprx_tanh).then_inc(s.gelus, 1)


def token_shift(nc, g, d, ps, big, w2a, g2, kept, masks):
    mu = COL["mu_shift"]
    with ExitStack() as mem:
        diff = mem.enter_context(tensor(nc, "diff", [P, 2, T], F32))
        sdiff = mem.enter_context(tensor(nc, "sample_diff", [P, RWC_T, NS], F32))
        with phase(nc, "w_in", "steps", "pool_steps", "shifted", "act_steps") as (s, block):
            @block.sync
            def _(sp):
                sp.dma_start(w2a[0:64, :], d.rw_w2[0]).then_inc(s.w_in, 16)
                sp.dma_start(w2a[64:128, :], d.rw_a2[0]).then_inc(s.w_in, 16)
                sp.dma_start(g2[:, :], d.rw_g2[0]).then_inc(s.w_in, 16)
                sp.wait_ge(s.w_in, 48)

            @block.vector
            def _(dve):
                link = linker(dve, s.steps)
                link(dve.memset(big[:, 0:RWC_T, 0:PAD], 0.0))
                p_s = big[:, 0:RWC_T, PAD + T:PAD + NT]
                link(dve.tensor_tensor(sdiff[:, :, :], g.shift0[:, :, :], p_s, ALU.subtract))
                link(dve.tensor_tensor(sdiff[:, :, :], sdiff[:, :, :],
                                       g.par[:, mu:mu + RWC_T].unsqueeze(2).to_broadcast([P, RWC_T, NS]), ALU.mult))
                link(dve.tensor_tensor(p_s, p_s, sdiff[:, :, :], ALU.add))
                order = [12, 13] + list(range(12))
                for n, k in enumerate(order):
                    row = big[:, k, :]
                    link(dve.tensor_tensor(diff[:, n % 2, :], row[:, PAD - 1:PAD - 1 + T], row[:, PAD:PAD + T], ALU.subtract))
                    dve.scalar_tensor_tensor(row[:, PAD:PAD + T], diff[:, n % 2, :], g.par[:, mu + k:mu + k + 1],
                                             row[:, PAD:PAD + T], ALU.mult, ALU.add).then_inc(s.shifted, 1)

            @block.scalar
            def _(act):
                act.wait_ge(s.shifted, 2)
                act.wait_ge(s.steps, 4)
                act.activation(big[:, 13, PAD:PAD + NT], big[:, 13, PAD:PAD + NT], ACT.Sigmoid).then_inc(s.act_steps, 1)
                act.activation(big[0:64, 12, PAD:PAD + NT], big[0:64, 12, PAD:PAD + NT], ACT.Tanh).then_inc(s.act_steps, 1)

            @block.gpsimd
            def _(pool):
                link = linker(pool, s.pool_steps)
                link(pool.memset(kept[:, :], 1.0))
                link(pool.memset(kept[:, 0:T:C], 0.0))
                link(pool.memset(kept[:, T:NT], 0.0))
                for m in range(8):
                    link(pool.tensor_copy(masks[:, 10 + m, :], g.ident[:, 16 * m:16 * m + 1].to_broadcast([P, C])))
                for m in range(10):
                    link(pool.memset(masks[:, m, :], 1.0))
                for h in range(2):
                    rows = slice(64 * h, 64 * h + 64)

                    def cut(m, pattern, base, mult, keep_where, shape=None):
                        v = masks[rows, m, :]
                        if shape:
                            v = v.rearrange("p (a b) -> p a b", b=shape)
                        link(pool.affine_select(out=v, in_=v, compare_op=keep_where, fill=0.0, base=base,
                                                pattern=pattern, channel_multiplier=mult))
                    cut(0, [[1, C]], 0, -1, ALU.is_gt)
                    cut(1, [[1, C]], 0, -1, ALU.is_ge)
                    cut(2, [[-1, C]], 0, 1, ALU.is_gt)
                    for lvl in range(6):
                        b = 1 << lvl
                        n = C // (2 * b)
                        v = masks[rows, 3 + lvl, :].rearrange("p (a b) -> p a b", b=2 * b)
                        link(pool.affine_select(out=v, in_=v, compare_op=ALU.is_ge, fill=0.0, base=0,
                                                pattern=[[-2 * b, n], [0, 2 * b]], channel_multiplier=1))
                        link(pool.affine_select(out=v, in_=v, compare_op=ALU.is_gt, fill=0.0, base=b,
                                                pattern=[[2 * b, n], [0, 2 * b]], channel_multiplier=-1))
                        link(pool.affine_select(out=v, in_=v, compare_op=ALU.is_ge, fill=0.0, base=-b,
                                                pattern=[[0, n], [1, 2 * b]], channel_multiplier=0))
                    v = masks[rows, 9, :].rearrange("p (a b) -> p a b", b=2)
                    link(pool.affine_select(out=v, in_=v, compare_op=ALU.is_equal, fill=0.0, base=-1,
                                            pattern=[[-2, C // 2], [0, 2]], channel_multiplier=1))
                    link(pool.affine_select(out=v, in_=v, compare_op=ALU.is_equal, fill=0.0, base=0,
                                            pattern=[[0, C // 2], [1, 2]], channel_multiplier=0))


def rwkv_pair(nc, g, d, ps, big, w2a, g2, kept, masks, i):
    par = g.par
    with ExitStack() as mem:
        def sb(name, shape):
            return mem.enter_context(tensor(nc, name, shape, F32))

        names = ["r", "k", "v", "lw", "cum", "a", "kk", "bonus", "e_cum", "e_neg", "e_prev", "tmp"]
        buf = {n: sb(f"pair_{n}", [P, NT]) for n in names}
        rs, ks, vs, lw, cum, a, kk, bonus, e_cum, e_neg, e_prev, tmp = (buf[n] for n in names)
        col = sb("pair_par", [P, 8])
        w2s, g2s = sb("w2_slice", [P, P]), sb("g2_slice", [P, P])
        vec = sb("sample_vec", [P, 5, NS])
        vs8 = sb("sample_v", [P, NS])
        dend = sb("chunk_decay", [P, NC])
        S = sb("state", [P, 3, HD])
        u = sb("u", [P, 2, 2, HD])
        s8 = sb("sample_state", [P, NS, HD])
        t8 = sb("sample_tmp", [P, 2, NS, HD])
        p8 = sb("sample_prod", [P, NS, HD])
        sa = sb("sample_sa", [P, NS])
        s_rows = sb("state_rows_out", [HD, P])
        inv, prod = sb("inverse", [P, T]), sb("level_product", [P, T])
        spare = [g.X[:, :, :].rearrange("p k c -> p (k c)")[:, n * T:(n + 1) * T] for n in range(4)]
        a_tok, b_tok, k_tok, v_tok = spare
        inv_t, lt, mak, mrb, mrk = (x[:, 0:T] for x in (lw, cum, e_cum, e_neg, e_prev))
        gt, hh = kk[:, 0:T], ks[:, 0:T]

        def tokm(x):
            return x.rearrange("p (t h c) -> p t h c", t=TT, h=2)

        def halves(x, b):
            return x[:, b * 512:(b + 1) * 512].rearrange("p (n c) -> p n c", c=64)

        def bank(b):
            return ps[:, b, :].rearrange("p (n c) -> p n c", c=64)

        def mask(m):
            return masks[:, m, :].unsqueeze(1).to_broadcast([P, 8, C])

        two = (0, 1)

        def blocks(half):
            for t in range(4):
                for cp in two:
                    for hp in two:
                        c = 2 * (4 * half + t) + cp
                        yield (slice(t * P + hp * 64, t * P + hp * 64 + 64), slice(64 * cp, 64 * cp + 64),
                               slice(64 * hp, 64 * hp + 64), slice(c * C, (c + 1) * C), 4 * half + t, hp)

        with phase(nc, "copied", "z_made", "a_made", "sig", "dve", "cummed", "exps", "sq", "ssum", "root",
                   "bon", "bsum", "ready", "turned", "tok_copied", "gram", "gram_taken", "level_t", "p_made",
                   "p_taken", "x_made", "x_taken", "xt_made", "xt_taken", "g_made", "g_taken", "u_made", "u_taken",
                   "s_made", "s_taken", "y_made", "y_taken", "vec_taken", "spread", "spread_made", "spread_used",
                   "s8_in", "s8_done", "stored", "mean", "cent", "csq", "var", "vroot", "gsum", "rows_t", "rows_c",
                   "decayed", "y8", "act_steps", "k_inverted", "k_spread", "v_inverted", "v_spread", "v_copied") as (s, block):

            @block.sync
            def _(sp):
                states = d.state_rwkv_wkv[0].rearrange("b h v k -> b (h v) k")
                sp.dma_start(s8[:, :, :], states[:, ds(i * P, P), :].rearrange("b p k -> p b k")).then_inc(s.s8_in, 16)
                sp.wait_ge(s.s8_done, 1)
                out_s = d.wkv_s[0].rearrange("b h v k -> b (h v) k")
                sp.dma_start(out_s[:, ds(i * P, P), :].rearrange("b p k -> p b k"), s8[:, :, :]).then_inc(s.stored, 16)
                sp.wait_ge(s.rows_c, 1)
                sp.dma_start(d.wkv_p[0, 0, ds(2 * i, 2), :, :].rearrange("h v k -> v h k"),
                             s_rows[:, :].rearrange("v (h k) -> v h k", h=2)).then_inc(s.stored, 16)
                sp.wait_ge(s.stored, 32)

            @block.gpsimd
            def _(pool):
                pool.tensor_copy(w2s[:, :], w2a[:, ds(i * P, P)]).then_inc(s.copied, 1)
                pool.tensor_copy(col[:, 0:7], par[:, ds(COL["rw_w0"] + i, 7, 4)]).then_inc(s.copied, 1)
                pool.tensor_copy(rs[:, :], big[:, ds(i, 1), PAD:PAD + NT].rearrange("p a c -> p (a c)")).then_inc(s.copied, 1)
                pool.tensor_copy(g2s[:, :], g2[:, ds(i * P, P)]).then_inc(s.copied, 1)
                pool.memset(S[:, 0, :], 0.0).then_inc(s.copied, 1)
                pool.wait_ge(s.gram_taken, 10)
                for lvl in range(1, 6):
                    if lvl > 1:
                        pool.wait_ge(s.p_taken, 2 * (lvl - 1))
                    for b in two:
                        pool.tensor_tensor(halves(tmp, b), halves(lt, b), mask(3 + lvl), ALU.mult).then_inc(s.level_t, 1)

            @block.vector
            def _(dve):
                link = linker(dve, s.dve)
                w0, a0, c_kk, c_ka, c_rk, lnw, lnb = (col[:, n:n + 1] for n in range(7))
                link(dve.tensor_copy(ks[:, :], big[:, ds(i + RWT, 1), PAD:PAD + NT].rearrange("p a c -> p (a c)")))
                dve.wait_ge(s.copied, 2)
                link(dve.tensor_scalar(col[:, 7:8], c_ka, -1.0, 1.0, ALU.mult, ALU.add))
                link(dve.tensor_scalar(kk[:, :], ks[:, :], c_kk, None, ALU.mult))
                dve.sem_inc(s.sq, 1)
                dve.wait_ge(s.sig, 2)
                link(dve.tensor_scalar(lw[:, :], lw[:, :], DECAY, None, ALU.mult))
                link(dve.tensor_copy(vec[:, 0, :], lw[:, T:NT]))
                link(dve.memset(lw[:, T:NT], 0.0))
                link(dve.tensor_tensor_scan(cum[:, :], kept[:, :], lw[:, :], 0.0, ALU.mult, ALU.add))
                link(dve.tensor_tensor(e_prev[:, :], cum[:, :], lw[:, :], ALU.subtract))
                dve.sem_inc(s.cummed, 1)
                link(dve.tensor_scalar(bonus[:, :], a[:, :], c_ka, col[:, 7:8], ALU.mult, ALU.add))
                link(dve.tensor_tensor(ks[:, :], ks[:, :], bonus[:, :], ALU.mult))
                dve.wait_ge(s.copied, 3)
                link(dve.scalar_tensor_tensor(bonus[:, :], rs[:, :], c_rk, ks[:, :], ALU.mult, ALU.mult))
                dve.sem_inc(s.bon, 1)
                dve.wait_ge(s.root, 1)
                link(dve.tensor_scalar(tmp[:, 0:N4], tmp[:, 0:N4], 1e-12, None, ALU.max))
                link(dve.reciprocal(tmp[:, 0:N4], tmp[:, 0:N4]))
                dve.sem_inc(s.k_inverted, 1)
                dve.wait_ge(s.bsum, 1)
                dve.wait_ge(s.v_copied, 1)
                link(dve.tensor_tensor(cols3(bonus[:, :]), bank3(ps, 4), cols3(vs[:, :]), ALU.mult))
                dve.wait_ge(s.k_spread, 1)
                link(dve.tensor_tensor(cols4(kk[:, :]), cols4(kk[:, :]), ps[:, 0:4, 0:N4], ALU.mult))
                dve.wait_ge(s.exps, 4)
                link(dve.tensor_tensor(a[:, :], kk[:, :], a[:, :], ALU.mult))
                link(dve.tensor_tensor(a[:, :], a[:, :], e_neg[:, :], ALU.mult))
                dve.sem_inc(s.ready, 1)
                link(dve.scalar_tensor_tensor(kk[:, :], kk[:, :], -1.0, e_prev[:, :], ALU.mult, ALU.mult))
                dve.sem_inc(s.ready, 1)
                link(dve.tensor_tensor(ks[:, :], ks[:, :], e_neg[:, :], ALU.mult))
                dve.sem_inc(s.ready, 1)
                link(dve.tensor_tensor(rs[:, :], rs[:, :], e_cum[:, :], ALU.mult))
                dve.sem_inc(s.ready, 1)
                for n, x in ((1, kk), (2, a), (3, ks), (4, rs)):
                    link(dve.tensor_copy(vec[:, n, :], x[:, T:NT]))
                link(dve.tensor_copy(vs8[:, :], vs[:, T:NT]))
                link(dve.tensor_copy(dend[:, :], e_cum[:, C - 1:T:C]))
                dve.sem_inc(s.vec_taken, 1)
                for n in range(1, 8, 2):
                    dve.wait_ge(s.turned, n + 1)
                    dst = (b_tok, a_tok, k_tok, v_tok)[n // 2]
                    dve.tensor_copy(dst[:, 512:1024], ps[:, n, :]).then_inc(s.tok_copied, 1)
                for n, (dst, m) in enumerate(((lt, 0), (inv, 9), (mak, 0), (mrb, 1), (mrk, 1))):
                    for h in two:
                        dve.wait_ge(s.gram, 2 * n + h + 1)
                        dve.tensor_tensor(tokm(dst)[:, :, h, :], bank((2 * n + h) % 6), mask(m), ALU.mult).then_inc(s.gram_taken, 1)
                dve.wait_ge(s.gram_taken, 10)
                idb = g.ident2[:, :].unsqueeze(1).to_broadcast([P, 8, C])
                for b in two:
                    link(dve.tensor_tensor(halves(inv_t, b), halves(lt, b), mask(3), ALU.mult))
                    link(dve.tensor_tensor(halves(inv_t, b), halves(inv_t, b), idb, ALU.add))
                    link(dve.tensor_tensor(halves(inv, b), halves(inv, b), idb, ALU.add))
                    dve.sem_inc(s.x_taken, 1)
                    dve.sem_inc(s.xt_taken, 1)
                for lvl in range(1, 6):
                    for b in two:
                        dve.wait_ge(s.xt_made, 2 * (lvl - 1) + b + 1)
                        if lvl < 5:
                            dve.wait_ge(s.x_made, 2 * (lvl - 1) + b + 1)
                            dve.tensor_tensor(halves(inv, b), bank(2 + b), halves(inv, b), ALU.add).then_inc(s.x_taken, 1)
                        dve.tensor_tensor(halves(inv_t, b), bank(4 + b), halves(inv_t, b), ALU.add).then_inc(s.xt_taken, 1)
                dve.wait_ge(s.s8_in, 16)
                sample_step(dve, link, s, g, ps, s8, t8, p8, sa, vec, vs8, tmp)
                dve.wait_ge(s.g_taken, 6)
                for c in range(NC):
                    dve.wait_ge(s.u_made, c + 1)
                    rows = slice(64 * (c % 2), 64 * (c % 2) + 64)
                    if c >= 2:
                        dve.wait_ge(s.y_made, c - 1)
                    dve.tensor_tensor(u[rows, (c // 2) % 2, :, :], ps[rows, 4:6, 0:HD],
                                      tokm(hh)[rows, c // 2, :, :], ALU.add).then_inc(s.u_taken, 1)
                    dve.wait_ge(s.s_made, c + 1)
                    dve.wait_ge(s.decayed, c + 1)
                    dve.scalar_tensor_tensor(S[:, (c + 1) % 2, :], ps[:, 6 + c % 2, 0:HD], dend[:, c:c + 1], S[:, 2, :],
                                             ALU.mult, ALU.add).then_inc(s.s_taken, 1)
                dve.wait_ge(s.y_taken, 1)
                for cp in two:
                    y = tokm(tmp[:, 0:T])[:, :, cp, :]
                    link(dve.tensor_tensor(y, y, bank(2 + cp), ALU.add))
                dve.sem_inc(s.y8, 1)
                dve.wait_ge(s.mean, 1)
                link(dve.scalar_tensor_tensor(cols3(e_cum[:, :]), bank3(ps, 2), -1.0 / HD, cols3(tmp[:, :]), ALU.mult, ALU.add))
                dve.sem_inc(s.cent, 1)
                dve.wait_ge(s.vroot, 1)
                link(dve.reciprocal(e_prev[:, 0:N4], e_prev[:, 0:N4]))
                dve.sem_inc(s.v_inverted, 1)
                dve.wait_ge(s.v_spread, 1)
                link(dve.tensor_tensor(cols4(e_cum[:, :]), cols4(e_cum[:, :]), ps[:, 4:8, 0:N4], ALU.mult))
                link(dve.tensor_scalar(e_cum[:, :], e_cum[:, :], lnw, lnb, ALU.mult, ALU.add))
                link(dve.tensor_tensor(e_cum[:, :], e_cum[:, :], bonus[:, :], ALU.add))
                dve.wait_ge(s.gsum, 1)
                row = big[:, ds(i, 1), PAD:PAD + NT].rearrange("p a (n c) -> p (a n) c", n=3)
                link(dve.tensor_tensor(row, bank3(ps, 0), cols3(e_cum[:, :]), ALU.mult))

            @block.scalar
            def _(act):
                w0, a0 = col[:, 0:1], col[:, 1:2]
                act.activation(vs[:, :], big[:, ds(i + 2 * RWT, 1), PAD:PAD + NT].rearrange("p a c -> p (a c)"), ACT.Copy).then_inc(s.v_copied, 1)
                act.wait_ge(s.copied, 2)
                act.wait_ge(s.z_made, 1)
                act.activation(cols3(lw[:, :]), bank3(ps, 0), ACT.Sigmoid, bias=w0).then_inc(s.sig, 1)
                act.wait_ge(s.a_made, 1)
                act.activation(cols3(a[:, :]), bank3(ps, 3), ACT.Sigmoid, bias=a0).then_inc(s.sig, 1)
                act.wait_ge(s.sq, 1)
                act.activation(tmp[:, :], kk[:, :], ACT.Square).then_inc(s.act_steps, 1)
                act.wait_ge(s.cummed, 1)
                act.activation(e_neg[:, :], cum[:, :], ACT.Exp, scale=-1.0).then_inc(s.exps, 1)
                act.activation(e_prev[:, :], e_prev[:, :], ACT.Exp).then_inc(s.exps, 1)
                act.activation(e_cum[:, :], cum[:, :], ACT.Exp).then_inc(s.exps, 1)
                act.activation(vec[:, 0, :], vec[:, 0, :], ACT.Exp).then_inc(s.exps, 1)
                act.wait_ge(s.ssum, 1)
                act.activation(tmp[:, 0:N4], ps[:, 0, 0:N4], ACT.Sqrt).then_inc(s.root, 1)
                for n in range(0, 8, 2):
                    act.wait_ge(s.turned, n + 1)
                    dst = (b_tok, a_tok, k_tok, v_tok)[n // 2]
                    act.activation(dst[:, 0:512], ps[:, n, :], ACT.Copy).then_inc(s.act_steps, 1)
                for lvl in range(1, 6):
                    for b in two:
                        act.wait_ge(s.p_made, 2 * (lvl - 1) + b + 1)
                        if lvl > 1:
                            act.wait_ge(s.xt_made, 2 * (lvl - 1))
                        act.activation(halves(prod, b), bank(b), ACT.Copy).then_inc(s.p_taken, 1)
                for n, dst in enumerate((gt, prod, hh)):
                    for b in two:
                        act.wait_ge(s.g_made, 2 * n + b + 1)
                        to = tokm(dst)[:, :, b, :] if n == 0 else halves(dst, b)
                        act.activation(to, bank(2 * n + b), ACT.Copy).then_inc(s.g_taken, 1)
                for c in range(NC):
                    if c:
                        act.wait_ge(s.s_taken, c)
                    act.activation(S[:, 2, :], S[:, c % 2, :], ACT.Copy, scale=dend[:, c:c + 1]).then_inc(s.decayed, 1)
                act.wait_ge(s.y_made, NC)
                act.activation(tmp[:, 0:T].rearrange("p (b c) -> p b c", b=2), ps[:, 0:2, :], ACT.Copy).then_inc(s.y_taken, 1)
                act.wait_ge(s.rows_t, 1)
                act.activation(s_rows[:, :], ps[0:HD, 5, 0:P], ACT.Copy).then_inc(s.rows_c, 1)
                act.wait_ge(s.cent, 1)
                act.activation(e_neg[:, :], e_cum[:, :], ACT.Square).then_inc(s.csq, 1)
                act.wait_ge(s.var, 1)
                act.activation(e_prev[:, 0:N4], ps[:, 5, 0:N4], ACT.Sqrt, scale=1.0 / HD, bias=g.epsc[:, 1:2]).then_inc(s.vroot, 1)

            @block.tensor
            def _(pe):
                def head_sums(x, first, done):
                    for n in range(3):
                        last = pe.matmul(ps[:, first + n, 0:N3], g.blockones[:, :], x[:, n * N3:(n + 1) * N3], start=True, stop=True)
                    last.then_inc(done, 1)

                def packed_sums(x, bank_at, done):
                    for n in range(4):
                        last = pe.matmul(ps[32 * n:32 * n + 32, bank_at, 0:N4], g.blockones[:, 0:P:4], x[:, n * N4:(n + 1) * N4],
                                         start=True, stop=True, skip_group_check=True)
                    last.then_inc(done, 1)

                def unpack(x, first, done):
                    for n in range(4):
                        rows = masks[:, 10 + 2 * n:12 + 2 * n, :].rearrange("p a c -> p (a c)")
                        last = pe.matmul(ps[:, first + n, 0:N4], rows, x[:, 0:N4], start=True, stop=True)
                    last.then_inc(done, 1)

                def block_row(w, x, first, done):
                    for n in range(3):
                        last = pe.matmul(ps[:, first + n, 0:N3], w, x[:, PAD + n * N3:PAD + (n + 1) * N3], start=True, stop=True)
                    last.then_inc(done, 1)

                pe.wait_ge(s.copied, 1)
                block_row(w2s[0:64, :], big[0:64, 12, :], 0, s.z_made)
                block_row(w2s[64:128, :], big[64:128, 12, :], 3, s.a_made)
                pe.wait_ge(s.act_steps, 1)
                pe.wait_ge(s.sig, 1)
                packed_sums(tmp, 0, s.ssum)
                pe.wait_ge(s.sig, 2)
                pe.wait_ge(s.bon, 1)
                head_sums(bonus, 4, s.bsum)
                pe.wait_ge(s.k_inverted, 1)
                unpack(tmp, 0, s.k_spread)
                pe.wait_ge(s.ready, 4)
                for n in range(8):
                    src = (a, kk, ks, vs)[n // 2]
                    for t in range(4):
                        tt = 4 * (n % 2) + t
                        last = pe.transpose(ps[:, n, t * P:(t + 1) * P], src[:, tt * P:(tt + 1) * P], g.ident[:, :])
                    last.then_inc(s.turned, 1)
                gram = ((a, kk), (kk, a), (ks, kk), (a, rs), (ks, rs))
                for n, (l, r) in enumerate(gram):
                    for h in two:
                        g_at = 2 * n + h
                        hp = slice(64 * h, 64 * h + 64)
                        if g_at < 6:
                            if g_at % 2:
                                pe.wait_ge(s.tok_copied, g_at // 2 + 1)
                            else:
                                pe.wait_ge(s.act_steps, 2 + g_at // 2)
                        else:
                            pe.wait_ge(s.gram_taken, g_at - 5)
                        for c in range(NC):
                            cp, cols = slice(64 * (c % 2), 64 * (c % 2) + 64), slice(c * C, (c + 1) * C)
                            last = pe.matmul(ps[cp, g_at % 6, (c // 2) * 64:(c // 2 + 1) * 64], l[hp, cols], r[hp, cols],
                                             start=True, stop=True)
                        last.then_inc(s.gram, 1)
                pe.wait_ge(s.gram_taken, 10)
                for lvl in range(1, 6):
                    for b in two:
                        pe.wait_ge(s.level_t, 2 * (lvl - 1) + b + 1)
                        pe.wait_ge(s.x_taken, 2 * (lvl - 1) + b + 1)
                        for at, cp, hp, _, tt, h in blocks(b):
                            m = slice(tt * P + h * 64, tt * P + h * 64 + 64)
                            last = pe.matmul(ps[cp, b, at], tmp[cp, m], inv[cp, m], start=True, stop=True)
                        last.then_inc(s.p_made, 1)
                    for b in two:
                        pe.wait_ge(s.p_taken, 2 * (lvl - 1) + b + 1)
                        pe.wait_ge(s.xt_taken, 2 * (lvl - 1) + b + 1)
                        if lvl < 5:
                            for at, cp, hp, _, tt, h in blocks(b):
                                m = slice(tt * P + h * 64, tt * P + h * 64 + 64)
                                last = pe.matmul(ps[cp, 2 + b, at], inv_t[cp, m], prod[cp, m], start=True, stop=True)
                            last.then_inc(s.x_made, 1)
                        for at, cp, hp, _, tt, h in blocks(b):
                            m = slice(tt * P + h * 64, tt * P + h * 64 + 64)
                            last = pe.matmul(ps[cp, 4 + b, at], prod[cp, m], inv_t[cp, m], start=True, stop=True)
                        last.then_inc(s.xt_made, 1)
                pe.wait_ge(s.xt_taken, 12)
                for cp in two:
                    cpr = slice(64 * cp, 64 * cp + 64)
                    for tt in range(TT):
                        for h in two:
                            hpr = slice(64 * h, 64 * h + 64)
                            m = slice(tt * P + h * 64, tt * P + h * 64 + 64)
                            last = pe.matmul(ps[hpr, cp, tt * C:(tt + 1) * C], a_tok[cpr, m], inv_t[cpr, m],
                                             start=True, stop=True)
                    last.then_inc(s.g_made, 1)
                for n, (l, r) in enumerate(((mak, v_tok), (inv_t, prod))):
                    for b in two:
                        if n:
                            pe.wait_ge(s.g_taken, 3 + b)
                        for at, cp, hp, _, tt, h in blocks(b):
                            m = slice(tt * P + h * 64, tt * P + h * 64 + 64)
                            last = pe.matmul(ps[cp, 2 * (n + 1) + b, at], l[cp, m], r[cp, m], start=True, stop=True)
                        last.then_inc(s.g_made, 1)
                pe.wait_ge(s.act_steps, 5)
                pe.wait_ge(s.tok_copied, 4)
                for n in range(5):
                    pe.wait_ge(s.spread, n + 1)
                    if n >= 2:
                        pe.wait_ge(s.spread_used, n - 1)
                    pe.matmul(ps[:, 6 + n % 2, :], g.blockones[:, :], t8[:, n % 2, :, :].rearrange("p b k -> p (b k)"),
                              start=True, stop=True).then_inc(s.spread_made, 1)
                pe.wait_ge(s.spread_used, 5)
                pe.wait_ge(s.g_taken, 6)
                pe.wait_ge(s.copied, 5)
                for c in range(NC):
                    tt, cp = c // 2, c % 2
                    cpr = slice(64 * cp, 64 * cp + 64)
                    ub = (c // 2) % 2
                    cols = slice(c * C, (c + 1) * C)
                    if c:
                        pe.wait_ge(s.s_taken, c)
                    for h in two:
                        hpr = slice(64 * h, 64 * h + 64)
                        last = pe.matmul(ps[cpr, 4 + h, 0:HD], gt[hpr, cols], S[hpr, c % 2, :], start=True, stop=True)
                    last.then_inc(s.u_made, 1)
                    heads = [(slice(64 * h, 64 * h + 64), slice(tt * P + h * 64, tt * P + h * 64 + 64),
                              u[cpr, ub, h, :], ps[64 * h:64 * h + 64, 6 + cp, 0:HD],
                              ps[64 * h:64 * h + 64, c // 8, (c % 8) * C:(c % 8 + 1) * C],
                              ps[64 * h:64 * h + 64, 2 + cp, tt * C:(tt + 1) * C]) for h in two]
                    for hpr, m, _, new, y_s, y in heads:
                        pe.matmul(y_s, S[hpr, c % 2, :], rs[hpr, cols], start=True, stop=True)
                        pe.matmul(new, k_tok[cpr, m], v_tok[cpr, m], start=True, stop=False)
                        pe.matmul(y, v_tok[cpr, m], mrk[cpr, m], start=True, stop=False)
                    pe.wait_ge(s.u_taken, c + 1)
                    for hpr, m, uh, new, _, y in heads:
                        last = pe.matmul(new, b_tok[cpr, m], uh, start=False, stop=True)
                    last.then_inc(s.s_made, 1)
                    for hpr, m, uh, new, _, y in heads:
                        last = pe.matmul(y, uh, mrb[cpr, m], start=False, stop=True)
                    last.then_inc(s.y_made, 1)
                pe.wait_ge(s.y_taken, 1)
                pe.wait_ge(s.s_taken, NC)
                pe.transpose(ps[0:HD, 5, 0:P], S[:, NC % 2, :], g.ident[:, :]).then_inc(s.rows_t, 1)
                pe.wait_ge(s.y8, 2)
                head_sums(tmp, 2, s.mean)
                pe.wait_ge(s.csq, 1)
                pe.wait_ge(s.rows_c, 1)
                packed_sums(e_neg, 5, s.var)
                pe.wait_ge(s.cent, 1)
                block_row(g2s[:, :], big[:, 13, :], 0, s.gsum)
                pe.wait_ge(s.v_inverted, 1)
                unpack(e_prev, 4, s.v_spread)


def sample_step(dve, link, s, g, ps, s8, t8, p8, sa, vec, vs8, y):
    order = [1, 0, 2, 3, 4]

    def fill(n):
        if n >= 2:
            dve.wait_ge(s.spread_made, n - 1)
        link(dve.tensor_tensor(t8[:, n % 2, :, :], g.ident2[:, :].unsqueeze(1).to_broadcast([P, NS, HD]),
                               vec[:, order[n], :].unsqueeze(2).to_broadcast([P, NS, HD]), ALU.mult))
        dve.sem_inc(s.spread, 1)

    def spread(n):
        dve.wait_ge(s.spread_made, n + 1)
        return ps[:, 6 + n % 2, :].rearrange("p (b k) -> p b k", k=HD)

    fill(0)
    fill(1)
    for n in range(5):
        x = spread(n)
        if n == 0:
            link(dve.tensor_tensor(p8[:, :, :], s8[:, :, :], x, ALU.mult))
            link(dve.tensor_reduce(sa[:, :], p8[:, :, :], AX.X, ALU.add))
        elif n == 1:
            link(dve.tensor_tensor(s8[:, :, :], s8[:, :, :], x, ALU.mult))
        elif n < 4:
            rows = (sa, vs8)[n - 2]
            link(dve.tensor_tensor(p8[:, :, :], x, rows[:, :].unsqueeze(2).to_broadcast([P, NS, HD]), ALU.mult))
            link(dve.tensor_tensor(s8[:, :, :], s8[:, :, :], p8[:, :, :], ALU.add))
        else:
            dve.sem_inc(s.s8_done, 1)
            link(dve.tensor_tensor(p8[:, :, :], s8[:, :, :], x, ALU.mult))
            link(dve.tensor_reduce(y[:, T:NT], p8[:, :, :], AX.X, ALU.add))
            dve.sem_inc(s.y8, 1)
        dve.sem_inc(s.spread_used, 1)
        if n + 2 < 5:
            fill(n + 2)


def memory_attention(nc, g, d, ps, layer):
    with ExitStack() as mem:
        Q = mem.enter_context(tensor(nc, "mem_q", [P, MH, NT]))
        kt = mem.enter_context(tensor(nc, "mem_kt", [P, MH, MEM]))
        vtok = mem.enter_context(tensor(nc, "mem_v", [P, 2, MH * P]))
        memory_kv(nc, g, d, ps, layer, kt, vtok)
        with ExitStack() as inner:
            H = parts(nc, inner, "h_mem", [P, DT, NT])
            rms_norm(nc, g, ps, H, COL["g_mem"] + layer * DT)
            project(nc, ps, tiles_of(d.wq_mem[layer], DT), DT, MH // 2, H, kept_in(lambda m: Q[:, m, :]))
        norm_queries(nc, g, ps, Q, layer)
        memory_attention_samples(nc, g, d, ps, layer, Q)
        with ExitStack() as inner:
            bufs = record(
                q=inner.enter_context(tensor(nc, "head_q", [P, T])), k=inner.enter_context(tensor(nc, "head_k", [P, MEM])),
                v=inner.enter_context(tensor(nc, "head_v", [P, 2, P])), p=inner.enter_context(tensor(nc, "probs", [P, 2, MEM])),
                pt=inner.enter_context(tensor(nc, "probs_t", [P, 2, MEM])), stat=inner.enter_context(tensor(nc, "stats", [P, 2, 4])))
            with nc.Fori(0, MH) as head:
                memory_attention_head(nc, g, ps, Q, kt, vtok, bufs, head)
        with ExitStack() as inner:
            O = parts(nc, inner, "mem_out", [P, MH, NT])
            project(nc, ps, tiles_of(d.wo_mem[layer], MH), MH, DT // 2, O, add_to_residual(g), split=[Q[:, h, :] for h in range(MH)])


def memory_kv(nc, g, d, ps, layer, kt, vtok):
    with ExitStack() as mem:
        mt = mem.enter_context(tensor(nc, "mem_tokens", [P, 2, D]))
        mg = mem.enter_context(tensor(nc, "mem_normed", [P, DT, MEM]))
        W = [mem.enter_context(tensor(nc, f"mem_w{n}", [P, DT, 512])) for n in range(2)]
        ktok = mem.enter_context(tensor(nc, "mem_k", [P, 2, 512]))
        junk = mem.enter_context(tensor(nc, "mem_squares", [P, D]))
        ss = mem.enter_context(tensor(nc, "mem_sums", [P, 12]))
        gain = COL["g_memkv"] + layer * DT
        with phase(nc, "mem_in", ("w_in", 2), "sums", "rms", "rstd", "normed", "turned", "gained", "k_made", "v_made",
                   "k_rms", "k_rstd", "k_normed", "v_taken", "k_turned", "kt_taken", "stored") as (s, block):
            @block.sync
            def _(sp):
                sp.dma_start(mt[:, :, :], d.mem_prompt[0].rearrange("(t p) c -> p t c", p=P)).then_inc(s.mem_in, 16)
                for n, w in enumerate((d.wk_mem, d.wv_mem)):
                    sp.dma_start(W[n][:, :, :], weight_blocks(w[layer], DT)).then_inc(s.w_in[n], 16)
                sp.wait_ge(s.k_normed, 8)
                sp.dma_start(d.mem_k_p[layer, 0].rearrange("(t p) h c -> p t (h c)", p=P), ktok[:, :, :]).then_inc(s.stored, 16)
                sp.wait_ge(s.v_taken, 1)
                sp.dma_start(d.mem_v_p[layer, 0].rearrange("(t p) h c -> p t (h c)", p=P), vtok[:, :, :]).then_inc(s.stored, 16)
                sp.wait_ge(s.stored, 32)

            @block.scalar
            def _(act):
                act.wait_ge(s.mem_in, 16)
                for t in range(2):
                    if t:
                        act.wait_ge(s.sums, 1)
                    act.activation(junk[:, :], mt[:, t, :], ACT.Square, accum_out=ss[:, t:t + 1]).then_inc(s.sums, 1)
                act.wait_ge(s.sums, 2)
                act.activation(ss[:, 2:4], ss[:, 0:2], ACT.Sqrt, scale=1.0 / D, bias=g.epsc[:, 0:1]).then_inc(s.rms, 1)
                act.wait_ge(s.k_made, 2)
                for t in range(2):
                    for h in range(MH):
                        n = 4 * t + h
                        act.wait_ge(s.sums, 2 + n)
                        act.activation(junk[:, 0:P], ps[:, 4 + t, h * P:(h + 1) * P], ACT.Square,
                                       accum_out=ss[:, 4 + n:5 + n]).then_inc(s.sums, 1)
                act.wait_ge(s.sums, 10)
                act.activation(ss[:, 4:12], ss[:, 4:12], ACT.Sqrt, scale=1.0 / P, bias=g.epsc[:, 0:1]).then_inc(s.k_rms, 1)
                act.wait_ge(s.v_made, 2)
                act.activation(vtok[:, :, :], ps[:, 6:8, :], ACT.Copy).then_inc(s.v_taken, 1)
                act.wait_ge(s.k_turned, 1)
                for t in range(2):
                    act.activation(kt[:, :, t * P:(t + 1) * P], ps[:, t, :].rearrange("p (h c) -> p h c", h=MH), ACT.Copy).then_inc(s.kt_taken, 1)

            @block.vector
            def _(dve):
                dve.wait_ge(s.rms, 1)
                dve.reciprocal(ss[:, 2:4], ss[:, 2:4]).then_inc(s.rstd, 1)
                dve.wait_ge(s.rstd, 1)
                for t in range(2):
                    dve.tensor_scalar(mt[:, t, :], mt[:, t, :], ss[:, 2 + t:3 + t], None, ALU.mult).then_inc(s.normed, 1)
                dve.wait_ge(s.turned, 4)
                for k in range(DT):
                    dve.tensor_scalar(mg[:, k, :], ps[:, k // 2, (k % 2) * MEM:(k % 2 + 1) * MEM],
                                      g.par[:, gain + k:gain + k + 1], None, ALU.mult).then_inc(s.gained, 1)
                dve.wait_ge(s.k_rms, 1)
                dve.reciprocal(ss[:, 4:12], ss[:, 4:12]).then_inc(s.k_rstd, 1)
                dve.wait_ge(s.k_rstd, 1)
                for t in range(2):
                    for h in range(MH):
                        dve.scalar_tensor_tensor(ktok[:, t, h * P:(h + 1) * P], ps[:, 4 + t, h * P:(h + 1) * P],
                                                 ss[:, 4 + 4 * t + h:5 + 4 * t + h], g.kn[:, layer, :],
                                                 ALU.mult, ALU.mult).then_inc(s.k_normed, 1)

            @block.tensor
            def _(pe):
                pe.wait_ge(s.normed, 2)
                for k in range(DT):
                    for t in range(2):
                        last = pe.transpose(ps[:, k // 2, (k % 2) * MEM + t * P:(k % 2) * MEM + (t + 1) * P],
                                            mt[:, t, k * P:(k + 1) * P], g.ident[:, :])
                    if k % 2:
                        last.then_inc(s.turned, 1)
                pe.wait_ge(s.gained, DT)
                for n, done in enumerate((s.k_made, s.v_made)):
                    pe.wait_ge(s.w_in[n], 16)
                    for t in range(2):
                        for k in range(DT):
                            last = pe.matmul(ps[:, 4 + 2 * n + t, :], mg[:, k, t * P:(t + 1) * P], W[n][:, k, :],
                                             start=k == 0, stop=k == DT - 1)
                        last.then_inc(done, 1)
                pe.wait_ge(s.k_normed, 8)
                for t in range(2):
                    for h in range(MH):
                        last = pe.transpose(ps[:, t, h * P:(h + 1) * P], ktok[:, t, h * P:(h + 1) * P], g.ident[:, :])
                last.then_inc(s.k_turned, 1)


def norm_queries(nc, g, ps, Q, layer):
    qn = COL["qn_mem"] + layer
    with ExitStack() as mem:
        sq = mem.enter_context(tensor(nc, "q_squares", [P, 2, NT]))
        rms = mem.enter_context(tensor(nc, "q_rms", [P, NT]))
        with phase(nc, "squared", "summed", "rooted", "inverted", "spread", "scaled") as (s, block):
            @block.scalar
            def _(act):
                for h in range(MH):
                    if h >= 2:
                        act.wait_ge(s.summed, h - 1)
                    act.activation(sq[:, h % 2, :], Q[:, h, :], ACT.Square).then_inc(s.squared, 1)
                act.wait_ge(s.summed, MH)
                act.activation(cols3(rms[:, :]), bank3(ps, 0), ACT.Sqrt, scale=1.0 / P, bias=g.epsc[:, 0:1]).then_inc(s.rooted, 1)

            @block.tensor
            def _(pe):
                for h in range(MH):
                    pe.wait_ge(s.squared, h + 1)
                    for n in range(3):
                        last = pe.matmul(ps[32 * h:32 * h + 32, n, 0:N3], g.ones[:, 0:32], sq[:, h % 2, n * N3:(n + 1) * N3],
                                         start=True, stop=True, skip_group_check=True)
                    last.then_inc(s.summed, 1)
                for n in range(3):
                    pe.wait_ge(s.inverted, n + 1)
                    for h in range(MH):
                        if n:
                            pe.wait_ge(s.scaled, MH * (n - 1) + h + 1)
                        pe.matmul(ps[:, 4 + h, 0:N3], row_to_all(g, 32 * h), rms[:, n * N3:(n + 1) * N3],
                                  start=True, stop=True).then_inc(s.spread, 1)

            @block.vector
            def _(dve):
                def invert(n):
                    dve.reciprocal(rms[:, n * N3:(n + 1) * N3], rms[:, n * N3:(n + 1) * N3]).then_inc(s.inverted, 1)

                dve.wait_ge(s.rooted, 1)
                invert(0)
                for n in range(3):
                    if n < 2:
                        invert(n + 1)
                    cols = slice(n * N3, (n + 1) * N3)
                    for h in range(MH):
                        dve.wait_ge(s.spread, MH * n + h + 1)
                        dve.scalar_tensor_tensor(Q[:, h, cols], Q[:, h, cols], g.par[:, qn:qn + 1], ps[:, 4 + h, 0:N3],
                                                 ALU.mult, ALU.mult).then_inc(s.scaled, 1)


def memory_attention_samples(nc, g, d, ps, layer, Q):
    scale = P ** -0.5
    NQ = NS * MH
    with ExitStack() as mem:
        KA = mem.enter_context(tensor(nc, "cache_k", [P, NS, 2, 512]))
        VA = mem.enter_context(tensor(nc, "cache_v", [P, NS, 2, 512]))
        qd = mem.enter_context(tensor(nc, "q_diag", [P, 2, MH, P]))
        prod = mem.enter_context(tensor(nc, "products", [P, 2, 512]))
        Z = mem.enter_context(tensor(nc, "scores", [P, 2, NQ]))
        stat = mem.enter_context(tensor(nc, "s_stats", [NQ, 4]))
        pz = mem.enter_context(tensor(nc, "s_probs", [NQ, MEM]))
        pt = mem.enter_context(tensor(nc, "s_probs_t", [P, 2, NQ]))
        with phase(nc, ("k_in", NS), "v_in", "diag", "spread", "steps", "scored", "z_turned", "shift", "exped",
                   "normed", "p_turned", "p_taken", "valued", "stored") as (s, block):
            @block.sync
            def _(sp):
                for b in range(NS):
                    sp.dma_start(KA[:, b, :, :], d.cache_mem_k[layer, b].rearrange("(t p) h c -> p t (h c)", p=P)).then_inc(s.k_in[b], 16)
                for b in range(NS):
                    sp.dma_start(VA[:, b, :, :], d.cache_mem_v[layer, b].rearrange("(t p) h c -> p t (h c)", p=P)).then_inc(s.v_in, 16)

            @block.gpsimd
            def _(pool):
                for b in range(NS):
                    if b >= 2:
                        pool.wait_ge(s.spread, b - 1)
                    pool.tensor_tensor(qd[:, b % 2, :, :], g.ident[:, :].unsqueeze(1).to_broadcast([P, MH, P]),
                                       Q[:, :, T + b:T + b + 1].to_broadcast([P, MH, P]), ALU.mult).then_inc(s.diag, 1)

            @block.vector
            def _(dve):
                link = linker(dve, s.steps)
                for b in range(NS):
                    dve.wait_ge(s.k_in[b], 16)
                    dve.wait_ge(s.spread, b + 1)
                    for t in range(2):
                        link(dve.tensor_tensor(prod[:, t, :], KA[:, b, t, :], ps[:, b % 2, :], ALU.mult))
                        link(dve.tensor_reduce(Z[:, t, b * MH:(b + 1) * MH], prod[:, t, :].rearrange("p (h c) -> p h c", h=MH),
                                               AX.X, ALU.add))
                    dve.sem_inc(s.scored, 1)
                dve.wait_ge(s.z_turned, 1)
                link(dve.tensor_reduce(stat[:, 0:1], ps[0:NQ, 2, 0:MEM], AX.X, ALU.max))
                dve.tensor_scalar(stat[:, 1:2], stat[:, 0:1], -scale, None, ALU.mult).then_inc(s.shift, 1)
                dve.wait_ge(s.exped, 1)
                link(dve.reciprocal(stat[:, 3:4], stat[:, 2:3]))
                dve.tensor_scalar(pz[:, :], pz[:, :], stat[:, 3:4], None, ALU.mult).then_inc(s.normed, 1)
                dve.wait_ge(s.valued, 1)
                dve.tensor_copy(Q[:, :, T:NT], ps[:, 4, 0:NQ].rearrange("p (h b) -> p h b", h=MH)).then_inc(s.stored, 1)

            @block.scalar
            def _(act):
                act.wait_ge(s.shift, 1)
                act.activation(pz[:, :], ps[0:NQ, 2, 0:MEM], ACT.Exp, scale=scale, bias=stat[:, 1:2],
                               accum_out=stat[:, 2:3]).then_inc(s.exped, 1)
                act.wait_ge(s.p_turned, 1)
                act.activation(pt[:, :, :], ps[:, 3, 0:2 * NQ].rearrange("p (t n) -> p t n", t=2), ACT.Copy).then_inc(s.p_taken, 1)

            @block.tensor
            def _(pe):
                for b in range(NS):
                    pe.wait_ge(s.diag, b + 1)
                    if b >= 2:
                        pe.wait_ge(s.scored, b - 1)
                    pe.matmul(ps[:, b % 2, :], g.ones[:, :], qd[:, b % 2, :, :].rearrange("p h c -> p (h c)"),
                              start=True, stop=True).then_inc(s.spread, 1)
                pe.wait_ge(s.scored, NS)
                for t in range(2):
                    last = pe.transpose(ps[0:NQ, 2, t * P:(t + 1) * P], Z[:, t, :], g.ident[:, :])
                last.then_inc(s.z_turned, 1)
                pe.wait_ge(s.normed, 1)
                for t in range(2):
                    last = pe.transpose(ps[:, 3, t * NQ:(t + 1) * NQ], pz[:, t * P:(t + 1) * P], g.ident[0:NQ, 0:NQ])
                last.then_inc(s.p_turned, 1)
                pe.wait_ge(s.v_in, 16 * NS)
                pe.wait_ge(s.p_taken, 1)
                for b in range(NS):
                    for h in range(MH):
                        for t in range(2):
                            last = pe.matmul(ps[:, 4, h * NS + b:h * NS + b + 1], VA[:, b, t, h * P:(h + 1) * P],
                                             pt[:, t, b * MH + h:b * MH + h + 1], start=t == 0, stop=t == 1)
                last.then_inc(s.valued, 1)


def memory_attention_head(nc, g, ps, Q, kt, vtok, b, i):
    scale = P ** -0.5

    def score(n):
        return ps[:, (0, 1, 6)[n % 3], 0:MEM]

    with phase(nc, "copied", "scored", "steps", "shift", "exped", "scaled", "turned", "taken", "valued", "done") as (s, block):
        @block.gpsimd
        def _(pool):
            pool.tensor_copy(b.k[:, :], kt[:, ds(i, 1), :].rearrange("p a c -> p (a c)")).then_inc(s.copied, 1)

        @block.tensor
        def _(pe):
            pe.wait_ge(s.copied, 3)
            for n in range(TT + 2):
                for m in ((0, 1) if n == 0 else (n + 1,)):
                    if m < TT:
                        if m >= 3:
                            pe.wait_ge(s.exped, m - 2)
                        pe.matmul(score(m), b.q[:, m * P:(m + 1) * P], b.k[:, :], start=True, stop=True).then_inc(s.scored, 1)
                if 1 <= n <= TT:
                    m = n - 1
                    pe.wait_ge(s.scaled, m + 1)
                    if m >= 2:
                        pe.wait_ge(s.taken, m - 1)
                    for t in range(2):
                        last = pe.transpose(ps[:, 2 + m % 2, t * P:(t + 1) * P], b.p[:, m % 2, t * P:(t + 1) * P], g.ident[:, :])
                    last.then_inc(s.turned, 1)
                if n >= 2:
                    m = n - 2
                    pe.wait_ge(s.taken, m + 1)
                    for t in range(2):
                        last = pe.matmul(ps[:, 4 + m // 4, (m % 4) * P:(m % 4 + 1) * P], b.v[:, t, :], b.pt[:, m % 2, t * P:(t + 1) * P],
                                         start=t == 0, stop=t == 1)
                    last.then_inc(s.valued, 1)

        @block.vector
        def _(dve):
            dve.tensor_copy(b.v[:, :, :], vtok[:, :, ds(i * P, P)]).then_inc(s.copied, 1)
            link = linker(dve, s.steps)
            for n in range(TT + 1):
                if n < TT:
                    dve.wait_ge(s.scored, n + 1)
                    st = b.stat[:, n % 2, :]
                    link(dve.tensor_reduce(st[:, 0:1], score(n), AX.X, ALU.max))
                    dve.tensor_scalar(st[:, 1:2], st[:, 0:1], -scale, None, ALU.mult).then_inc(s.shift, 1)
                if n:
                    m = n - 1
                    dve.wait_ge(s.exped, m + 1)
                    st = b.stat[:, m % 2, :]
                    link(dve.reciprocal(st[:, 3:4], st[:, 2:3]))
                    dve.tensor_scalar(b.p[:, m % 2, :], b.p[:, m % 2, :], st[:, 3:4], None, ALU.mult).then_inc(s.scaled, 1)

        @block.scalar
        def _(act):
            act.activation(b.q[:, :], Q[:, ds(i, 1), 0:T].rearrange("p a c -> p (a c)"), ACT.Copy).then_inc(s.copied, 1)
            for n in range(TT + 1):
                if n < TT:
                    act.wait_ge(s.shift, n + 1)
                    if n >= 2:
                        act.wait_ge(s.turned, n - 1)
                    st = b.stat[:, n % 2, :]
                    act.activation(b.p[:, n % 2, :], score(n), ACT.Exp, scale=scale, bias=st[:, 1:2],
                                   accum_out=st[:, 2:3]).then_inc(s.exped, 1)
                if n:
                    m = n - 1
                    act.wait_ge(s.turned, m + 1)
                    if m >= 2:
                        act.wait_ge(s.valued, m - 1)
                    act.activation(b.pt[:, m % 2, :], ps[:, 2 + m % 2, 0:MEM], ACT.Copy).then_inc(s.taken, 1)
            act.wait_ge(s.valued, TT)
            act.activation(Q[:, ds(i, 1), 0:T].rearrange("p a (n c) -> p (a n) c", n=2), ps[:, 4:6, :], ACT.Copy).then_inc(s.done, 1)


def stick_breaking(nc, g, d, ps):
    wqkv = d.w_qkv_sb[0]
    with ExitStack() as mem:
        QK = mem.enter_context(tensor(nc, "sb_qk", [P, 2 * DT, NT]))
        V = g.X[:, :, :].rearrange("p k c -> p (k c)")[:, 0:TT * D].rearrange("p (t c) -> p t c", t=TT)
        with ExitStack() as inner:
            H = parts(nc, inner, "h_sb", [P, DT, NT])
            rms_norm(nc, g, ps, H, COL["g_mix"] + DT, spill=d.spill)
            for first, scale in ((0, HD ** -0.5), (DT, 1.0)):
                keep = kept_in(lambda m, first=first: QK[:, first + m.start:first + m.stop, :] if isinstance(m, slice)
                               else QK[:, ds(first + m.start, 1), :], scale)
                project(nc, ps, tiles_of(wqkv[:, first * P:first * P + D], DT), DT, DT // 2, H, keep)
            sb_values(nc, g, d, ps, H, V)
        sb_store_keys(nc, g, d, ps, QK)
        sb_attention(nc, g, d, ps, QK, V)
        with ExitStack() as inner:
            O = parts(nc, inner, "sb_out", [P, DT, NT])
            project(nc, ps, tiles_of(d.w_out_sb[0], DT), DT, DT // 2, O, add_to_residual(g),
                    split=[QK[:, k, :] for k in range(DT)], reload=d.spill)


def sb_values(nc, g, d, ps, H, V):
    QC = 256
    with ExitStack() as mem:
        raw = mem.enter_context(tensor(nc, "v_raw", [P, 2, DT, QC]))
        W = parts(nc, mem, "v_w", [P, DT, QC])
        v8 = mem.enter_context(tensor(nc, "sample_v_rows", [P, D]))
        wv = weight_blocks(d.w_qkv_sb[0][:, 2 * D:3 * D], DT)
        NQ = D // QC
        NG = NQ * (TT + 1)
        with phase(nc, ("w_in", 2), "w_high", "w_low", "made", "taken_act", "taken_dve", "stored") as (s, block):
            @block.sync
            def _(sp):
                for q in range(NQ):
                    if q >= 2:
                        sp.wait_ge(s.w_low, 2 * (q - 1))
                    sp.dma_start(raw[:, q % 2, :, :], wv[:, :, q * QC:(q + 1) * QC]).then_inc(s.w_in[q % 2], 16)
                sp.wait_ge(s.taken_act, NG // 2)
                sp.wait_ge(s.taken_dve, NG // 2)
                sp.dma_start(d.sb_v_p[0, 0].rearrange("(t p) h c -> p t (h c)", p=P), V).then_inc(s.stored, 16)
                sp.dma_start(d.sb_v_s[0, :, 0].rearrange("b h c -> b (h c)"), v8[P - NS:P, :]).then_inc(s.stored, 16)
                sp.wait_ge(s.stored, 32)

            @block.gpsimd
            def _(pool):
                for q in range(NQ):
                    pool.wait_ge(s.w_high, q + 1)
                    half = slice(0, DT // 2)
                    pool.tensor_tensor(W.lo[:, half, :], raw[:, q % 2, half, :], W.hi[:, half, :].bitcast(F32), ALU.subtract).then_inc(s.w_low, 1)

            @block.tensor
            def _(pe):
                for n in range(NG):
                    q, t = divmod(n, TT + 1)
                    c = t * P if t < TT else NT - P
                    if t == 0:
                        pe.wait_ge(s.w_low, 2 * (q + 1))
                    if n >= 8:
                        pe.wait_ge(s.taken_dve if n % 2 else s.taken_act, (n - 8) // 2 + 1)
                    for k in range(DT):
                        for m, (xp, wp) in enumerate(((H.hi, W.hi), (H.lo, W.hi), (H.hi, W.lo))):
                            last = pe.matmul(ps[:, n % 8, 0:QC], xp[:, k, c:c + P], wp[:, k, :],
                                             start=k == 0 and m == 0, stop=k == DT - 1 and m == 2)
                    last.then_inc(s.made, 1)

            def place(n):
                q, t = divmod(n, TT + 1)
                cols = slice(q * QC, (q + 1) * QC)
                return (V[:, t, cols], ps[:, n % 8, 0:QC]) if t < TT else (v8[96:P, cols], ps[96:P, n % 8, 0:QC])

            @block.scalar
            def _(act):
                for q in range(NQ):
                    act.wait_ge(s.w_in[q % 2], 16 * (q // 2 + 1))
                    if q:
                        act.wait_ge(s.made, q * (TT + 1))
                    act.activation(W.hi[:, :, :], raw[:, q % 2, :, :], ACT.Copy).then_inc(s.w_high, 1)
                    for n in range(q * (TT + 1), (q + 1) * (TT + 1)):
                        if n % 2 == 0:
                            act.wait_ge(s.made, n + 1)
                            act.activation(*place(n), ACT.Copy).then_inc(s.taken_act, 1)

            @block.vector
            def _(dve):
                for q in range(NQ):
                    dve.wait_ge(s.w_high, q + 1)
                    half = slice(DT // 2, DT)
                    dve.tensor_tensor(W.lo[:, half, :], raw[:, q % 2, half, :], W.hi[:, half, :].bitcast(F32), ALU.subtract).then_inc(s.w_low, 1)
                    for n in range(q * (TT + 1), (q + 1) * (TT + 1)):
                        if n % 2:
                            dve.wait_ge(s.made, n + 1)
                            dve.tensor_copy(*place(n)).then_inc(s.taken_dve, 1)


def sb_store_keys(nc, g, d, ps, QK):
    with ExitStack() as mem:
        rows = mem.enter_context(tensor(nc, "k_rows", [P, TT + 1, D]))
        turn_rows(nc, g, ps, lambda k: QK[:, DT + k, :], rows, d.sb_k_p[0, 0].rearrange("t h c -> t (h c)"),
                  d.sb_k_s[0, :, 0].rearrange("b h c -> b (h c)"))


def sb_attention(nc, g, d, ps, QK, V):
    with ExitStack() as mem:
        def sb(name, shape):
            return mem.enter_context(tensor(nc, name, shape))

        b = record(
            q=sb("pair_q", [P, T]), k=sb("pair_k", [P, T]), v=sb("pair_v", [P, TT, P]), bias=sb("pair_bias", [P, 2]),
            A=sb("logits", [P, 3, 2, 512]), B=sb("softplus", [P, 2, 2, 512]), S=parts(nc, mem, "softplus", [P, 2, 2, 512]),
            kring=sb("k_ring", [P, KR, D]), vring=sb("v_ring", [P, VR, D]), prod=sb("products", [P, D]), pool_prod=sb("pool_products", [P, 2, D]),
            qrows=sb("query_rows", [P, D]),
            tail=mem.enter_context(tensor(nc, "tail_r", [P, P], F32R)), rest=mem.enter_context(tensor(nc, "rest_r", [P, P], F32R)),
            Z=sb("cache_logits", [P, 512]), 
            att=sb("cache_weights", [P, 512]), kept=sb("page_kept", [P, 512]), qcol=sb("q_column", [P, DT]))
        with phase(nc, "made", "masks") as (s, block):
            @block.scalar
            def _(act):
                act.activation(b.tail[:, :], g.tail[:, :], ACT.Copy).then_inc(s.masks, 1)
                act.activation(b.rest[:, :], g.rest[:, :], ACT.Copy).then_inc(s.masks, 1)

            @block.gpsimd
            def _(pool):
                link = linker(pool, s.made)
                link(pool.memset(b.kept[:, :], 1.0))
                link(pool.memset(b.kept[:, 0:512:PAGES], 0.0))
        sb_turn(nc, g, d, ps, QK, V, b, 0, prompt=False, values=False, keys=True)
        with nc.Fori(0, NS - 1) as i:
            sb_turn(nc, g, d, ps, QK, V, b, i, prompt=True, values=True, keys=True)
        sb_turn(nc, g, d, ps, QK, V, b, NS - 1, prompt=True, values=True, keys=False)


KR = 4
VR = 4
SB_STEPS = [(1, st) for st in range(7, -1, -1)] + [(0, st) for st in range(3, -1, -1)]
CAP = float(np.exp(40.0))
ACC, OUT, PV, PV_COL = 2, 4, 5, 7


def pool_page(p):
    return p % 3 != 0


def sb_turn(nc, g, d, ps, QK, V, b, i, prompt, values, keys):
    steps = SB_STEPS if prompt else []
    N = len(steps)
    two = (0, 1)
    L, tot = b.prod[:, 0:512], b.prod[:, 512:1024]
    b_next = i if not values else i + 1

    def span(n):
        tq, st = steps[n]
        return slice(max(0, P * st - 512 * tq), 512)

    def diagonal(n):
        tq, st = steps[n]
        return P * st >= 512 * tq

    def first(n):
        return n == 0 or steps[n][0] != steps[n - 1][0]

    def last_of(n):
        return n == N - 1 or steps[n][0] != steps[n + 1][0]

    def z_of(n, h):
        return ps[:, h, span(n)]

    def A_of(n, h):
        return b.A[:, n % 3, h, span(n)]

    def B_of(n, h):
        return b.B[:, n % 2, h, span(n)]

    def S_of(part, n, h):
        return part[:, n % 2, h, span(n)]

    with phase(nc, "copied", "z", "z_added", "exped", "capped", "logged", "soft", "high", "low", "summed", "arg", "weight", "rested",
               "out_done", "out_taken", ("k_in", KR), ("v_in", VR), ("k_used", KR), "v_used", "dve", "q_diag", "spread",
               "q_rows", "pool_prod", "prod_free", "cz", "cexp", "clog", "csoft", "ctri", "ctot", "carg", "catt",
               "pv_kept", "pv_turned", "pv_taken", "pool_steps") as (s, block):

        @block.sync
        def _(sp):
            for p in range(PAGES):
                if keys:
                    page = sp.value_load(b_pages(g, b_next, p), min_val=0, max_val=d.cache_sb_k.shape[1] - 1)
                    if p >= KR:
                        sp.wait_ge(s.k_used[p % KR], p // KR)
                    sp.dma_start(b.kring[:, p % KR, :], d.cache_sb_k[0, ds(page, 1), :, :, :].rearrange("a p h c -> p (a h c)")).then_inc(s.k_in[p % KR], 16)
                if values:
                    page = sp.value_load(b_pages(g, i, p), min_val=0, max_val=d.cache_sb_v.shape[1] - 1)
                    if p >= VR:
                        sp.wait_ge(s.v_used, p - VR + 1)
                    sp.dma_start(b.vring[:, p % VR, :], d.cache_sb_v[0, ds(page, 1), :, :, :].rearrange("a p h c -> p (a h c)")).then_inc(s.v_in[p % VR], 16)

        @block.gpsimd
        def _(pool):
            page = [0]

            def multiply_page():
                p = page[0]
                page[0] += 1
                if pool_page(p):
                    m = sum(pool_page(x) for x in range(p))
                    pool.wait_ge(s.k_in[p % KR], 16 * (p // KR + 1))
                    if m >= 2:
                        pool.wait_ge(s.prod_free, m - 1)
                    pool.tensor_tensor(b.pool_prod[:, m % 2, :], b.kring[:, p % KR, :], b.qrows[:, :], ALU.mult).then_inc(s.pool_prod, 1)
                    pool.wait_ge(s.pool_prod, m + 1)
                    pool.sem_inc(s.k_used[p % KR], 1)

            if keys:
                pool.tensor_copy(b.qcol[:, :], QK[:, 0:DT, ds(b_next + T, 1)].rearrange("p k a -> p (k a)")).then_inc(s.pool_steps, 1)
                pool.wait_ge(s.pool_steps, 1)
                pool.tensor_tensor(b.prod[:, :].rearrange("p (k c) -> p k c", c=P), g.ident[:, :].unsqueeze(1).to_broadcast([P, DT, P]),
                                   b.qcol[:, :].unsqueeze(2).to_broadcast([P, DT, P]), ALU.mult).then_inc(s.q_diag, 1)
            if prompt:
                pool.tensor_copy(b.v[:, :, :], V[:, :, ds(i * P, P)]).then_inc(s.copied, 1)
            if keys:
                pool.wait_ge(s.q_rows, 2)
                while page[0] < PAGES:
                    multiply_page()

        @block.vector
        def _(dve):
            link = linker(dve, s.dve)
            page = [0]

            def score_page():
                p = page[0]
                page[0] += 1
                if pool_page(p):
                    m = sum(pool_page(x) for x in range(p))
                    dve.wait_ge(s.pool_prod, m + 1)
                    product = b.pool_prod[:, m % 2, :]
                else:
                    product = b.prod[:, :]
                    dve.wait_ge(s.k_in[p % KR], 16 * (p // KR + 1))
                    link(dve.tensor_tensor(product, b.kring[:, p % KR, :], b.qrows[:, :], ALU.mult))
                    dve.sem_inc(s.k_used[p % KR], 1)
                link(dve.tensor_reduce(b.Z[:, PAGES - 1 - p:512:PAGES], product.rearrange("p (h c) -> p h c", c=HD), AX.X, ALU.add))
                if pool_page(p):
                    dve.sem_inc(s.prod_free, 1)

            def score_pages(n):
                for _ in range(min(n if prompt else PAGES, PAGES - page[0]) if keys else 0):
                    score_page()

            if prompt:
                dve.tensor_copy(b.k[:, :], QK[:, ds(i + DT, 1), 0:T].rearrange("p a c -> p (a c)")).then_inc(s.copied, 1)
                link(dve.tensor_copy(b.bias[:, :], g.sbb[:, ds(i * 2, 2)]))
                dve.sem_inc(s.copied, 1)
            if keys:
                dve.wait_ge(s.q_rows, 2)
            for n in range(N + 1):
                if n < N:
                    for h in two:
                        dve.wait_ge(s.exped, 2 * n + h + 1)
                        dve.tensor_scalar(B_of(n, h), B_of(n, h), CAP, None, ALU.min).then_inc(s.capped, 1)
                score_pages(1)
                if n:
                    for h in two:
                        dve.wait_ge(s.high, 2 * (n - 1) + h + 1)
                        dve.tensor_tensor(S_of(b.S.lo, n - 1, h), B_of(n - 1, h), S_of(b.S.hi, n - 1, h).bitcast(F32), ALU.subtract).then_inc(s.low, 1)
                score_pages(1)
                if n:
                    for h in two:
                        dve.wait_ge(s.summed, 2 * (n - 1) + h + 1)
                        dve.tensor_tensor(A_of(n - 1, h), A_of(n - 1, h), ps[:, ACC + h, span(n - 1)], ALU.subtract).then_inc(s.arg, 1)
                score_pages(1)
                if n < N:
                    for h in two:
                        dve.wait_ge(s.z_added, 2 * n + h + 1)
                        dve.wait_ge(s.logged, 2 * n + h + 1)
                        dve.tensor_tensor(B_of(n, h), B_of(n, h), A_of(n, h), ALU.max).then_inc(s.soft, 1)
            if values:
                dve.wait_ge(s.v_used, PAGES)
                dve.tensor_copy(b.prod[0:SBH, :].rearrange("p (a c) -> p a c", a=2), ps[0:SBH, PV:PV + 2, :]).then_inc(s.pv_kept, 1)
                dve.wait_ge(s.pv_turned, 1)
                for o in two:
                    dve.tensor_copy(QK[64 * o:64 * o + 64, 0:DT, ds(i + T, 1)],
                                    ps[64 * o:64 * o + 64, PV_COL, o:DT * SBH:SBH + 2].unsqueeze(2)).then_inc(s.pv_taken, 1)
            if keys:
                Zh = b.Z[:, :].rearrange("p (h n) -> p h n", n=PAGES)
                link(dve.tensor_tensor(Zh, Zh, g.sbb[:, :].unsqueeze(2).to_broadcast([P, SBH, PAGES]), ALU.add))
                dve.tensor_scalar(L, b.Z[:, :], 40.0, None, ALU.min).then_inc(s.cz, 1)
                dve.wait_ge(s.clog, 1)
                dve.tensor_tensor(L, L, b.Z[:, :], ALU.max).then_inc(s.csoft, 1)
                dve.wait_ge(s.ctri, 1)
                link(dve.tensor_tensor(b.Z[:, :], b.Z[:, :], ps[:, ACC, :], ALU.subtract))
                dve.wait_ge(s.ctot, 1)
                link(dve.tensor_tensor(b.Z[:, :], b.Z[:, :], tot, ALU.add))
                link(dve.tensor_tensor_scan(L, b.kept[:, :], tot, 0.0, ALU.mult, ALU.add))
                dve.tensor_tensor(b.Z[:, :], b.Z[:, :], L, ALU.subtract).then_inc(s.carg, 1)

        @block.scalar
        def _(act):
            act.preload_act_table_set("natural_log_exp_and_others")

            def read_logits(n):
                for h in two:
                    act.wait_ge(s.z, 2 * n + h + 1)
                    if n >= 2:
                        act.wait_ge(s.low, 2 * (n - 2) + h + 1)
                    act.activation(B_of(n, h), z_of(n, h), ACT.Exp, bias=b.bias[:, h:h + 1]).then_inc(s.exped, 1)
                for h in two:
                    if n >= 3:
                        act.wait_ge(s.out_done, 2 * (n - 3) + h + 1)
                    act.activation(A_of(n, h), z_of(n, h), ACT.Identity, bias=b.bias[:, h:h + 1]).then_inc(s.z_added, 1)

            if prompt:
                act.activation(b.q[:, :], QK[:, ds(i, 1), 0:T].rearrange("p a c -> p (a c)"), ACT.Copy).then_inc(s.copied, 1)
            if keys:
                act.wait_ge(s.spread, 1)
                for n in two:
                    act.activation(b.qrows[:, n * 512:(n + 1) * 512], ps[:, ACC + n, :], ACT.Copy).then_inc(s.q_rows, 1)
            if prompt:
                act.wait_ge(s.copied, 4)
            if prompt:
                read_logits(0)
            for n in range(N + 1):
                if n < N:
                    for h in two:
                        act.wait_ge(s.capped, 2 * n + h + 1)
                        act.activation(B_of(n, h), B_of(n, h), ACT.Ln, bias=g.ones[:, 0:1]).then_inc(s.logged, 1)
                if n + 1 < N:
                    read_logits(n + 1)
                if n:
                    for h in two:
                        act.wait_ge(s.arg, 2 * (n - 1) + h + 1)
                        act.activation(A_of(n - 1, h), A_of(n - 1, h), ACT.Exp).then_inc(s.weight, 1)
                if n < N:
                    for h in two:
                        act.wait_ge(s.soft, 2 * n + h + 1)
                        if n >= 2:
                            act.wait_ge(s.rested, 2 * (n - 2) + h + 1)
                        act.activation(S_of(b.S.hi, n, h), B_of(n, h), ACT.Copy).then_inc(s.high, 1)
                if n and last_of(n - 1):
                    act.wait_ge(s.out_done, 2 * n)
                    tq = steps[n - 1][0]
                    act.activation(QK[:, ds(i, 1), 512 * tq:512 * tq + 512].rearrange("p a c -> p (a c)"), ps[:, OUT, :], ACT.Copy).then_inc(s.out_taken, 1)
            if keys:
                act.wait_ge(s.cz, 1)
                act.activation(L, L, ACT.Exp).then_inc(s.cexp, 1)
                act.wait_ge(s.cexp, 1)
                act.activation(L, L, ACT.Ln, bias=g.ones[:, 0:1]).then_inc(s.clog, 1)
                act.wait_ge(s.ctri, 2)
                act.activation(tot, ps[:, ACC + 1, :], ACT.Copy).then_inc(s.ctot, 1)
                act.wait_ge(s.carg, 1)
                if values:
                    act.wait_ge(s.v_used, PAGES)
                act.activation(b.att[:, :], b.Z[:, :], ACT.Exp).then_inc(s.catt, 1)

        @block.tensor
        def _(pe):
            page = [0]

            def logits(n):
                tq, st = steps[n]
                for h in two:
                    r = slice(64 * h, 64 * h + 64)
                    if n:
                        pe.wait_ge(s.z_added, 2 * (n - 1) + h + 1)
                        pe.wait_ge(s.exped, 2 * (n - 1) + h + 1)
                    q = b.q[r, 512 * tq + span(n).start:512 * tq + 512]
                    if diagonal(n):
                        pe.matmul(z_of(n, h), b.k[r, st * P:(st + 1) * P], q, start=True, stop=False, skip_group_check=True)
                        pe.matmul(z_of(n, h)[:, 0:P], g.ident[:, :], g.blocked[:, :], start=False, stop=True,
                                  skip_group_check=True).then_inc(s.z, 1)
                    else:
                        pe.matmul(z_of(n, h), b.k[r, st * P:(st + 1) * P], q, start=True, stop=True).then_inc(s.z, 1)

            def value_page():
                if not values or page[0] == PAGES:
                    return
                p = page[0]
                page[0] += 1
                pe.wait_ge(s.v_in[p % VR], 16 * (p // VR + 1))
                at = b.att[:, PAGES - 1 - p:512:PAGES]
                for n in two:
                    last = pe.matmul(ps[0:SBH, PV + n, :], at, b.vring[:, p % VR, n * 512:(n + 1) * 512],
                                     start=p == 0, stop=p == PAGES - 1, skip_group_check=True)
                last.then_inc(s.v_used, 1)

            if keys:
                pe.wait_ge(s.q_diag, 1)
                for n in two:
                    last = pe.matmul(ps[:, ACC + n, :], g.ones[:, :], b.prod[:, n * 512:(n + 1) * 512], start=True, stop=True)
                last.then_inc(s.spread, 1)
            if prompt:
                pe.wait_ge(s.copied, 4)
            if prompt:
                logits(0)
            for n in range(N + 1):
                if n + 1 < N:
                    logits(n + 1)
                if n:
                    m = n - 1
                    for h in two:
                        if keys and m == 0 and h == 0:
                            pe.wait_ge(s.q_rows, 2)
                        pe.wait_ge(s.low, 2 * m + h + 1)
                        pe.matmul(ps[:, ACC + h, span(m)], b.tail[:, :], S_of(b.S.hi, m, h), start=first(m), stop=False, skip_group_check=True)
                        pe.matmul(ps[:, ACC + h, span(m)], b.tail[:, :], S_of(b.S.lo, m, h), start=False, stop=last_of(m),
                                  skip_group_check=True).then_inc(s.summed, 1)
                value_page()
                value_page()
                if n:
                    for h in two:
                        pe.wait_ge(s.arg, 2 * m + h + 1)
                        pe.matmul(ps[:, ACC + h, span(m)], b.rest[:, :], S_of(b.S.hi, m, h), start=False, stop=False, skip_group_check=True)
                        pe.matmul(ps[:, ACC + h, span(m)], b.rest[:, :], S_of(b.S.lo, m, h), start=False, stop=last_of(m),
                                  skip_group_check=True).then_inc(s.rested, 1)
                value_page()
                if n:
                    if first(m) and m:
                        pe.wait_ge(s.out_taken, 1)
                    for h in two:
                        pe.wait_ge(s.weight, 2 * m + h + 1)
                        pe.matmul(ps[64 * h:64 * h + 64, OUT, span(m)], b.v[:, steps[m][1], 64 * h:64 * h + 64], A_of(m, h),
                                  start=first(m), stop=last_of(m), skip_group_check=True).then_inc(s.out_done, 1)
            if values:
                pe.wait_ge(s.pv_kept, 1)
                for k in range(DT):
                    last = pe.transpose(ps[:, PV_COL, k * SBH:(k + 1) * SBH], b.prod[0:SBH, k * P:(k + 1) * P], g.ident[0:SBH, 0:SBH])
                last.then_inc(s.pv_turned, 1)
            if keys:
                pe.wait_ge(s.csoft, 1)
                for n, m in enumerate((g.tail, g.ones)):
                    pe.matmul(ps[:, ACC + n, :], m[:, :], L, start=True, stop=True).then_inc(s.ctri, 1)


def b_pages(g, b, p):
    at = b * PAGES + p
    return g.pages[0:1, at:at + 1] if isinstance(at, int) else g.pages[0:1, ds(at, 1)]


def store_outputs(nc, g, d, ps):
    with ExitStack() as mem:
        rows = mem.enter_context(tensor(nc, "y_rows", [P, TT + 1, D]))
        turn_rows(nc, g, ps, lambda k: g.X[:, k, :], rows, d.y_prompt[0], d.y_sample[:, 0, :])


def turn_rows(nc, g, ps, tile, out, to_prompt, to_samples):
    with phase(nc, "turned", "taken_act", "taken_dve", "stored") as (s, block):
        NG = 2 * (TT + 1)

        @block.tensor
        def _(pe):
            for n in range(NG):
                t, half = n // 2, n % 2
                w = P if t < TT else NS
                if n >= 8:
                    pe.wait_ge(s.taken_dve if half else s.taken_act, (n - 8) // 2 + 1)
                for k in range(4):
                    last = pe.transpose(ps[0:w, n % 8, k * P:(k + 1) * P], tile(4 * half + k)[:, t * P:t * P + w],
                                        g.ident[:, :])
                last.then_inc(s.turned, 1)

        @block.scalar
        def _(act):
            for n in range(0, NG, 2):
                w = P if n // 2 < TT else NS
                act.wait_ge(s.turned, n + 1)
                act.activation(out[0:w, n // 2, 0:512], ps[0:w, n % 8, :], ACT.Copy).then_inc(s.taken_act, 1)

        @block.vector
        def _(dve):
            for n in range(1, NG, 2):
                w = P if n // 2 < TT else NS
                dve.wait_ge(s.turned, n + 1)
                dve.tensor_copy(out[0:w, n // 2, 512:1024], ps[0:w, n % 8, :]).then_inc(s.taken_dve, 1)

        @block.sync
        def _(sp):
            for t in range(TT + 1):
                sp.wait_ge(s.taken_act, t + 1)
                sp.wait_ge(s.taken_dve, t + 1)
                if t < TT:
                    sp.dma_start(to_prompt[t * P:(t + 1) * P, :], out[:, t, :]).then_inc(s.stored, 16)
                else:
                    sp.dma_start(to_samples, out[0:NS, t, :]).then_inc(s.stored, 16)
            sp.wait_ge(s.stored, 16 * (TT + 1))


def program(nc, d):
    ctx = ExitStack()
    probe = ctx.enter_context(nc.semaphore("first"))
    FIRST_SEM[0] = probe.num
    with ctx:
        def sb(name, shape, dt=F32):
            return ctx.enter_context(tensor(nc, name, shape, dt))

        g = record(
            X=sb("residual", [P, DT, NT]), ones=sb("ones", [P, P]), ident=sb("ident", [P, P]),
            blockones=sb("blockones", [P, P]), ident2=sb("ident2", [P, 64]), tail=sb("tail", [P, P]),
            rest=sb("rest", [P, P]), blocked=sb("blocked", [P, P]), epsc=sb("eps", [P, 2]), par=sb("params", [P, 2 * P]),
            shift0=sb("shift0", [P, RWC_T, NS]), conv0=sb("conv0", [P, LRU_T, 24]), h0=sb("h0", [P, LRU_T, NS]),
            kn=sb("kn", [P, 2, P]), sbb=sb("sb_bias", [P, SBH]), pages=sb("pages", [1, NS * PAGES], I32))
        ps = ctx.enter_context(nc.psum_tensor("ps", [P, 8, 512], F32))
        constants(nc, g)
        load_inputs(nc, g, d, ps)
        layer0_mixer(nc, g, d, ps)
        memory_attention(nc, g, d, ps, 0)
        ffn(nc, g, d, ps, 0)
        stick_breaking(nc, g, d, ps)
        memory_attention(nc, g, d, ps, 1)
        ffn(nc, g, d, ps, 1)
        store_outputs(nc, g, d, ps)


OUTS = [("y_prompt", (1, T, D)), ("y_sample", (NS, 1, D)), ("wkv_p", (1, 1, 8, HD, HD)), ("wkv_s", (1, NS, 8, HD, HD)),
        ("shift_p", (1, 1, RW_COLS)), ("shift_s", (1, NS, RW_COLS)), ("lru_h_p", (1, 1, RW)), ("lru_h_s", (1, NS, RW)),
        ("lru_conv_p", (1, 1, 3, RW)), ("lru_conv_s", (1, NS, 3, RW)), ("sb_k_p", (1, 1, T, SBH, HD)),
        ("sb_k_s", (1, NS, 1, SBH, HD)), ("sb_v_p", (1, 1, T, SBH, HD)), ("sb_v_s", (1, NS, 1, SBH, HD)),
        ("mem_k_p", (2, 1, MEM, MH, P)), ("mem_v_p", (2, 1, MEM, MH, P))]


def kernel(**inputs):
    import numpy as _np
    import concourse.bacc as _bacc
    from concourse.bass_utils import run_bass_kernel_spmd as _run

    nc = _bacc.Bacc("TRN2", target_bir_lowering=False, num_devices=1)
    arrays, aps = {}, {}
    for name, value in inputs.items():
        a = _np.ascontiguousarray(value)
        arrays[f"in_{name}"] = a
        aps[name] = nc.dram_tensor(f"in_{name}", a.shape, mybir.dt.from_np(a.dtype), kind="ExternalInput").ap()
    for name, shape in OUTS:
        aps[name] = nc.dram_tensor(f"out_{name}", shape, F32, kind="ExternalOutput").ap()
    aps["spill"] = nc.dram_tensor("residual_spill", (P, DT, NT), F32, kind="Internal").ap()
    program(nc, record(rows=aps, **aps))
    r = _run(nc, [arrays], core_ids=[0])
    return tuple(r.results[0][f"out_{name}"] for name, _ in OUTS)
```
